# Optimizing a Trainium2 kernel written in Bass

```python
import math
import jax, jax.numpy as jnp
from jax import lax
import numpy as np

D_MODEL = 1024
BATCH = 1
SEQ = 256
DEPTH = 1

CHUNK = 64
Q_BLOCK = 128
EPS = 1e-6
M_HEADS = 4
M_DK = 128
M_DV = 256
M_QK = M_HEADS * M_DK
M_V = M_HEADS * M_DV
CONV_W = 4
D_HEADS = 8
D_DH = 64
D_QK = D_HEADS * 2 * D_DH
D_V = D_HEADS * 2 * D_DH
X_HEADS = 4
X_DH = D_MODEL // X_HEADS
N_MEM = 256
N_EXPERTS = 32
TOP_K = 4
D_FF = D_MODEL
SWIGLU_LIMIT = 7.0
SWIGLU_ALPHA = 1.702
N_BRANCHES = 2
IN_SIZES = [M_QK, M_QK, M_V, M_V, 2 * M_HEADS, D_QK, D_QK, D_V, N_BRANCHES * D_MODEL]
N_IN = sum(IN_SIZES)
IN_SPLITS = np.cumsum(IN_SIZES[:-1]).tolist()

kernel_name = "hybrid_mlstm_diffattn_moe_stream_block"

def rmsnorm(x, g):
    xf = x.astype(jnp.float32)
    y = xf * lax.rsqrt(jnp.mean(xf * xf, axis=-1, keepdims=True) + EPS)
    return (y * g.astype(jnp.float32)).astype(x.dtype)

def causal_conv(x, w):
    S = x.shape[1]
    xp = jnp.pad(x, ((0, 0), (CONV_W - 1, 0), (0, 0)))
    return sum(w[j] * xp[:, j:j + S] for j in range(CONV_W))

def mlstm_chunkwise(q, k, v, i_pre, f_pre):
    B, S, H, DK = q.shape
    DV = v.shape[-1]
    NC, L = S // CHUNK, CHUNK
    f32 = jnp.float32
    q = q.astype(f32) * (DK ** -0.5)
    qc = q.reshape(B, NC, L, H, DK).transpose(1, 0, 3, 2, 4)
    kc = k.astype(f32).reshape(B, NC, L, H, DK).transpose(1, 0, 3, 2, 4)
    vc = v.astype(f32).reshape(B, NC, L, H, DV).transpose(1, 0, 3, 2, 4)
    fc = jax.nn.log_sigmoid(f_pre.astype(f32)).reshape(B, NC, L, H).transpose(1, 0, 3, 2)
    ic = i_pre.astype(f32).reshape(B, NC, L, H).transpose(1, 0, 3, 2)
    causal = jnp.tril(jnp.ones((L, L), dtype=bool))

    def step(carry, inp):
        C, n, m = carry
        qb, kb, vb, fb, ib = inp
        b = jnp.cumsum(fb, axis=-1)
        b_last = b[..., -1]
        dm = jnp.where(causal, b[..., :, None] - b[..., None, :] + ib[..., None, :], -jnp.inf)
        inter = b + m[..., None]
        m_t = jnp.maximum(inter, jnp.max(dm, axis=-1))
        w_inter = jnp.exp(inter - m_t)
        s = jnp.einsum('bhtd,bhsd->bhts', qb, kb) * jnp.exp(dm - m_t[..., None])
        num = jnp.einsum('bhts,bhsv->bhtv', s, vb) + w_inter[..., None] * jnp.einsum('bhvd,bhtd->bhtv', C, qb)
        den = jnp.sum(s, axis=-1) + w_inter * jnp.einsum('bhd,bhtd->bht', n, qb)
        h = num / jnp.maximum(jnp.abs(den), jnp.exp(-m_t))[..., None]
        g = b_last[..., None] - b + ib
        m_new = jnp.maximum(b_last + m, jnp.max(g, axis=-1))
        wk = jnp.exp(g - m_new[..., None])
        decay = jnp.exp(b_last + m - m_new)
        C_new = decay[..., None, None] * C + jnp.einsum('bhs,bhsv,bhsd->bhvd', wk, vb, kb)
        n_new = decay[..., None] * n + jnp.einsum('bhs,bhsd->bhd', wk, kb)
        return (C_new, n_new, m_new), h

    init = (jnp.zeros((B, H, DV, DK), f32), jnp.zeros((B, H, DK), f32), jnp.zeros((B, H), f32))
    _, hs = lax.scan(step, init, (qc, kc, vc, fc, ic))
    return hs.transpose(1, 0, 3, 2, 4).reshape(B, S, H, DV).astype(v.dtype)

def diff_attention(q, k, v, lam, gain, lam_init):
    B, S, H = q.shape[:3]
    nb = S // Q_BLOCK
    q = q * (D_DH ** -0.5)
    k_chunk = jnp.arange(S) // CHUNK
    qb = q.reshape(B, nb, Q_BLOCK, H, 2, D_DH).transpose(1, 0, 2, 3, 4, 5)

    def block(args):
        qblk, idx = args
        q_chunk = (idx * Q_BLOCK + jnp.arange(Q_BLOCK)) // CHUNK
        mask = k_chunk[None, :] <= q_chunk[:, None]
        s = jnp.einsum('bqhcd,bkhcd->bhcqk', qblk, k).astype(jnp.float32)
        p = jax.nn.softmax(jnp.where(mask, s, -jnp.inf), axis=-1)
        a = p[:, :, 0] - lam * p[:, :, 1]
        return jnp.einsum('bhqk,bkhv->bqhv', a.astype(v.dtype), v)

    out = lax.map(block, (qb, jnp.arange(nb)))
    out = out.transpose(1, 0, 2, 3, 4).reshape(B, S, H, 2 * D_DH)
    return rmsnorm(out, gain) * (1.0 - lam_init)

def hybrid_mixer(h, w_in, conv_w, b_if, m_gain, lam_p, d_gain, w_bm, w_bd, b_gate, w_out, lam_init):
    B, S, _ = h.shape
    z = h @ w_in
    qm, km, vm, om, ifm, qd, kd, vd, gates = jnp.split(z, IN_SPLITS, axis=-1)
    qk = jax.nn.silu(causal_conv(jnp.concatenate([qm, km], axis=-1), conv_w))
    qm, km = qk[..., :M_QK], qk[..., M_QK:]
    hm = mlstm_chunkwise(qm.reshape(B, S, M_HEADS, M_DK), km.reshape(B, S, M_HEADS, M_DK),
                         vm.reshape(B, S, M_HEADS, M_DV),
                         ifm[..., :M_HEADS] + b_if[:M_HEADS], ifm[..., M_HEADS:] + b_if[M_HEADS:])
    hm = jax.nn.sigmoid(om) * rmsnorm(hm, m_gain).reshape(B, S, M_V)
    branch_m = hm @ w_bm
    lp = lam_p.astype(jnp.float32)
    lam = jnp.exp(jnp.sum(lp[0] * lp[1])) - jnp.exp(jnp.sum(lp[2] * lp[3])) + lam_init
    hd = diff_attention(qd.reshape(B, S, D_HEADS, 2, D_DH), kd.reshape(B, S, D_HEADS, 2, D_DH),
                        vd.reshape(B, S, D_HEADS, 2 * D_DH), lam, d_gain, lam_init)
    branch_d = hd.reshape(B, S, D_V) @ w_bd
    g = jax.nn.sigmoid(gates + b_gate)
    return (g[..., :D_MODEL] * branch_m + g[..., D_MODEL:] * branch_d) @ w_out

def cross_attention(h, memn, wq, wkv, wo):
    B, S, _ = h.shape
    M = memn.shape[1]
    q = (h @ wq).reshape(B, S, X_HEADS, X_DH) * (X_DH ** -0.5)
    kv = memn @ wkv
    k = kv[..., :D_MODEL].reshape(B, M, X_HEADS, X_DH)
    v = kv[..., D_MODEL:].reshape(B, M, X_HEADS, X_DH)
    p = jax.nn.softmax(jnp.einsum('bshd,bmhd->bhsm', q, k).astype(jnp.float32), axis=-1)
    o = jnp.einsum('bhsm,bmhd->bshd', p.astype(v.dtype), v).reshape(B, S, D_MODEL)
    return o @ wo

def moe(h, w_r, b_r, w_gu, b_gu, w_dn, b_dn):
    B, S, D = h.shape
    t = h.reshape(B * S, D)
    logits = (t @ w_r + b_r).astype(jnp.float32)
    top_v, top_i = lax.top_k(logits, TOP_K)
    top_w = jax.nn.softmax(top_v, axis=-1)
    combine = jnp.sum(jax.nn.one_hot(top_i, N_EXPERTS, dtype=jnp.float32) * top_w[..., None], axis=1)

    def expert(acc, p):
        wgu, bgu, wdn, bdn, c = p
        gu = t @ wgu + bgu
        gate = jnp.minimum(gu[:, :D_FF], SWIGLU_LIMIT)
        up = jnp.clip(gu[:, D_FF:], -SWIGLU_LIMIT, SWIGLU_LIMIT)
        y = ((up + 1.0) * (gate * jax.nn.sigmoid(SWIGLU_ALPHA * gate))) @ wdn + bdn
        return acc + c[:, None] * y, None

    acc, _ = lax.scan(expert, jnp.zeros_like(t), (w_gu, b_gu, w_dn, b_dn, combine.T.astype(t.dtype)))
    return acc.reshape(B, S, D)

def setup_inputs(seed: int = 0) -> dict:
    key = jax.random.key(seed)
    ks = jax.random.split(key, 32)
    f32 = jnp.float32
    D, E, L = D_MODEL, N_EXPERTS, DEPTH

    def nrm(k, shape, scale):
        return jax.random.normal(k, shape, f32) * scale

    def gain(k, shape):
        return 1.0 + nrm(k, shape, 0.02)

    f_bias = jnp.broadcast_to(jnp.linspace(3.0, 6.0, M_HEADS, dtype=f32), (L, M_HEADS))
    b_if = jnp.concatenate([nrm(ks[3], (L, M_HEADS), 0.1), f_bias + nrm(ks[4], (L, M_HEADS), 0.1)], axis=-1)
    return {
        "x": nrm(ks[0], (BATCH, SEQ, D), 1.0),
        "mem": nrm(ks[1], (BATCH, N_MEM, D), 1.0),
        "norm_mix": gain(ks[2], (L, D)),
        "w_in": nrm(ks[5], (L, D, N_IN), D ** -0.5),
        "conv_w": nrm(ks[6], (L, CONV_W, 2 * M_QK), CONV_W ** -0.5),
        "b_if": b_if,
        "mlstm_gain": gain(ks[7], (L, M_HEADS, M_DV)),
        "diff_lambda": nrm(ks[8], (L, 4, D_DH), 0.1),
        "diff_gain": gain(ks[9], (L, 2 * D_DH)),
        "w_branch_m": nrm(ks[10], (L, M_V, D), M_V ** -0.5),
        "w_branch_d": nrm(ks[11], (L, D_V, D), D_V ** -0.5),
        "b_gate": nrm(ks[12], (L, N_BRANCHES * D), 0.1),
        "w_out": nrm(ks[13], (L, D, D), D ** -0.5),
        "norm_xattn": gain(ks[14], (L, D)),
        "norm_mem": gain(ks[15], (L, D)),
        "wq_x": nrm(ks[16], (L, D, D), D ** -0.5),
        "wkv_x": nrm(ks[17], (L, D, 2 * D), D ** -0.5),
        "wo_x": nrm(ks[18], (L, D, D), D ** -0.5),
        "norm_ffn": gain(ks[19], (L, D)),
        "w_router": nrm(ks[20], (L, D, E), D ** -0.5),
        "b_router": nrm(ks[21], (L, E), 0.01),
        "w_gu": nrm(ks[22], (L, E, D, 2 * D_FF), D ** -0.5),
        "b_gu": nrm(ks[23], (L, E, 2 * D_FF), 0.02),
        "w_dn": nrm(ks[24], (L, E, D_FF, D), D_FF ** -0.5),
        "b_dn": nrm(ks[25], (L, E, D), 0.02),
        "norm_final": gain(ks[26], (D,)),
    }

def reference(x, mem, norm_mix, w_in, conv_w, b_if, mlstm_gain, diff_lambda, diff_gain,
              w_branch_m, w_branch_d, b_gate, w_out, norm_xattn, norm_mem, wq_x, wkv_x, wo_x,
              norm_ffn, w_router, b_router, w_gu, b_gu, w_dn, b_dn, norm_final):
    for l in range(DEPTH):
        lam_init = 0.8 - 0.6 * math.exp(-0.3 * l)
        x = x + hybrid_mixer(rmsnorm(x, norm_mix[l]), w_in[l], conv_w[l], b_if[l], mlstm_gain[l],
                             diff_lambda[l], diff_gain[l], w_branch_m[l], w_branch_d[l], b_gate[l],
                             w_out[l], lam_init)
        x = x + cross_attention(rmsnorm(x, norm_xattn[l]), rmsnorm(mem, norm_mem[l]),
                                wq_x[l], wkv_x[l], wo_x[l])
        x = x + moe(rmsnorm(x, norm_ffn[l]), w_router[l], b_router[l], w_gu[l], b_gu[l],
                    w_dn[l], b_dn[l])
    return rmsnorm(x, norm_final)


_drawn_inputs = setup_inputs


def setup_inputs(seed=0):
    import zlib

    import numpy as np

    out = dict(_drawn_inputs(seed))
    spreads = {}
    factors = {'mlstm_gain': 2.921,
     'norm_xattn': 5.213,
     'norm_mem': 4.819,
     'b_router': 16.257,
     'b_gu': 21.649,
     'b_dn': 25.066,
     'norm_final': 7.897,
     'norm_ffn': 5.545}
    for name, (base, spread) in spreads.items():
        noise = np.random.default_rng([zlib.crc32(name.encode()), seed]).standard_normal(out[name].shape)
        drawn = base * np.exp(spread * noise) if base else spread * noise
        out[name] = __import__('jax').numpy.asarray(drawn.astype(out[name].dtype))
    for name, factor in factors.items():
        out[name] = (out[name] * factor).astype(out[name].dtype)
    return out
```

```python
from contextlib import ExitStack

import concourse.bass as bass
from concourse import mybir

P = 128
D = 1024
T = 256
TT = T // P
KC = D // P
BLK = 512
SLOTS = 6
EPS = 1e-6
M_HEADS, M_DK, M_DV = 4, 128, 256
D_HEADS, D_DH = 8, 64
X_HEADS, X_DH = 4, 256
E, TOP_K = 32, 4
CAP = 64
HALF = D // 2
LIMIT, ALPHA = 7.0, 1.702
LAM_INIT = 0.8 - 0.6
CONV_W = 4
NEG = -1e30
IF_COL = 3072
COL = {"qm": 0, "km": 512, "vm": 1024, "om": 2048, "qd": 3080, "kd": 4104, "vd": 5128, "gm": 6152, "gd": 7176}

VECS = [("norm_mix", 8), ("norm_xattn", 8), ("norm_mem", 8), ("norm_ffn", 8), ("mlstm_gain", 8),
        ("diff_gain", 1), ("b_gate", 16), ("conv_w", 32)]
VCOL, NVEC = {}, 0
for _name, _n in VECS:
    VCOL[_name] = NVEC
    NVEC += _n

EVACUATES = {
    "xT": "dve", "qm": "dve", "km": "dve", "vm": "act", "om": "act", "qd": "act", "kd": "dve", "vd": "act",
    "hmT": "dve", "memT": "dve", "kx": "act", "vx": "act", "gm": "act", "bm": "dve", "hdT": "dve",
    "gd": "act", "bd": "dve", "out": "dve", "x1T": "dve", "qx": "act", "oxT": "act", "wo": "dve", "x2T": "dve",
}
TRANSPOSES = ("xT", "hmT", "memT", "hdT", "x1T", "oxT", "x2T")
TOKEN_MAJOR = ("vm", "vd", "vx", "out", "wo")
ORDER = [
    ("vectors", 0), ("normx", 0), ("xT", 0), ("qm", 0), ("km", 0), ("gates", 0), ("vm", 0), ("gates2", 0),
    ("vm", 1),
    ("mls", 0), ("om", 0), ("mlo", 0), ("mls", 1), ("om", 1), ("mlo", 1),
    ("mls", 2), ("qd", 0), ("mlo", 2), ("mls", 3), ("qd", 1), ("mlo", 3),
    ("kd", 0), ("mlnorm", 0), ("hmT", 0), ("normmem", 0), ("kd", 1), ("vd", 0), ("vd", 1),
    ("memT", 0),
    ("dfs", 0), ("kx", 0), ("dfo", 0), ("dfs", 1), ("kx", 1), ("dfo", 1),
    ("dfs", 2), ("vx", 0), ("dfo", 2), ("dfs", 3), ("vx", 1), ("dfo", 3),
    ("dfs", 4), ("gm", 0), ("dfo", 4), ("dfs", 5), ("gm", 1), ("dfo", 5),
    ("dfs", 6), ("bm", 0), ("dfo", 6), ("dfs", 7), ("bm", 1), ("dfo", 7),
    ("dfnorm", 0), ("gd", 0), ("gd", 1), ("hdT", 0), ("bd", 0), ("bd", 1), ("out", 0), ("out", 1),
    ("norm1", 0), ("x1T", 0), ("qx", 0), ("qx", 1),
    ("xas", 0), ("xas", 1), ("xao", 0), ("xas", 2), ("xao", 1), ("xas", 3), ("xao", 2), ("xao", 3),
    ("oxT", 0), ("wo", 0), ("wo", 1), ("norm2", 0), ("x2T", 0), ("route", 0),
]


def tiles_of(step):
    return 4 if step in TRANSPOSES else 2


def nth(events):
    return {step: i for i, (step, _) in enumerate(x for x in ORDER if x[0] in events)}


NORM_SQ = nth(("normx", "normmem", "norm1", "norm2"))
NORM_VAR = nth(("normx", "normmem", "norm1", "norm2", "mlnorm", "dfnorm"))
NORM_VAR["final"] = len(NORM_VAR)
NORM_COL = {"normx": 0, "norm1": 2, "norm2": 4, "normmem": 6, "final": 16}


def plan():
    first, owner, blocks = {}, [], []
    count = {"act": 0, "dve": 0}
    for step, k in ORDER:
        if step not in EVACUATES:
            continue
        first[step, k] = len(owner)
        for _ in range(tiles_of(step)):
            count[EVACUATES[step]] += 1
            owner.append((EVACUATES[step], count[EVACUATES[step]]))
        if step not in TRANSPOSES:
            blocks.append((step, k))
    return first, owner, blocks


TILE, OWNER, BLOCKS = plan()
NB = len(BLOCKS)


def program(nc, x, mem, norm_mix, w_in, conv_w, b_if, mlstm_gain, diff_lambda, diff_gain, w_branch_m,
            w_branch_d, b_gate, w_out, norm_xattn, norm_mem, wq_x, wkv_x, wo_x, norm_ffn, w_router,
            b_router, w_gu, b_gu, w_dn, b_dn, norm_final, out):
    f32, i32 = mybir.dt.float32, mybir.dt.int32
    ALU, ACT, AX = mybir.AluOpType, mybir.ActivationFunctionType, mybir.AxisListType
    assert NB % SLOTS == 0

    ctx = ExitStack()
    with ctx:
        def sb(name, shape, dt=f32):
            return ctx.enter_context(nc.sbuf_tensor(name, shape, dt))

        def sem(name):
            return ctx.enter_context(nc.semaphore(name))

        ring = sb("ring", [P, SLOTS, 8 * BLK])
        mat = [sb(f"mat{i}", [P, TT * D]) for i in range(11)]
        RES, HT, QK, VM, HM, OM, QD, KD, VD, HD, GM = mat
        HMT, MEMT, KX, VX = QK, VM, HM, OM
        MEMN, HDT, GD, NRM = HD, QD, KD, VD
        QX, OX, OXT = QK, HD, QD

        def nat(m):
            return m[:, :].rearrange("p (t d) -> p t d", t=TT)

        def fm(m):
            return m[:, :].rearrange("p (c t) -> p c t", t=T)

        ident = sb("ident", [P, P])
        ones = sb("ones", [P, T])
        strict = sb("strict", [P, P])
        causal = sb("causal", [P, P])
        chunk_mask = sb("chunk_mask", [P, 3, P])
        slot_no = sb("slot_no", [P, 2 * CAP])
        head_row = VD[0:M_HEADS, 0:M_HEADS * P].rearrange("h (j p) -> h j p", p=P)
        vec_rows = sb("vec_rows", [NVEC, P])
        vec = sb("vec", [P, NVEC])
        w_if = sb("w_if", [P, KC, 2 * M_HEADS])
        b_if_c = sb("b_if_c", [M_HEADS, 2])
        lam_row = sb("lam_row", [1, 4 * D_DH])
        lam_w = sb("lam_w", [1, D_DH])
        lam_s = sb("lam_s", [1, 4])
        neg_lam = sb("neg_lam", [P, 1])
        w_r = sb("w_r", [P, KC, E])
        b_r = sb("b_r", [1, E])
        fin_gain = sb("fin_gain", [P, D])
        stat = sb("stat", [P, 64])
        gate = OM[0:M_HEADS, :].rearrange("h (j t) -> h j t", t=T)
        a_em = sb("a_em", [P, TT, 2 * M_HEADS])
        m_all = GM[:, 0:M_HEADS * T].rearrange("p (h t) -> p h t", t=T)
        decay = GM[:, D:D + 6 * P].rearrange("p (b n) -> p b n", b=2)
        work = sb("work", [P, 4, BLK])
        work_t = sb("work_t", [P, BLK])
        squares = work[:, :, :].rearrange("p (t a) n -> p t (a n)", t=TT)
        fin_row = work[0:1, 0:2, :].rearrange("p a n -> p (a n)")
        bgu = KX
        bdn = VX[0:E, 0:D]

        bank = [ctx.enter_context(nc.psum_tensor(f"bank{i}", [P, BLK], f32)) for i in range(8)]
        A = bank[4:8]

        consts_done = sem("consts_done")
        small_in = sem("small_in")
        x_in, mem_in = sem("x_in"), sem("mem_in")
        w_loaded = [sem(f"w_loaded{i}") for i in range(SLOTS)]
        w_used = [sem(f"w_used{i}") for i in range(SLOTS - 1)]
        tile_ready = sem("tile_ready")
        evac = {"act": sem("evac_act"), "dve": sem("evac_dve")}
        dve_step, act_step, pool_step = sem("dve_step"), sem("act_step"), sem("pool_step")
        norm_sq, norm_var, norm_std, norm_done = sem("norm_sq"), sem("norm_var"), sem("norm_std"), sem("norm_done")
        vec_cols = sem("vec_cols")
        vec_ready, vec_done = sem("vec_ready"), sem("vec_done")
        lam_sum, lam_exp, lam_set, lam_bc = sem("lam_sum"), sem("lam_exp"), sem("lam_set"), sem("lam_bc")
        conv_out, conv_sig = sem("conv_out"), sem("conv_sig")
        if_ready, f_abs, f_ln, bm_ready, em_ready, gate_rows = (
            sem("if_ready"), sem("f_abs"), sem("f_ln"), sem("bm_ready"), sem("em_ready"), sem("gate_rows"))
        gate_bc, gate_cols = sem("gate_bc"), sem("gate_cols")
        ml_gap, ml_decay, ml_scores, ml_probs, ml_num, ml_rden, ml_h = (
            sem("ml_gap"), sem("ml_decay"), sem("ml_scores"), sem("ml_probs"), sem("ml_num"), sem("ml_rden"), sem("ml_h"))
        hm_done = sem("hm_done")
        df_scores, df_max, df_exp, df_a, df_aT, df_aTs, df_o, df_h, hd_done = (
            sem("df_scores"), sem("df_max"), sem("df_exp"), sem("df_a"), sem("df_aT"), sem("df_aTs"),
            sem("df_o"), sem("df_h"), sem("hd_done"))
        xa_scores, xa_max, xa_exp, xa_pT, xa_pTs, xa_o, xa_rec, xa_h = (
            sem("xa_scores"), sem("xa_max"), sem("xa_exp"), sem("xa_pT"), sem("xa_pTs"), sem("xa_o"),
            sem("xa_rec"), sem("xa_h"))
        lg_ready, lg_max, lg_exp, mask_ready, rank_ready, comb_ready, combT_ready, combT_done, route_done = (
            sem("lg_ready"), sem("lg_max"), sem("lg_exp"), sem("mask_ready"), sem("rank_ready"),
            sem("comb_ready"), sem("combT_ready"), sem("combT_done"), sem("route_done"))
        pick_ready, pickw_ready, xg_ready, xg_done, sel_ready = (
            sem("pick_ready"), sem("pickw_ready"), sem("xg_ready"), sem("xg_done"), sem("sel_ready"))
        g_ready, u_ready, g_clip, g_sig, gs_done, a_ready, aT_ready, aT_done, wT_ready, wT_done = (
            sem("g_ready"), sem("u_ready"), sem("g_clip"), sem("g_sig"), sem("gs_done"), sem("a_ready"), sem("aT_ready"), sem("aT_done"),
            sem("wT_ready"), sem("wT_done"))
        y_ready, y_done, added, rank_moved = sem("y_ready"), sem("y_done"), sem("added"), sem("rank_moved")
        fin_res, out_ready, stored = (
            sem("fin_res"), sem("out_ready"), sem("stored"))
        N_SMALL, CONSTS = 14, 10
        bias_in = sem("bias_in")

        H2 = NRM
        taken = [0]

        def part(*shape, rows=P):
            n = shape[0] * shape[1]
            taken[0] += n
            return QX[0:rows, taken[0] - n:taken[0]].rearrange("p (a b) -> p a b", b=shape[1])

        xg = part(KC, CAP)
        pick = part(TT, CAP)
        pickw = part(TT, 2 * CAP)
        wT = part(TT, P)
        combT = part(TT, P, rows=E)
        lg = part(8 * TT, E).rearrange("p (j t) e -> p j t e", t=TT)
        sel = sb("sel", [P, CAP])
        rank = sb("rank", [P, TT, E + 1])
        comb = sb("comb", [P, TT, E + 1])
        top = sb("top", [P, TT, 8])
        most = sb("most", [P, 2])
        most_i = sb("most_i", [P, 1], i32)
        G_, U_, S_, A_ = (work[:, j, :] for j in range(4))
        y_sb = OXT[:, 0:BLK]
        gbank, ubank, xbank, tbank = bank[4], bank[5], bank[6], bank[7]

        def wait_evacuated(eng, n):
            if n >= 0:
                who, k = OWNER[n]
                eng.wait_ge(evac[who], k)

        def wait_job(eng, step, k=0):
            wait_evacuated(eng, TILE[step, k] + tiles_of(step) - 1)

        block = ctx.enter_context(nc.Block())

        @block.sync
        def _(sp):
            sources = {"kx": (wkv_x[0], 0), "vx": (wkv_x[0], D), "bm": (w_branch_m[0], 0), "bd": (w_branch_d[0], 0),
                       "out": (w_out[0], 0), "qx": (wq_x[0], 0), "wo": (wo_x[0], 0)}
            sp.dma_start(nat(RES), x[0].rearrange("(t p) d -> p t d", p=P)).then_inc(x_in, 16)

            def free_slot(eng, n):
                eng.wait_ge(tile_ready, TILE[BLOCKS[n]] + 2)

            for n, (step, k) in enumerate(BLOCKS):
                w, c = sources[step] if step in sources else (w_in[0], COL[step])
                c += k * BLK
                if n >= SLOTS:
                    free_slot(sp, n - SLOTS)
                sp.dma_start(ring[:, n % SLOTS, :].rearrange("p (k n) -> p k n", k=KC),
                             w[:, c:c + BLK].rearrange("(k p) n -> p k n", p=P)).then_inc(w_loaded[n % SLOTS], 16)
                if n == SLOTS:
                    sp.wait_ge(tile_ready, TILE["xT", 0] + 4)
                    sp.dma_start(nat(MEMN), mem[0].rearrange("(t p) d -> p t d", p=P)).then_inc(mem_in, 16)

            gu = w_gu[0].rearrange("e (h k p) n -> p e h k n", h=2, p=P)
            dn = w_dn[0].rearrange("e (h k p) n -> p e h k n", h=2, p=P)

            def load_block(e, j):
                part, h = j // 2, j % 2
                src = (gu[:, bass.ds(e, 1), h, :, part * D:(part + 1) * D] if part < 2
                       else dn[:, bass.ds(e, 1), h, :, :])
                sp.dma_start(ring[:, j, :].rearrange("p (k n) -> p k n", k=4),
                             src.rearrange("p e k n -> p (e k) n")).then_inc(w_loaded[j], 16)

            def stream(before, first):
                with sp.Fori(first, E) as e:
                    for j in range(SLOTS):
                        sp.wait_ge(w_used[j] if j < SLOTS - 1 else y_ready, e + before * E)
                        load_block(e, j)

            for j in range(SLOTS):
                free_slot(sp, NB - SLOTS + j)
                load_block(0, j)
            stream(0, 1)
            sp.wait_ge(route_done, 1)
            n_most = sp.value_load(most_i[0:1, 0:1], min_val=0, max_val=T)
            for p in range(1, T // CAP):
                with sp.If(n_most > p * CAP):
                    stream(p, 0)
            sp.wait_ge(out_ready, TT)
            sp.dma_start(out[0].rearrange("(t p) d -> p t d", p=P), nat(RES)).then_inc(stored, 16)
            sp.wait_ge(stored, 16)

        @block.gpsimd
        def _(pool):
            steps = [0]

            def after(ins):
                steps[0] += 1
                ins.then_inc(pool_step, 1)
                pool.wait_ge(pool_step, steps[0])

            pool.memset(ones[:, :], 1.0).then_inc(consts_done, 1)
            after(pool.memset(ident[:, :], 0.0))
            pool.affine_select(out=ident[:, :], in_=ident[:, :], compare_op=ALU.not_equal, fill=1.0, base=0,
                               pattern=[[-1, P]], channel_multiplier=1).then_inc(consts_done, 1)
            after(pool.memset(strict[:, :], 1.0))
            pool.affine_select(out=strict[:, :], in_=strict[:, :], compare_op=ALU.is_gt, fill=0.0, base=0,
                               pattern=[[1, P]], channel_multiplier=-1).then_inc(consts_done, 1)
            after(pool.memset(causal[:, :], 1.0))
            pool.affine_select(out=causal[:, :], in_=causal[:, :], compare_op=ALU.is_ge, fill=0.0, base=0,
                               pattern=[[1, P]], channel_multiplier=-1).then_inc(consts_done, 1)
            after(pool.memset(chunk_mask[:, :, :], 0.0))
            for b in (0, 2):
                pool.memset(chunk_mask[0:64, b, 64:P], NEG).then_inc(consts_done, 1)
            pool.iota(slot_no[:, :], pattern=[[0, 2], [1, CAP]], base=0, channel_multiplier=0,
                      allow_small_or_imprecise_dtypes=True).then_inc(consts_done, 1)
            after(pool.memset(head_row[:, :, :], 0.0))
            pool.affine_select(out=head_row[:, :, :], in_=head_row[:, :, :], compare_op=ALU.not_equal, fill=1.0,
                               base=0, pattern=[[-1, M_HEADS], [0, P]], channel_multiplier=1).then_inc(consts_done, 1)
            pool.memset(rank[:, :, E:E + 1], -1.0).then_inc(consts_done, 1)
            pool.memset(comb[:, :, E:E + 1], 0.0).then_inc(consts_done, 1)

            def selectors(before, first):
                with pool.Fori(first, E) as e:
                    pool.wait_ge(u_ready, e + before * E)
                    pool.tensor_copy(sel[:, :], ident[:, bass.ds(e, 1)].to_broadcast([P, CAP])).then_inc(sel_ready, 1)

            pool.wait_ge(consts_done, CONSTS)
            pool.wait_ge(xa_o, X_HEADS)
            after(pool.memset(bgu[:, :], 0.0))
            pool.dma_start(bgu[0:E, :], b_gu[0]).then_inc(bias_in, 16)
            pool.dma_start(bdn, b_dn[0]).then_inc(bias_in, 16)
            pool.tensor_copy(sel[:, :], ident[:, 0:1].to_broadcast([P, CAP])).then_inc(sel_ready, 1)
            selectors(0, 1)
            pool.wait_ge(route_done, 1)
            n_most = pool.value_load(most_i[0:1, 0:1], min_val=0, max_val=T)
            for p in range(1, T // CAP):
                with pool.If(n_most > p * CAP):
                    selectors(p, 0)

        @block.scalar
        def _(act):
            n_step = [0]

            def link(ins):
                n_step[0] += 1
                ins.then_inc(act_step, 1)
                act.wait_ge(act_step, n_step[0])

            def small(dst, src):
                act.dma_start(dst, src).then_inc(small_in, 16)

            rows = {"norm_mix": norm_mix, "norm_xattn": norm_xattn, "norm_mem": norm_mem, "norm_ffn": norm_ffn,
                    "diff_gain": diff_gain, "b_gate": b_gate}
            for name, n in VECS:
                if name in rows:
                    src = rows[name].rearrange("l (r p) -> (l r) p", p=P)
                elif name == "mlstm_gain":
                    src = mlstm_gain[0].rearrange("h (r p) -> (h r) p", p=P)
                else:
                    src = conv_w[0].rearrange("j (r p) -> (j r) p", p=P)
                small(vec_rows[VCOL[name]:VCOL[name] + n, :], src)
            small(w_if[:, :, :], w_in[0][:, IF_COL:IF_COL + 2 * M_HEADS].rearrange("(k p) n -> p k n", p=P))
            act.dma_start(b_if_c[:, :], b_if[0].rearrange("(g h) -> h g", g=2),
                          allow_slow_non_contiguous=True).then_inc(small_in, 16)
            small(lam_row[:, :], diff_lambda.rearrange("l a d -> l (a d)"))
            small(w_r[:, :, :], w_router[0].rearrange("(k p) n -> p k n", p=P))
            small(b_r[:, :], b_router)
            small(fin_row, norm_final.rearrange("(l d) -> l d", l=1))

            def root_mean_square(step, src):
                c = NORM_COL[step]
                for t in range(TT):
                    last = act.activation(squares[:, t, :], nat(src)[:, t, :], ACT.Square, accum_out=stat[:, c + t:c + t + 1])
                last.then_inc(norm_sq, 1)
                root(step, slice(8 + c, 10 + c))

            def root(step, cols):
                act.wait_ge(norm_var, NORM_VAR[step] + 1)
                act.activation(stat[:, cols], stat[:, cols], ACT.Sqrt).then_inc(norm_std, 1)

            def copy_tile(n, dst, func=ACT.Copy, **kw):
                act.wait_ge(tile_ready, n + 1)
                return act.activation(dst, bank[n % 4][:, :], func, **kw)

            def conv_sigmoid(step):
                for c in range(4):
                    i = c + (4 if step == "km" else 0)
                    act.wait_ge(conv_out, i + 1)
                    act.activation(work[:, i % 2, T:2 * T], work[:, i % 2, 0:T], ACT.Sigmoid).then_inc(conv_sig, 1)

            def projection(step, k):
                for i in range(2):
                    n = TILE[step, k] + i
                    if step in ("om", "qd", "kx", "qx"):
                        m = {"om": OM, "qd": QD, "kx": KX, "qx": QX}[step]
                        dst = m[:, (4 * k + 2 * i) * T:(4 * k + 2 * i + 2) * T]
                    elif step in ("vm", "vd", "vx"):
                        m = {"vm": VM, "vd": VD, "vx": VX}[step]
                        dst = nat(m)[:, i, k * BLK:(k + 1) * BLK]
                    if step in ("kx", "vx"):
                        wait_job(act, "hmT")
                    if step in ("gm", "gd"):
                        act.wait_ge(tile_ready, n + 1)
                        g = GM if step == "gm" else GD
                        for j in range(2):
                            c = 4 * k + 2 * i + j
                            v = VCOL["b_gate"] + c + (KC if step == "gd" else 0)
                            last = act.activation(g[:, c * T:(c + 1) * T], bank[n % 4][:, j * T:(j + 1) * T],
                                                  ACT.Sigmoid, bias=vec[:, v:v + 1])
                        last.then_inc(evac["act"], 1)
                    elif step == "om":
                        copy_tile(n, dst, ACT.Sigmoid).then_inc(evac["act"], 1)
                    else:
                        copy_tile(n, dst).then_inc(evac["act"], 1)

            for step, k in ORDER:
                if step == "vectors":
                    act.wait_ge(lam_sum, 2)
                    act.activation(lam_s[:, 2:4], lam_s[:, 0:2], ACT.Exp).then_inc(lam_exp, 1)
                    act.wait_ge(lam_bc, 1)
                    act.activation(neg_lam[:, :], A[2][:, 0:1], ACT.Copy)
                    act.activation(fin_gain[:, 0:BLK], A[0][:, :], ACT.Copy)
                    act.activation(fin_gain[:, BLK:D], A[1][:, :], ACT.Copy).then_inc(vec_done, 1)
                elif step == "normx":
                    act.wait_ge(x_in, 16)
                    root_mean_square(step, RES)
                elif step == "normmem":
                    act.wait_ge(mem_in, 16)
                    root_mean_square(step, MEMN)
                elif step in ("norm1", "norm2"):
                    wait_job(act, "out" if step == "norm1" else "wo", 1)
                    root_mean_square(step, RES)
                elif step in ("qm", "km"):
                    conv_sigmoid(step)
                elif step == "gates":
                    act.wait_ge(f_abs, 1)
                    link(act.activation(gate[:, 2, :], gate[:, 2, :], ACT.Exp, scale=-1.0))
                    act.activation(gate[:, 2, :], gate[:, 2, :], ACT.Ln, bias=1.0).then_inc(f_ln, 1)
                    act.wait_ge(bm_ready, 1)
                    act.activation(gate[:, 6, :], gate[:, 6, :], ACT.Exp, scale=-1.0).then_inc(em_ready, 1)
                elif step == "gates2":
                    act.wait_ge(gate_bc, 1)
                    for b in range(2):
                        act.activation(m_all[:, 2 * b:2 * b + 2, :].rearrange("p h t -> p (h t)"), A[b][:, :], ACT.Copy)
                    act.activation(a_em[:, :, :].rearrange("p t c -> p (t c)"), A[2][:, 0:4 * M_HEADS],
                                   ACT.Copy).then_inc(gate_cols, 1)
                elif step == "mls":
                    act.wait_ge(ml_gap, k + 1)
                    act.activation(decay[:, k % 2, :], decay[:, k % 2, :], ACT.Exp, scale=-1.0).then_inc(ml_decay, 1)
                elif step == "mlo":
                    act.wait_ge(ml_rden, k + 1)
                    for t in range(TT):
                        link(act.activation(nat(HM)[:, t, k * M_DV:(k + 1) * M_DV],
                                            A[2 + k % 2][:, t * M_DV:(t + 1) * M_DV], ACT.Copy,
                                            scale=stat[:, 24 + 2 * (k % 2) + t:25 + 2 * (k % 2) + t]))
                        last = act.activation(squares[:, t, 0:M_DV], nat(HM)[:, t, k * M_DV:(k + 1) * M_DV], ACT.Square,
                                              accum_out=stat[:, 32 + 4 * t + k:33 + 4 * t + k])
                    last.then_inc(ml_h, 1)
                elif step == "mlnorm":
                    root(step, slice(32, 40))
                elif step == "dfs":
                    act.wait_ge(df_max, k + 1)
                    if k >= 1:
                        act.wait_ge(df_a, k)
                    for c in range(2):
                        for t, cols in ((0, slice(0, P)), (1, slice(P, 3 * P))):
                            i = 40 + 2 * c + t
                            last = act.activation(work[:, c, cols], work[:, c, cols], ACT.Exp, scale=D_DH ** -0.5,
                                                  bias=stat[:, i:i + 1], accum_out=stat[:, i + 4:i + 5])
                    last.then_inc(df_exp, 1)
                elif step == "dfo":
                    act.wait_ge(df_aT, k + 1)
                    act.activation(work_t[:, 0:3 * P], A[2][:, 0:3 * P], ACT.Copy).then_inc(df_aTs, 1)
                    act.wait_ge(df_o, k + 1)
                    act.activation(nat(HD)[:, :, k * P:(k + 1) * P],
                                   A[3][:, (k % 2) * T:(k % 2 + 1) * T].rearrange("p (t d) -> p t d", t=TT),
                                   ACT.Copy).then_inc(df_h, 1)
                elif step == "dfnorm":
                    root(step, slice(48, 64))
                elif step == "xas":
                    act.wait_ge(xa_max, k + 1)
                    if k >= 2:
                        act.wait_ge(xa_pT, k - 1)
                    s = 40 + 4 * (k % 2)
                    for t in range(TT):
                        last = act.activation(work[:, k % 2, t * X_DH:(t + 1) * X_DH], A[k % 2][:, t * X_DH:(t + 1) * X_DH],
                                              ACT.Exp, scale=X_DH ** -0.5, bias=stat[:, s + t:s + t + 1],
                                              accum_out=stat[:, s + 2 + t:s + 3 + t])
                    last.then_inc(xa_exp, 1)
                elif step == "xao":
                    act.wait_ge(xa_pT, k + 1)
                    act.activation(work_t[:, :], A[2][:, :], ACT.Copy).then_inc(xa_pTs, 1)
                    act.wait_ge(xa_o, k + 1)
                    act.wait_ge(xa_rec, k + 1)
                    s = 42 + 4 * (k % 2)
                    for t in range(TT):
                        last = act.activation(nat(OX)[:, t, k * X_DH:(k + 1) * X_DH], A[3][:, t * X_DH:(t + 1) * X_DH],
                                              ACT.Copy, scale=stat[:, s + t:s + t + 1])
                    last.then_inc(xa_h, 1)
                elif step == "oxT":
                    for i in range(4):
                        n = TILE[step, 0] + i
                        copy_tile(n, OXT[:, 2 * i * T:(2 * i + 2) * T]).then_inc(evac["act"], 1)
                elif step == "route":
                    act.wait_ge(lg_max, 1)
                    for t in range(TT):
                        last = act.activation(lg[:, 1, t, :], lg[:, 0, t, :], ACT.Exp, bias=stat[:, 24 + t:25 + t])
                    last.then_inc(lg_exp, 1)
                    act.wait_ge(combT_ready, 1)
                    act.activation(combT[:, :, :].rearrange("e t p -> e (t p)"), A[2][0:E, 0:T], ACT.Copy).then_inc(combT_done, 1)
                elif step in EVACUATES and EVACUATES[step] == "act":
                    projection(step, k)

            def experts(before):
                with act.Fori(0, E) as e:
                    n = e + (before * E + 1)
                    act.wait_ge(g_clip, n)
                    act.activation(S_, G_, ACT.Sigmoid, scale=ALPHA).then_inc(g_sig, 1)
                    act.wait_ge(wT_ready, n)
                    act.activation(wT[:, :, :].rearrange("p t c -> p (t c)"), tbank[:, 0:T], ACT.Copy).then_inc(wT_done, 1)
                    act.wait_ge(aT_ready, n)
                    act.activation(work_t[:, :], tbank[:, :], ACT.Copy).then_inc(aT_done, 1)

            experts(0)
            act.wait_ge(route_done, 1)
            n_most = act.value_load(most_i[0:1, 0:1], min_val=0, max_val=T)
            for p in range(1, T // CAP):
                with act.If(n_most > p * CAP):
                    experts(p)
            act.wait_ge(fin_res, 1)
            for t in range(TT):
                last = act.activation(squares[:, t, :], nat(RES)[:, t, :], ACT.Square, accum_out=stat[:, 16 + t:17 + t])
            last.then_inc(norm_sq, 1)
            act.wait_ge(norm_var, NORM_VAR["final"] + 1)
            act.activation(stat[:, 18:20], stat[:, 18:20], ACT.Sqrt).then_inc(norm_std, 1)

        @block.vector
        def _(dve):
            n_step = [0]

            def link(ins):
                n_step[0] += 1
                ins.then_inc(dve_step, 1)
                dve.wait_ge(dve_step, n_step[0])

            def inverse_root(step, sums, cols, n):
                dve.tensor_scalar(stat[:, cols], stat[:, sums], 1.0 / n, EPS, ALU.mult, ALU.add).then_inc(norm_var, 1)
                dve.wait_ge(norm_std, NORM_VAR[step] + 1)
                link(dve.reciprocal(stat[:, cols], stat[:, cols]))

            def normalise(step, src, dst):
                dve.wait_ge(norm_sq, NORM_SQ[step] + 1)
                c = NORM_COL[step]
                inverse_root(step, slice(c, c + 2), slice(8 + c, 10 + c), D)
                for t in range(TT):
                    last = dve.tensor_scalar(nat(dst)[:, t, :], nat(src)[:, t, :], stat[:, 8 + c + t:9 + c + t], None, ALU.mult)
                last.then_inc(norm_done, 1)

            def feature_major(step, gain, dst):
                for i in range(4):
                    n = TILE[step, 0] + i
                    dve.wait_ge(tile_ready, n + 1)
                    for j in range(2):
                        c = 2 * i + j
                        if step == "hmT":
                            last = dve.scalar_tensor_tensor(
                                fm(dst)[:, c, :], bank[n % 4][:, j * T:(j + 1) * T],
                                vec[:, VCOL["mlstm_gain"] + c:VCOL["mlstm_gain"] + c + 1], fm(OM)[:, c, :], ALU.mult, ALU.mult)
                        elif step == "hdT":
                            v = VCOL["diff_gain"]
                            last = dve.tensor_scalar(fm(dst)[:, c, :], bank[n % 4][:, j * T:(j + 1) * T],
                                                     vec[:, v:v + 1], 1.0 - LAM_INIT, ALU.mult, ALU.mult)
                        else:
                            v = VCOL[gain] + c
                            last = dve.tensor_scalar(fm(dst)[:, c, :], bank[n % 4][:, j * T:(j + 1) * T],
                                                     vec[:, v:v + 1], None, ALU.mult)
                    last.then_inc(evac["dve"], 1)

            def convolve(step):
                for c in range(4):
                    i = c + (4 if step == "km" else 0)
                    n = TILE[step, 0] + c // 2
                    dve.wait_ge(tile_ready, n + 1)
                    src = bank[n % 4][:, (c % 2) * T:(c % 2 + 1) * T]
                    chunk = c + (4 if step == "km" else 0)
                    y = work[:, i % 2, 0:T]
                    tap = [vec[:, VCOL["conv_w"] + 8 * j + chunk:VCOL["conv_w"] + 8 * j + chunk + 1] for j in range(CONV_W)]
                    link(dve.tensor_scalar(y, src, tap[3], None, ALU.mult))
                    for back in (1, 2, 3):
                        ins = dve.scalar_tensor_tensor(y[:, back:T], src[:, 0:T - back], tap[3 - back], y[:, back:T],
                                                       ALU.mult, ALU.add)
                        if back < 3:
                            link(ins)
                        else:
                            ins.then_inc(conv_out, 1)
                    dve.wait_ge(conv_sig, i + 1)
                    ins = dve.scalar_tensor_tensor(fm(QK)[:, chunk, :], y, M_DK ** -0.5 if step == "qm" else 1.0,
                                                   work[:, i % 2, T:2 * T], ALU.mult, ALU.mult)
                    if c % 2:
                        ins.then_inc(evac["dve"], 1)

            def projection(step, k):
                for i in range(2):
                    n = TILE[step, k] + i
                    dve.wait_ge(tile_ready, n + 1)
                    src = bank[n % 4][:, :]
                    cols = slice((4 * k + 2 * i) * T, (4 * k + 2 * i + 2) * T)
                    if step == "kd":
                        ins = dve.tensor_copy(KD[:, cols], src)
                    elif step == "bm":
                        wait_job(dve, "gm", 1)
                        ins = dve.tensor_tensor(GM[:, cols], src, GM[:, cols], ALU.mult)
                    elif step == "bd":
                        wait_job(dve, "gd", 1)
                        link(dve.tensor_tensor(GD[:, cols], src, GD[:, cols], ALU.mult))
                        ins = dve.tensor_tensor(GM[:, cols], GD[:, cols], GM[:, cols], ALU.add)
                    else:
                        r = nat(RES)[:, i, k * BLK:(k + 1) * BLK]
                        ins = dve.tensor_tensor(r, src, r, ALU.add)
                    ins.then_inc(evac["dve"], 1)

            def route():
                logit, prob, above, equal, mask, run = (lg[:, j, :, :] for j in range(6))
                dve.wait_ge(lg_ready, 1)
                link(dve.tensor_copy(logit, A[0][:, 0:TT * E].rearrange("p (t e) -> p t e", t=TT)))
                for t in range(TT):
                    last = dve.max(top[:, t, :], logit[:, t, :])
                link(last)
                dve.tensor_scalar(stat[:, 24:26], top[:, :, 0], -1.0, None, ALU.mult).then_inc(lg_max, 1)
                for t in range(TT):
                    fourth = top[:, t, TOP_K - 1:TOP_K]
                    dve.tensor_scalar(above[:, t, :], logit[:, t, :], fourth, None, ALU.is_gt)
                    last = dve.tensor_scalar(equal[:, t, :], logit[:, t, :], fourth, None, ALU.is_equal)
                link(last)
                link(dve.tensor_reduce(stat[:, 26:28], above, AX.X, ALU.add))
                dve.tensor_scalar(stat[:, 26:28], stat[:, 26:28], -1.0, float(TOP_K), ALU.mult, ALU.add)
                for t in range(TT):
                    last = dve.tensor_tensor_scan(run[:, t, :], ones[:, 0:E], equal[:, t, :], 0.0, ALU.mult, ALU.add)
                link(last)
                for t in range(TT):
                    last = dve.scalar_tensor_tensor(mask[:, t, :], run[:, t, :], stat[:, 26 + t:27 + t], equal[:, t, :],
                                                    ALU.is_le, ALU.mult)
                link(last)
                dve.tensor_tensor(mask, mask, above, ALU.add).then_inc(mask_ready, 1)
                dve.wait_ge(mask_ready, 1)
                dve.wait_ge(lg_exp, 1)
                link(dve.tensor_tensor(prob, prob, mask, ALU.mult))
                link(dve.tensor_reduce(stat[:, 28:30], prob, AX.X, ALU.add))
                link(dve.reciprocal(stat[:, 28:30], stat[:, 28:30]))
                for t in range(TT):
                    last = dve.tensor_scalar(comb[:, t, 0:E], prob[:, t, :], stat[:, 28 + t:29 + t], None, ALU.mult)
                last.then_inc(comb_ready, 1)
                dve.wait_ge(rank_ready, 1)
                places = A[1][:, 0:TT * E].rearrange("p (t e) -> p t e", t=TT)
                link(dve.scalar_tensor_tensor(rank[:, :, 0:E], places, 1.0, mask, ALU.add, ALU.mult))
                link(dve.tensor_scalar(rank[:, :, 0:E], rank[:, :, 0:E], -1.0, None, ALU.add))
                link(dve.tensor_reduce(most[:, 0:1], A[1][:, TT * E:(TT + 1) * E], AX.X, ALU.max))
                dve.tensor_copy(most_i[:, :], most[:, 0:1]).then_inc(route_done, 1)

            for step, k in ORDER:
                if step == "vectors":
                    dve.wait_ge(small_in, 16 * N_SMALL)
                    dve.wait_ge(consts_done, CONSTS)
                    for j in range(2):
                        last = dve.tensor_tensor_reduce(
                            out=lam_w[:, :], in0=lam_row[:, 2 * j * D_DH:(2 * j + 1) * D_DH],
                            in1=lam_row[:, (2 * j + 1) * D_DH:(2 * j + 2) * D_DH], scale=1.0, scalar=0.0,
                            op0=ALU.mult, op1=ALU.add, accum_out=lam_s[:, j:j + 1])
                        last.then_inc(lam_sum, 1)
                        dve.wait_ge(lam_sum, j + 1)
                    dve.wait_ge(lam_exp, 1)
                    link(dve.tensor_tensor(lam_s[:, 0:1], lam_s[:, 3:4], lam_s[:, 2:3], ALU.subtract))
                    dve.tensor_scalar(lam_s[:, 1:2], lam_s[:, 0:1], -LAM_INIT, None, ALU.add).then_inc(lam_set, 1)
                    dve.wait_ge(vec_ready, 1)
                    dve.tensor_copy(vec[:, :], A[3][:, 0:NVEC]).then_inc(vec_cols, 1)
                    dve.wait_ge(vec_cols, 1)
                elif step == "normx":
                    normalise(step, RES, HD)
                elif step == "xT":
                    feature_major(step, "norm_mix", HT)
                elif step in ("qm", "km"):
                    convolve(step)
                elif step == "gates":
                    dve.wait_ge(if_ready, 1)
                    dve.tensor_scalar(gate[:, 0, :], A[0][0:M_HEADS, 0:T], b_if_c[:, 0:1], None, ALU.add)
                    link(dve.tensor_scalar(gate[:, 1, :], A[0][0:M_HEADS, T:2 * T], b_if_c[:, 1:2], None, ALU.add))
                    dve.scalar_tensor_tensor(gate[:, 2, :], gate[:, 1, :], -1.0, gate[:, 1, :], ALU.mult,
                                             ALU.max).then_inc(f_abs, 1)
                    link(dve.tensor_scalar(gate[:, 3, :], gate[:, 1, :], 0.0, None, ALU.min))
                    dve.wait_ge(f_ln, 1)
                    link(dve.tensor_tensor(gate[:, 3, :], gate[:, 3, :], gate[:, 2, :], ALU.subtract))
                    link(dve.tensor_tensor_scan(gate[:, 4, :], ones[0:M_HEADS, :], gate[:, 3, :], 0.0, ALU.mult, ALU.add))
                    link(dve.tensor_tensor(gate[:, 0, :], gate[:, 0, :], gate[:, 4, :], ALU.subtract))
                    link(dve.tensor_tensor_scan(gate[:, 5, :], gate[:, 0, :], gate[:, 0, :], 0.0, ALU.max, ALU.max))
                    dve.tensor_tensor(gate[:, 6, :], gate[:, 4, :], gate[:, 5, :], ALU.add).then_inc(bm_ready, 1)
                elif step == "gates2":
                    pass
                elif step == "mls":
                    if k == 0:
                        dve.wait_ge(gate_cols, 1)
                    if k >= 2:
                        dve.wait_ge(ml_num, k - 1)
                    d = decay[:, k % 2, :]
                    dve.tensor_scalar(d[:, 0:T], m_all[:, k, :], a_em[:, 0, k:k + 1], 0.0, ALU.subtract, ALU.max)
                    dve.tensor_scalar(d[:, T:T + P], m_all[:, k, P:T], a_em[:, 1, k:k + 1], 0.0, ALU.subtract,
                                      ALU.max).then_inc(ml_gap, 1)
                    dve.wait_ge(ml_decay, k + 1)
                    for b in (0, 2):
                        last = dve.tensor_tensor(d[:, b * P:(b + 1) * P], d[:, b * P:(b + 1) * P], causal[:, :], ALU.mult)
                    link(last)
                    dve.wait_ge(ml_scores, k + 1)
                    dve.tensor_tensor(d, A[k % 2][:, 0:3 * P], d, ALU.mult).then_inc(ml_probs, 1)
                elif step == "mlo":
                    dve.wait_ge(ml_num, k + 1)
                    if k >= 2:
                        dve.wait_ge(ml_h, k - 1)
                    c = 24 + 2 * (k % 2)
                    den, em = A[k % 2][:, 3 * P:3 * P + TT], a_em[:, :, M_HEADS + k]
                    link(dve.tensor_tensor(stat[:, c:c + 2], den, em, ALU.max))
                    link(dve.scalar_tensor_tensor(stat[:, c:c + 2], den, -1.0, stat[:, c:c + 2], ALU.mult, ALU.max))
                    dve.reciprocal(stat[:, c:c + 2], stat[:, c:c + 2]).then_inc(ml_rden, 1)
                elif step == "mlnorm":
                    dve.wait_ge(ml_h, M_HEADS)
                    inverse_root(step, slice(32, 40), slice(32, 40), M_DV)
                    for j in range(2 * M_HEADS):
                        v = HM[:, j * M_DV:(j + 1) * M_DV]
                        last = dve.tensor_scalar(v, v, stat[:, 32 + j:33 + j], None, ALU.mult)
                    last.then_inc(hm_done, 1)
                elif step == "hmT":
                    wait_job(dve, "om", 1)
                    feature_major(step, None, HMT)
                elif step == "normmem":
                    normalise(step, MEMN, MEMN)
                elif step == "memT":
                    feature_major(step, "norm_mem", MEMT)
                elif step == "dfs":
                    dve.wait_ge(df_scores, k + 1)
                    if k >= 1:
                        dve.wait_ge(df_a, k)
                    for c in range(2):
                        dve.tensor_tensor_reduce(out=work[:, c, 0:P], in0=A[c][:, 0:P], in1=chunk_mask[:, 0, :], scale=1.0,
                                                 scalar=NEG, op0=ALU.add, op1=ALU.max, accum_out=stat[:, 40 + 2 * c:41 + 2 * c])
                        last = dve.tensor_tensor_reduce(
                            out=work[:, c, P:3 * P], in0=A[c][:, P:3 * P],
                            in1=chunk_mask[:, 1:3, :].rearrange("p b k -> p (b k)"), scale=1.0,
                            scalar=NEG, op0=ALU.add, op1=ALU.max, accum_out=stat[:, 41 + 2 * c:42 + 2 * c])
                    link(last)
                    dve.tensor_scalar(stat[:, 40:44], stat[:, 40:44], -(D_DH ** -0.5), None, ALU.mult).then_inc(df_max, 1)
                    dve.wait_ge(df_exp, k + 1)
                    link(dve.reciprocal(stat[:, 44:48], stat[:, 44:48]))
                    link(dve.tensor_scalar(stat[:, 46:48], stat[:, 46:48], neg_lam[:, 0:1], None, ALU.mult))
                    if k >= 1:
                        dve.wait_ge(df_aT, k)
                    for t, cols in ((0, slice(0, P)), (1, slice(P, 3 * P))):
                        link(dve.tensor_scalar(work[:, 2, cols], work[:, 1, cols], stat[:, 46 + t:47 + t], None, ALU.mult))
                        last = dve.scalar_tensor_tensor(work[:, 3, cols], work[:, 0, cols], stat[:, 44 + t:45 + t],
                                                        work[:, 2, cols], ALU.mult, ALU.add)
                    last.then_inc(df_a, 1)
                elif step == "dfnorm":
                    dve.wait_ge(df_h, D_HEADS)
                    for t in range(TT):
                        link(dve.tensor_tensor(squares[:, t, :], nat(HD)[:, t, :], nat(HD)[:, t, :], ALU.mult))
                        link(dve.tensor_reduce(stat[:, 48 + 8 * t:56 + 8 * t], squares[:, t, :].rearrange("p (h d) -> p h d", d=P),
                                               AX.X, ALU.add))
                    inverse_root(step, slice(48, 64), slice(48, 64), P)
                    for j in range(TT * D_HEADS):
                        v = HD[:, j * P:(j + 1) * P]
                        last = dve.tensor_scalar(v, v, stat[:, 48 + j:49 + j], None, ALU.mult)
                    last.then_inc(hd_done, 1)
                elif step == "hdT":
                    feature_major(step, None, HDT)
                elif step == "norm1":
                    normalise(step, RES, NRM)
                elif step == "x1T":
                    feature_major(step, "norm_xattn", HT)
                elif step == "xas":
                    dve.wait_ge(xa_scores, k + 1)
                    s = 40 + 4 * (k % 2)
                    if k >= 2:
                        dve.wait_ge(xa_h, k - 1)
                    link(dve.tensor_reduce(stat[:, s:s + 2], A[k % 2][:, :].rearrange("p (t m) -> p t m", t=TT), AX.X, ALU.max))
                    dve.tensor_scalar(stat[:, s:s + 2], stat[:, s:s + 2], -(X_DH ** -0.5), None, ALU.mult).then_inc(xa_max, 1)
                    dve.wait_ge(xa_exp, k + 1)
                    dve.reciprocal(stat[:, s + 2:s + 4], stat[:, s + 2:s + 4]).then_inc(xa_rec, 1)
                elif step == "norm2":
                    normalise(step, RES, H2)
                elif step == "x2T":
                    feature_major(step, "norm_ffn", HT)
                elif step == "route":
                    route()
                elif step in EVACUATES and EVACUATES[step] == "dve":
                    projection(step, k)

            def place_tokens(column):
                for t in range(TT):
                    last = dve.tensor_scalar(pick[:, t, :], slot_no[:, 0:CAP], rank[:, t, column], None, ALU.is_equal)
                last.then_inc(pick_ready, 1)

            def gathered(value):
                dve.wait_ge(xg_ready, value)
                gain = vec[:, VCOL["norm_ffn"]:VCOL["norm_ffn"] + KC]
                dve.tensor_tensor(xg[:, :, :], xbank[:, :].rearrange("p (k c) -> p k c", c=CAP),
                                  gain.unsqueeze(2).to_broadcast([P, KC, CAP]), ALU.mult).then_inc(xg_done, 1)

            def experts(before):
                made = before * (E + 1)
                if before:
                    dve.tensor_scalar(rank[:, :, :], rank[:, :, :], -float(CAP), None, ALU.add).then_inc(rank_moved, 1)
                    dve.wait_ge(rank_moved, before)
                    dve.wait_ge(xg_ready, made)
                place_tokens(slice(0, 1))
                gathered(made + 1)
                with dve.Fori(0, E) as e:
                    n = e + (before * E + 1)
                    for t in range(TT):
                        last = dve.tensor_scalar(pickw[:, t, :], slot_no[:, :], rank[:, t, bass.ds(e, 1)],
                                                 comb[:, t, bass.ds(e, 1)], ALU.is_equal, ALU.mult)
                    last.then_inc(pickw_ready, 1)
                    dve.wait_ge(xg_ready, e + (made + 1))
                    place_tokens(bass.ds(e + 1, 1))
                    dve.wait_ge(g_ready, n)
                    dve.tensor_scalar(G_, gbank[:, :], LIMIT, None, ALU.min).then_inc(g_clip, 1)
                    dve.wait_ge(u_ready, n)
                    dve.tensor_scalar(U_, ubank[:, :], LIMIT, -LIMIT, ALU.min, ALU.max)
                    dve.wait_ge(g_sig, n)
                    dve.tensor_tensor(S_, S_, G_, ALU.mult).then_inc(gs_done, 1)
                    dve.wait_ge(gs_done, n)
                    dve.scalar_tensor_tensor(A_, U_, 1.0, S_, ALU.add, ALU.mult).then_inc(a_ready, 1)
                    gathered(e + (made + 2))
                    dve.wait_ge(y_ready, n)
                    dve.tensor_copy(y_sb, tbank[:, :]).then_inc(y_done, 1)
                dve.wait_ge(added, (before + 1) * E)

            dve.wait_ge(route_done, 1)
            experts(0)
            n_most = dve.value_load(most_i[0:1, 0:1], min_val=0, max_val=T)
            for p in range(1, T // CAP):
                with dve.If(n_most > p * CAP):
                    experts(p)
            for t in range(TT):
                for h in range(2):
                    r = nat(RES)[:, t, h * HALF:(h + 1) * HALF]
                    last = dve.tensor_tensor(r, bank[2 * t + h][:, :], r, ALU.add)
            last.then_inc(fin_res, 1)
            dve.wait_ge(norm_sq, len(NORM_SQ) + 1)
            inverse_root("final", slice(16, 18), slice(18, 20), D)
            for t in range(TT):
                r = nat(RES)[:, t, :]
                dve.scalar_tensor_tensor(r, r, stat[:, 18 + t:19 + t], fin_gain[:, :], ALU.mult, ALU.mult).then_inc(out_ready, 1)

        @block.tensor
        def _(pe):
            pe.wait_ge(consts_done, CONSTS)
            pe.wait_ge(small_in, 16 * N_SMALL)

            inputs = {"kx": (MEMT, "memT", 0), "vx": (MEMT, "memT", 0), "bm": (HMT, "hmT", 0), "bd": (HDT, "hdT", 0),
                      "out": (GM, "bd", 1), "qx": (HT, "x1T", 0), "wo": (OXT, "oxT", 0)}
            natural = {"xT": HD, "hmT": HM, "memT": MEMN, "hdT": HD, "x1T": NRM, "oxT": OX, "x2T": H2}
            norm_of = {"xT": "normx", "memT": "normmem", "x1T": "norm1", "x2T": "norm2"}
            NORMS = {step: i for i, step in enumerate(s for s, _ in ORDER if s in NORM_SQ)}

            def transpose_all(step):
                src = nat(natural[step])
                if step in norm_of:
                    pe.wait_ge(norm_done, NORMS[norm_of[step]] + 1)
                elif step == "hmT":
                    pe.wait_ge(hm_done, 1)
                elif step == "hdT":
                    pe.wait_ge(hd_done, 1)
                else:
                    pe.wait_ge(xa_h, X_HEADS)
                for i in range(4):
                    n = TILE[step, 0] + i
                    wait_evacuated(pe, n - 4)
                    for j in range(2):
                        for t in range(TT):
                            c = 2 * i + j
                            last = pe.transpose(bank[n % 4][:, j * T + t * P:j * T + (t + 1) * P],
                                                src[:, t, c * P:(c + 1) * P], ident[:, :])
                    last.then_inc(tile_ready, 1)

            def projection(step, k):
                act_in, job, jk = inputs.get(step, (HT, "xT", 0))
                wait_job(pe, job, jk)
                b = BLOCKS.index((step, k))
                slot = b % SLOTS
                pe.wait_ge(w_loaded[slot], 16 * (b // SLOTS + 1))
                w = ring[:, slot, :].rearrange("p (k n) -> p k n", k=KC)
                for i in range(2):
                    n = TILE[step, k] + i
                    wait_evacuated(pe, n - 4)
                    if step in TOKEN_MAJOR:
                        for kk in range(KC):
                            last = pe.matmul(bank[n % 4][:, :], fm(act_in)[:, kk, i * P:(i + 1) * P], w[:, kk, :],
                                             start=kk == 0, stop=kk == KC - 1)
                    else:
                        for j in range(2):
                            for kk in range(KC):
                                c = 2 * i + j
                                last = pe.matmul(bank[n % 4][:, j * T:(j + 1) * T], w[:, kk, c * P:(c + 1) * P],
                                                 fm(act_in)[:, kk, :], start=kk == 0, stop=kk == KC - 1)
                    last.then_inc(tile_ready, 1)

            def one(out, lhsT, rhs):
                return pe.matmul(out, lhsT, rhs, start=True, stop=True)

            for step, k in ORDER:
                if step == "vectors":
                    pe.transpose(A[3][:, 0:NVEC], vec_rows[:, :], ident[0:NVEC, 0:NVEC]).then_inc(vec_ready, 1)
                    pe.wait_ge(lam_set, 1)
                    for h in range(2):
                        one(A[h][:, :], ones[0:1, 0:P], fin_row[0:1, h * HALF:(h + 1) * HALF])
                    one(A[2][:, 0:1], ones[0:1, 0:P], lam_s[0:1, 1:2]).then_inc(lam_bc, 1)
                elif step in TRANSPOSES:
                    transpose_all(step)
                elif step in EVACUATES:
                    projection(step, k)
                elif step == "gates":
                    wait_job(pe, "xT")
                    pe.wait_ge(vec_done, 1)
                    for g in range(2):
                        for kk in range(KC):
                            last = pe.matmul(A[0][0:M_HEADS, g * T:(g + 1) * T], w_if[:, kk, g * M_HEADS:(g + 1) * M_HEADS],
                                             fm(HT)[:, kk, :], start=kk == 0, stop=kk == KC - 1)
                    last.then_inc(if_ready, 1)
                elif step == "gates2":
                    pe.wait_ge(em_ready, 1)
                    for h in range(M_HEADS):
                        one(A[h // 2][:, (h % 2) * T:(h % 2 + 1) * T], head_row[:, h, :], gate[:, 5, :])
                    for t in range(TT):
                        for j, row in ((0, 0), (1, 6)):
                            c = (2 * t + j) * M_HEADS
                            last = pe.transpose(A[2][:, c:c + M_HEADS], gate[:, row, t * P:(t + 1) * P],
                                                ident[0:M_HEADS, 0:M_HEADS])
                    last.then_inc(gate_bc, 1)
                elif step == "mls":
                    wait_job(pe, "km")
                    if k == 0:
                        pe.wait_ge(gate_cols, 1)
                    if k >= 2:
                        pe.wait_ge(ml_rden, k - 1)
                    q, key = fm(QK)[:, k, :], fm(QK)[:, M_HEADS + k, :]
                    one(A[k % 2][:, 0:T], key[:, 0:P], q)
                    one(A[k % 2][:, T:T + P], key[:, P:T], q[:, P:T]).then_inc(ml_scores, 1)
                elif step == "mlo":
                    wait_job(pe, "vm", 1)
                    pe.wait_ge(ml_probs, k + 1)
                    if k >= 2:
                        pe.wait_ge(ml_h, k - 1)
                    w, num, den = decay[:, k % 2, :], A[2 + k % 2], A[k % 2]
                    v = [nat(VM)[:, t, k * M_DV:(k + 1) * M_DV] for t in range(TT)]
                    for rhs, dst in ((v, [num[:, t * M_DV:(t + 1) * M_DV] for t in range(TT)]),
                                     ([ones[:, 0:1]] * TT, [den[:, 3 * P + t:3 * P + t + 1] for t in range(TT)])):
                        one(dst[0], w[:, 0:P], rhs[0])
                        pe.matmul(dst[1], w[:, P:2 * P], rhs[0], start=True, stop=False)
                        last = pe.matmul(dst[1], w[:, 2 * P:3 * P], rhs[1], start=False, stop=True)
                    last.then_inc(ml_num, 1)
                elif step == "dfs":
                    wait_job(pe, "kd", 1)
                    if k >= 1:
                        pe.wait_ge(df_max, k)
                    for cols, qs, ks in ((slice(0, P), slice(0, P), slice(0, P)), (slice(P, 3 * P), slice(P, T), slice(0, T))):
                        for c in range(2):
                            rows = slice(c * D_DH, (c + 1) * D_DH)
                            last = one(A[c][:, cols], fm(QD)[rows, k, qs], fm(KD)[rows, k, ks])
                    last.then_inc(df_scores, 1)
                elif step == "dfo":
                    wait_job(pe, "vd", 1)
                    pe.wait_ge(df_a, k + 1)
                    if k >= 1:
                        pe.wait_ge(df_aTs, k)
                    for b in range(3):
                        last = pe.transpose(A[2][:, b * P:(b + 1) * P], work[:, 3, b * P:(b + 1) * P], ident[:, :])
                    last.then_inc(df_aT, 1)
                    pe.wait_ge(df_aTs, k + 1)
                    if k >= 2:
                        pe.wait_ge(df_h, k - 1)
                    o = A[3][:, (k % 2) * T:(k % 2 + 1) * T]
                    v = [nat(VD)[:, t, k * P:(k + 1) * P] for t in range(TT)]
                    one(o[:, 0:P], work_t[:, 0:P], v[0])
                    pe.matmul(o[:, P:T], work_t[:, P:2 * P], v[0], start=True, stop=False)
                    pe.matmul(o[:, P:T], work_t[:, 2 * P:3 * P], v[1], start=False, stop=True).then_inc(df_o, 1)
                elif step == "xas":
                    wait_job(pe, "qx", 1)
                    wait_job(pe, "kx", 1)
                    if k >= 2:
                        pe.wait_ge(xa_exp, k - 1)
                    for t in range(TT):
                        for j in range(2):
                            last = pe.matmul(A[k % 2][:, t * T:(t + 1) * T], fm(QX)[:, 2 * k + j, t * P:(t + 1) * P],
                                             fm(KX)[:, 2 * k + j, :], start=j == 0, stop=j == 1)
                    last.then_inc(xa_scores, 1)
                elif step == "xao":
                    wait_job(pe, "vx", 1)
                    pe.wait_ge(xa_exp, k + 1)
                    if k >= 1:
                        pe.wait_ge(xa_pTs, k)
                    for m in range(TT):
                        for t in range(TT):
                            c = (2 * m + t) * P
                            last = pe.transpose(A[2][:, c:c + P], work[:, k % 2, t * X_DH + m * P:t * X_DH + (m + 1) * P],
                                                ident[:, :])
                    last.then_inc(xa_pT, 1)
                    pe.wait_ge(xa_pTs, k + 1)
                    if k >= 1:
                        pe.wait_ge(xa_h, k)
                    for t in range(TT):
                        for m in range(TT):
                            c = (2 * m + t) * P
                            last = pe.matmul(A[3][:, t * X_DH:(t + 1) * X_DH], work_t[:, c:c + P],
                                             nat(VX)[:, m, k * X_DH:(k + 1) * X_DH], start=m == 0, stop=m == 1)
                    last.then_inc(xa_o, 1)
                elif step == "route":
                    wait_job(pe, "x2T")
                    for t in range(TT):
                        for kk in range(KC):
                            pe.matmul(A[0][:, t * E:(t + 1) * E], fm(HT)[:, kk, t * P:(t + 1) * P], w_r[:, kk, :],
                                      start=kk == 0, stop=False)
                        last = pe.matmul(A[0][:, t * E:(t + 1) * E], ones[0:1, 0:P], b_r[0:1, :], start=False, stop=True)
                    last.then_inc(lg_ready, 1)
                    pe.wait_ge(mask_ready, 1)
                    mask = lg[:, 4, :, :]
                    one(A[1][:, 0:E], strict[:, :], mask[:, 0, :])
                    for c, last_lhs in ((E, strict), (2 * E, ones)):
                        pe.matmul(A[1][:, c:c + E], ones[:, 0:P], mask[:, 0, :], start=True, stop=False)
                        last = pe.matmul(A[1][:, c:c + E], last_lhs[:, 0:P], mask[:, 1, :], start=False, stop=True)
                    last.then_inc(rank_ready, 1)
                    pe.wait_ge(comb_ready, 1)
                    for t in range(TT):
                        last = pe.transpose(A[2][0:E, t * P:(t + 1) * P], comb[:, t, 0:E], ident[:, :])
                    last.then_inc(combT_ready, 1)
                    pe.wait_ge(combT_done, 1)
                    pe.wait_ge(bias_in, 32)
                    for n in range(len(OWNER) - 4, len(OWNER)):
                        wait_evacuated(pe, n)
                    for t in range(TT):
                        for h in range(2):
                            pe.matmul(bank[2 * t + h][:, :], combT[:, t, :], bdn[:, h * HALF:(h + 1) * HALF],
                                      start=True, stop=False, skip_group_check=True)

            def gather():
                for kk in range(KC):
                    for t in range(TT):
                        last = pe.matmul(xbank[:, kk * CAP:(kk + 1) * CAP], nat(H2)[:, t, kk * P:(kk + 1) * P],
                                         pick[:, t, :], start=t == 0, stop=t == TT - 1)
                last.then_inc(xg_ready, 1)

            def experts(before):
                made = before * (E + 1)
                pe.wait_ge(pick_ready, made + 1)
                if before:
                    pe.wait_ge(xg_done, made)
                gather()
                with pe.Fori(0, E) as e:
                    n = e + (before * E + 1)
                    arrived = (e + (before * E + 1 + NB // SLOTS)) * 16
                    pe.wait_ge(xg_done, e + (made + 1))
                    for part, dst, ready in ((0, gbank, g_ready), (1, ubank, u_ready)):
                        for h in range(2):
                            j = 2 * part + h
                            pe.wait_ge(w_loaded[j], arrived)
                            for kk in range(4):
                                for half in range(2):
                                    last = pe.matmul(dst[half * CAP:(half + 1) * CAP, :], xg[:, 4 * h + kk, :],
                                                     ring[:, j, kk * D + half * HALF:kk * D + (half + 1) * HALF],
                                                     start=4 * h + kk == 0, stop=False)
                            last.then_inc(w_used[j], 1)
                        if part == 0:
                            pe.wait_ge(sel_ready, n)
                        for half in range(2):
                            c = part * D + half * HALF
                            last = pe.matmul(dst[half * CAP:(half + 1) * CAP, :], sel[:, :], bgu[:, c:c + HALF],
                                             start=False, stop=True)
                        last.then_inc(ready, 1)
                    pe.wait_ge(pick_ready, e + (made + 2))
                    gather()
                    pe.wait_ge(pickw_ready, n)
                    for t in range(TT):
                        last = pe.transpose(tbank[:, t * P:(t + 1) * P], pickw[:, t, :], ident[:, :])
                    last.then_inc(wT_ready, 1)
                    pe.wait_ge(wT_done, n)
                    pe.wait_ge(a_ready, n)
                    for c in range(4):
                        last = pe.transpose(tbank[:, c * P:(c + 1) * P], A_[:, c * P:(c + 1) * P], ident[:, :])
                    last.then_inc(aT_ready, 1)
                    pe.wait_ge(aT_done, n)
                    for h in range(2):
                        pe.wait_ge(w_loaded[4 + h], arrived)
                        for c in range(4):
                            for half in range(2):
                                last = pe.matmul(tbank[half * CAP:(half + 1) * CAP, :],
                                                 work_t[:, c * P + h * CAP:c * P + (h + 1) * CAP],
                                                 ring[:, 4 + h, c * D + half * HALF:c * D + (half + 1) * HALF],
                                                 start=4 * h + c == 0, stop=4 * h + c == 7)
                        last.then_inc(w_used[4] if h == 0 else y_ready, 1)
                    pe.wait_ge(y_done, n)
                    for t in range(TT):
                        for h in range(2):
                            rows = slice(h * CAP, (h + 1) * CAP)
                            last = pe.matmul(bank[2 * t + h][:, :], wT[rows, t, :], y_sb[rows, :],
                                             start=False, stop=False, skip_group_check=True)
                    last.then_inc(added, 1)

            experts(0)
            n_most = pe.value_load(most_i[0:1, 0:1], min_val=0, max_val=T)
            for p in range(1, T // CAP):
                with pe.If(n_most > p * CAP):
                    experts(p)


_INS = ["x", "mem", "norm_mix", "w_in", "conv_w", "b_if", "mlstm_gain", "diff_lambda", "diff_gain", "w_branch_m",
        "w_branch_d", "b_gate", "w_out", "norm_xattn", "norm_mem", "wq_x", "wkv_x", "wo_x", "norm_ffn", "w_router",
        "b_router", "w_gu", "b_gu", "w_dn", "b_dn", "norm_final"]


def kernel(**inputs):
    import numpy as np
    import concourse.bacc as bacc
    from concourse.bass_utils import run_bass_kernel_spmd

    nc = bacc.Bacc("TRN2", target_bir_lowering=False, num_devices=1)
    arrays, args = {}, []
    for name in _INS:
        a = np.ascontiguousarray(inputs[name])
        arrays[f"in_{name}"] = a
        args.append(nc.dram_tensor(f"in_{name}", a.shape, mybir.dt.from_np(a.dtype), kind="ExternalInput").ap())
    args.append(nc.dram_tensor("out_0", (1, T, D), mybir.dt.float32, kind="ExternalOutput").ap())
    program(nc, *args)
    r = run_bass_kernel_spmd(nc, [arrays], core_ids=[0])
    return r.results[0]["out_0"]
```

```python
from contextlib import ExitStack

import concourse.bass as bass
from concourse import mybir

P = 128
D = 1024
T = 256
TT = T // P
KC = D // P
BLK = 512
SLOTS = 6
EPS = 1e-6
M_HEADS, M_DK, M_DV = 4, 128, 256
D_HEADS, D_DH = 8, 64
X_HEADS, X_DH = 4, 256
E, TOP_K = 32, 4
CAP = 64
HALF = D // 2
LIMIT, ALPHA = 7.0, 1.702
LAM_INIT = 0.8 - 0.6
CONV_W = 4
NEG = -1e30
IF_COL = 3072
COL = {"qm": 0, "km": 512, "vm": 1024, "om": 2048, "qd": 3080, "kd": 4104, "vd": 5128, "gm": 6152, "gd": 7176}

VECS = [("norm_mix", 8), ("norm_xattn", 8), ("norm_mem", 8), ("norm_ffn", 8), ("mlstm_gain", 8),
        ("diff_gain", 1), ("b_gate", 16), ("conv_w", 32)]
VCOL, NVEC = {}, 0
for _name, _n in VECS:
    VCOL[_name] = NVEC
    NVEC += _n

EVACUATES = {
    "xT": "dve", "qm": "dve", "km": "dve", "vm": "act", "om": "act", "qd": "act", "kd": "act", "vd": "act",
    "hmT": "dve", "memT": "dve", "kx": "act", "vx": "act", "gm": "act", "bm": "dve", "hdT": "dve",
    "gd": "act", "bd": "dve", "out": "dve", "x1T": "dve", "qx": "act", "wo": "dve", "x2T": "dve",
}
TRANSPOSES = ("xT", "hmT", "memT", "hdT", "x1T", "x2T")
TOKEN_MAJOR = ("vm", "vd", "vx", "out", "wo")


def numbered(steps):
    count, out = {}, []
    for step in steps.split():
        out.append((step, count.get(step, 0)))
        count[step] = out[-1][1] + 1
    return out


ORDER = numbered("""
    normx vectors split xT   split qm gates   split km gates2
    split vm mls   split vm mls mlo   split om mls mlo   split om mls mlo   split qd mlo
    split qd mlnorm   split kd hmT   split kd
    dfs split dfa vd   dft dfs dfo split dfa vd   dft dfs dfo split dfa gm   dft dfs dfo split dfa gm
    dft dfs dfo split dfa bm   dft dfs dfo split dfa bm   dft dfs dfo split normmem dfa gd
    dft dfs dfo split dfa gd   dft dfo memT
    split dfnorm kx   hdT split kx   split bd   split bd   split vx   split out   split out
    norm1 split vx   x1T split qx   split qx
    xas xas xat xas xao xat xas xao xat xao xat xao
    split wo norm2 wo x2T norm2 x2T route
""")


def tiles_of(step):
    return 4 if step in TRANSPOSES and step != "x2T" else 2


def nth(events):
    return {x: i for i, x in enumerate(x for x in ORDER if x[0] in events)}


NORM_SQ = nth(("normx", "normmem", "norm1", "norm2"))
NORM_VAR = nth(("normx", "normmem", "norm1", "norm2", "mlnorm", "dfnorm"))
NORM_VAR["final", 0] = len(NORM_VAR)
NORM_COL = {"normx": 0, "norm1": 2, "norm2": 4, "normmem": 6}


def plan():
    first, owner, blocks = {}, [], []
    count = {"act": 0, "dve": 0}
    for step, k in ORDER:
        if step not in EVACUATES:
            continue
        first[step, k] = len(owner)
        for _ in range(tiles_of(step)):
            count[EVACUATES[step]] += 1
            owner.append((EVACUATES[step], count[EVACUATES[step]]))
        if step not in TRANSPOSES:
            blocks.append((step, k))
    return first, owner, blocks


TILE, OWNER, BLOCKS = plan()
NB = len(BLOCKS)


def program(nc, x, mem, norm_mix, w_in, conv_w, b_if, mlstm_gain, diff_lambda, diff_gain, w_branch_m,
            w_branch_d, b_gate, w_out, norm_xattn, norm_mem, wq_x, wkv_x, wo_x, norm_ffn, w_router,
            b_router, w_gu, b_gu, w_dn, b_dn, norm_final, out):
    f32, f32r, i32 = mybir.dt.float32, mybir.dt.float32r, mybir.dt.int32
    ALU, ACT, AX = mybir.AluOpType, mybir.ActivationFunctionType, mybir.AxisListType
    assert NB % 2 == 0 and BLOCKS[-2:] == [("wo", 0), ("wo", 1)]

    ctx = ExitStack()
    with ctx:
        def sb(name, shape, dt=f32):
            return ctx.enter_context(nc.sbuf_tensor(name, shape, dt))

        def sem(name):
            return ctx.enter_context(nc.semaphore(name))

        base = (nc.sbuf_base + 31) // 32 * 32
        BLOCK_BYTES, MAT_BYTES = KC * BLK * 4, TT * D * 4
        arena = sb("arena", [P, (SLOTS * BLOCK_BYTES + 11 * MAT_BYTES) // 4])
        assert nc.sbuf_base == base + 4 * arena.shape[1]

        def at(name, shape, offset, dt=f32):
            return nc.alloc_sbuf_tensor_at(name, shape, dt, offset=base + offset)

        ring = at("ring", [P, SLOTS, KC * BLK], 0)
        halves = at("halves", [P, 2, 2, KC * BLK], 2 * BLOCK_BYTES, f32r)
        mat = [at(f"mat{i}", [P, TT * D], SLOTS * BLOCK_BYTES + i * MAT_BYTES) for i in range(11)]

        def pair(i):
            return [at(f"{part}{i}", [P, TT * D], SLOTS * BLOCK_BYTES + (i + j) * MAT_BYTES, f32r)
                    for j, part in enumerate(("hi", "lo"))]

        pair1, pair3, pair7 = pair(1), pair(3), pair(7)
        RES, X2T, QK, VM, HM, OM, QD, KD, VD, GM = (mat[i] for i in (0, 1, 3, 4, 5, 6, 7, 8, 9, 10))
        XN, MEMN, HD, GD, KX, VX, NRM, QX = (mat[i] for i in (9, 3, 5, 6, 9, 6, 5, 10))
        XT, MEMT = pair1, pair1
        HMT, MIX, OXT = pair3, pair3, pair3
        HDT, X1T = pair7, pair7

        def nat(m):
            return m[:, :].rearrange("p (t d) -> p t d", t=TT)

        def fm(m):
            return m[:, :].rearrange("p (c t) -> p c t", t=T)

        ident = sb("ident", [P, P])
        ones = sb("ones", [P, T])
        strict = sb("strict", [P, P])
        causal = sb("causal", [P, P])
        chunk_mask = sb("chunk_mask", [P, 3, P])
        slot_no = sb("slot_no", [P, 2 * CAP])
        head_row = QD[0:M_HEADS, 0:M_HEADS * P].rearrange("h (j p) -> h j p", p=P)
        vec_rows = sb("vec_rows", [NVEC, P])
        vec = sb("vec", [P, NVEC])
        w_if = sb("w_if", [P, KC, 2 * M_HEADS])
        if_nat = sb("if_nat", [P, TT * 2 * M_HEADS])
        b_if_c = sb("b_if_c", [M_HEADS, 2])
        lam_row = sb("lam_row", [1, 4 * D_DH])
        lam_w = sb("lam_w", [1, D_DH])
        lam_s = sb("lam_s", [1, 4])
        neg_lam = sb("neg_lam", [P, 1])
        w_r = sb("w_r", [P, KC, E])
        b_r = sb("b_r", [1, E])
        fin_gain = sb("fin_gain", [P, D])
        stat = sb("stat", [P, 64])
        gate = OM[0:M_HEADS, :].rearrange("h (j t) -> h j t", t=T)
        a_em = sb("a_em", [P, TT, 2 * M_HEADS])
        m_all = GM[:, 0:M_HEADS * T].rearrange("p (h t) -> p h t", t=T)
        decay = GM[:, D:D + 6 * P].rearrange("p (b n) -> p b n", b=2)
        work = sb("work", [P, 4, BLK])
        work_t = sb("work_t", [P, BLK])
        squares = work[:, :, :].rearrange("p (t a) n -> p t (a n)", t=TT)
        fin_row = GM[0:1, 0:D]
        bgu = KX
        bdn = VX[0:E, 0:D]

        bank = [ctx.enter_context(nc.psum_tensor(f"bank{i}", [P, BLK], f32)) for i in range(8)]
        A = bank[4:8]

        consts_done = sem("consts_done")
        small_in = sem("small_in")
        x_in, mem_in = sem("x_in"), sem("mem_in")
        w_loaded = [sem(f"w_loaded{i}") for i in range(SLOTS)]
        w_used = [sem(f"w_used{i}") for i in range(SLOTS - 1)]
        tile_ready = sem("tile_ready")
        hi_made, split_made = sem("hi_made"), sem("split_made")
        hi_part = sem("hi_part")
        if_nat_ready, if_rows = sem("if_nat_ready"), sem("if_rows")
        evac = {"act": sem("evac_act"), "dve": sem("evac_dve")}
        dve_step, act_step, pool_step = sem("dve_step"), sem("act_step"), sem("pool_step")
        norm_sq, norm_var, norm_std, norm_done = sem("norm_sq"), sem("norm_var"), sem("norm_std"), sem("norm_done")
        vec_cols = sem("vec_cols")
        hm_gated, mix_sum, mix_hi, mix_done = sem("hm_gated"), sem("mix_sum"), sem("mix_hi"), sem("mix_done")
        vec_ready, vec_done = sem("vec_ready"), sem("vec_done")
        lam_sum, lam_exp, lam_set, lam_bc = sem("lam_sum"), sem("lam_exp"), sem("lam_set"), sem("lam_bc")
        conv_out, conv_sig = sem("conv_out"), sem("conv_sig")
        if_ready, f_abs, f_ln, bm_ready, em_ready, gate_rows = (
            sem("if_ready"), sem("f_abs"), sem("f_ln"), sem("bm_ready"), sem("em_ready"), sem("gate_rows"))
        gate_bc, gate_cols = sem("gate_bc"), sem("gate_cols")
        ml_gap, ml_decay, ml_scores, ml_probs, ml_num, ml_rden, ml_h = (
            sem("ml_gap"), sem("ml_decay"), sem("ml_scores"), sem("ml_probs"), sem("ml_num"), sem("ml_rden"), sem("ml_h"))
        hm_done = sem("hm_done")
        df_scores, df_max, df_exp, df_a, df_aT, df_aTs, df_o, df_h, hd_done = (
            sem("df_scores"), sem("df_max"), sem("df_exp"), sem("df_a"), sem("df_aT"), sem("df_aTs"),
            sem("df_o"), sem("df_h"), sem("hd_done"))
        xa_scores, xa_max, xa_exp, xa_p, xa_pT, xa_pTs, xa_o, xa_hi, xa_h = (
            sem("xa_scores"), sem("xa_max"), sem("xa_exp"), sem("xa_p"), sem("xa_pT"), sem("xa_pTs"), sem("xa_o"),
            sem("xa_hi"), sem("xa_h"))
        lg_ready, lg_max, lg_exp, mask_ready, rank_ready, comb_ready, combT_ready, combT_done, route_done = (
            sem("lg_ready"), sem("lg_max"), sem("lg_exp"), sem("mask_ready"), sem("rank_ready"),
            sem("comb_ready"), sem("combT_ready"), sem("combT_done"), sem("route_done"))
        pick_ready, pickw_ready, xg_ready, xg_done, sel_ready = (
            sem("pick_ready"), sem("pickw_ready"), sem("xg_ready"), sem("xg_done"), sem("sel_ready"))
        g_ready, u_ready, g_clip, g_sig, gs_done, a_ready, aT_ready, aT_done, wT_ready, wT_done = (
            sem("g_ready"), sem("u_ready"), sem("g_clip"), sem("g_sig"), sem("gs_done"), sem("a_ready"), sem("aT_ready"), sem("aT_done"),
            sem("wT_ready"), sem("wT_done"))
        y_ready, y_done, added, rank_moved = sem("y_ready"), sem("y_done"), sem("added"), sem("rank_moved")
        fin_res, out_ready, stored = (
            sem("fin_res"), sem("out_ready"), sem("stored"))
        N_SMALL, CONSTS = 14, 10
        bias_in = sem("bias_in")

        H2 = NRM
        taken = [0]

        def part(*shape, rows=P):
            n = shape[0] * shape[1]
            taken[0] += n
            return QX[0:rows, taken[0] - n:taken[0]].rearrange("p (a b) -> p a b", b=shape[1])

        xg = part(KC, CAP)
        pick = part(TT, CAP)
        pickw = part(TT, 2 * CAP)
        wT = part(TT, P)
        combT = part(TT, P, rows=E)
        lg = part(8 * TT, E).rearrange("p (j t) e -> p j t e", t=TT)
        sel = sb("sel", [P, CAP])
        rank = sb("rank", [P, TT, E + 1])
        comb = sb("comb", [P, TT, E + 1])
        top = sb("top", [P, TT, 8])
        most = sb("most", [P, 2])
        most_i = sb("most_i", [P, 1], i32)
        G_, U_, S_, A_ = (work[:, j, :] for j in range(4))
        y_sb = mat[7][:, 0:BLK]
        gbank, ubank, xbank, tbank = bank[4], bank[5], bank[6], bank[7]

        HALVED = {"xT": XT, "hmT": HMT, "memT": MEMT, "hdT": HDT, "x1T": X1T}
        HI_PART = [step for step, _ in ORDER if step in HALVED]
        GAIN = {"xT": "norm_mix", "memT": "norm_mem", "x1T": "norm_xattn"}

        def wait_evacuated(eng, n):
            if n >= 0:
                who, k = OWNER[n]
                eng.wait_ge(evac[who], k)

        def wait_job(eng, step, k=0):
            wait_evacuated(eng, TILE[step, k] + tiles_of(step) - 1)

        def block_done(eng, n):
            step, k = BLOCKS[n]
            eng.wait_ge(tile_ready, TILE["wo", 1] + k + 1 if step == "wo" else TILE[step, k] + 2)

        block = ctx.enter_context(nc.Block())

        @block.sync
        def _(sp):
            sources = {"kx": (wkv_x[0], 0), "vx": (wkv_x[0], D), "bm": (w_branch_m[0], 0), "bd": (w_branch_d[0], 0),
                       "out": (w_out[0], 0), "qx": (wq_x[0], 0), "wo": (wo_x[0], 0)}
            sp.dma_start(nat(RES), x[0].rearrange("(t p) d -> p t d", p=P)).then_inc(x_in, 16)
            sp.wait_ge(small_in, 16 * N_SMALL)
            for n, (step, k) in enumerate(BLOCKS):
                w, c = sources[step] if step in sources else (w_in[0], COL[step])
                c += k * BLK
                if n >= 2:
                    sp.wait_ge(split_made, n - 1)
                sp.dma_start(ring[:, n % 2, :].rearrange("p (k n) -> p k n", k=KC),
                             w[:, c:c + BLK].rearrange("(k p) n -> p k n", p=P)).then_inc(w_loaded[n % 2], 16)
                if (step, k) == ("gd", 1):
                    block_done(sp, BLOCKS.index(("bm", 1)))
                    sp.dma_start(nat(MEMN), mem[0].rearrange("(t p) d -> p t d", p=P)).then_inc(mem_in, 16)

            gu = w_gu[0].rearrange("e (h k p) n -> p e h k n", h=2, p=P)
            dn = w_dn[0].rearrange("e (h k p) n -> p e h k n", h=2, p=P)

            def load_block(e, j):
                part, h = j // 2, j % 2
                src = (gu[:, bass.ds(e, 1), h, :, part * D:(part + 1) * D] if part < 2
                       else dn[:, bass.ds(e, 1), h, :, :])
                sp.dma_start(ring[:, j, :].rearrange("p (k n) -> p k n", k=4),
                             src.rearrange("p e k n -> p (e k) n")).then_inc(w_loaded[j], 16)

            def stream(before, first):
                with sp.Fori(first, E) as e:
                    for j in range(SLOTS):
                        sp.wait_ge(w_used[j] if j < SLOTS - 1 else y_ready, e + before * E)
                        load_block(e, j)

            for j in range(SLOTS):
                if j < 2:
                    sp.wait_ge(split_made, NB - 1 + j)
                else:
                    block_done(sp, NB - 2 + (j - 2) // 2)
                load_block(0, j)
            stream(0, 1)
            sp.wait_ge(route_done, 1)
            n_most = sp.value_load(most_i[0:1, 0:1], min_val=0, max_val=T)
            for p in range(1, T // CAP):
                with sp.If(n_most > p * CAP):
                    stream(p, 0)
            sp.wait_ge(out_ready, TT)
            sp.dma_start(out[0].rearrange("(t p) d -> p t d", p=P), nat(RES)).then_inc(stored, 16)
            sp.wait_ge(stored, 16)

        @block.gpsimd
        def _(pool):
            steps = [0]

            def after(ins):
                steps[0] += 1
                ins.then_inc(pool_step, 1)
                pool.wait_ge(pool_step, steps[0])

            pool.memset(ones[:, :], 1.0).then_inc(consts_done, 1)
            after(pool.memset(ident[:, :], 0.0))
            pool.affine_select(out=ident[:, :], in_=ident[:, :], compare_op=ALU.not_equal, fill=1.0, base=0,
                               pattern=[[-1, P]], channel_multiplier=1).then_inc(consts_done, 1)
            after(pool.memset(strict[:, :], 1.0))
            pool.affine_select(out=strict[:, :], in_=strict[:, :], compare_op=ALU.is_gt, fill=0.0, base=0,
                               pattern=[[1, P]], channel_multiplier=-1).then_inc(consts_done, 1)
            after(pool.memset(causal[:, :], 1.0))
            pool.affine_select(out=causal[:, :], in_=causal[:, :], compare_op=ALU.is_ge, fill=0.0, base=0,
                               pattern=[[1, P]], channel_multiplier=-1).then_inc(consts_done, 1)
            after(pool.memset(chunk_mask[:, :, :], 0.0))
            for b in (0, 2):
                pool.memset(chunk_mask[0:64, b, 64:P], NEG).then_inc(consts_done, 1)
            pool.iota(slot_no[:, :], pattern=[[0, 2], [1, CAP]], base=0, channel_multiplier=0,
                      allow_small_or_imprecise_dtypes=True).then_inc(consts_done, 1)
            after(pool.memset(head_row[:, :, :], 0.0))
            pool.affine_select(out=head_row[:, :, :], in_=head_row[:, :, :], compare_op=ALU.not_equal, fill=1.0,
                               base=0, pattern=[[-1, M_HEADS], [0, P]], channel_multiplier=1).then_inc(consts_done, 1)
            pool.memset(rank[:, :, E:E + 1], -1.0).then_inc(consts_done, 1)
            pool.memset(comb[:, :, E:E + 1], 0.0).then_inc(consts_done, 1)

            def selectors(before, first):
                with pool.Fori(first, E) as e:
                    pool.wait_ge(u_ready, e + before * E)
                    pool.tensor_copy(sel[:, :], ident[:, bass.ds(e, 1)].to_broadcast([P, CAP])).then_inc(sel_ready, 1)

            pool.wait_ge(consts_done, CONSTS)
            pool.wait_ge(xa_o, X_HEADS)
            after(pool.memset(bgu[:, :], 0.0))
            pool.dma_start(bgu[0:E, :], b_gu[0]).then_inc(bias_in, 16)
            pool.dma_start(bdn, b_dn[0]).then_inc(bias_in, 16)
            pool.tensor_copy(sel[:, :], ident[:, 0:1].to_broadcast([P, CAP])).then_inc(sel_ready, 1)
            selectors(0, 1)
            pool.wait_ge(route_done, 1)
            n_most = pool.value_load(most_i[0:1, 0:1], min_val=0, max_val=T)
            for p in range(1, T // CAP):
                with pool.If(n_most > p * CAP):
                    selectors(p, 0)

        @block.scalar
        def _(act):
            n_step = [0]

            def link(ins):
                n_step[0] += 1
                ins.then_inc(act_step, 1)
                act.wait_ge(act_step, n_step[0])

            def small(dst, src):
                act.dma_start(dst, src).then_inc(small_in, 16)

            rows = {"norm_mix": norm_mix, "norm_xattn": norm_xattn, "norm_mem": norm_mem, "norm_ffn": norm_ffn,
                    "diff_gain": diff_gain, "b_gate": b_gate}
            for name, n in VECS:
                if name in rows:
                    src = rows[name].rearrange("l (r p) -> (l r) p", p=P)
                elif name == "mlstm_gain":
                    src = mlstm_gain[0].rearrange("h (r p) -> (h r) p", p=P)
                else:
                    src = conv_w[0].rearrange("j (r p) -> (j r) p", p=P)
                small(vec_rows[VCOL[name]:VCOL[name] + n, :], src)
            small(w_if[:, :, :], w_in[0][:, IF_COL:IF_COL + 2 * M_HEADS].rearrange("(k p) n -> p k n", p=P))
            act.dma_start(b_if_c[:, :], b_if[0].rearrange("(g h) -> h g", g=2),
                          allow_slow_non_contiguous=True).then_inc(small_in, 16)
            small(lam_row[:, :], diff_lambda.rearrange("l a d -> l (a d)"))
            small(w_r[:, :, :], w_router[0].rearrange("(k p) n -> p k n", p=P))
            small(b_r[:, :], b_router)
            small(fin_row, norm_final.rearrange("(l d) -> l d", l=1))

            def root_mean_square(step, k, src, tiles=range(TT), junk=squares):
                c = NORM_COL[step]
                for t in tiles:
                    last = act.activation(junk[:, t, :], nat(src)[:, t, :], ACT.Square, accum_out=stat[:, c + t:c + t + 1])
                last.then_inc(norm_sq, 1)
                root(step, k, slice(8 + c + tiles[0], 9 + c + tiles[-1]))

            def root(step, k, cols):
                act.wait_ge(norm_var, NORM_VAR[step, k] + 1)
                act.activation(stat[:, cols], stat[:, cols], ACT.Sqrt).then_inc(norm_std, 1)

            def copy_tile(n, dst, func=ACT.Copy, **kw):
                act.wait_ge(tile_ready, n + 1)
                return act.activation(dst, bank[n % 4][:, :], func, **kw)

            def split(n):
                act.wait_ge(w_loaded[n % 2], 16 * (n // 2 + 1))
                if n >= 2:
                    block_done(act, n - 2)
                for h in range(2):
                    cols = slice(h * KC * BLK // 2, (h + 1) * KC * BLK // 2)
                    act.activation(halves[:, n % 2, 0, cols], ring[:, n % 2, cols], ACT.Copy).then_inc(hi_made, 1)

            def conv_sigmoid(step):
                for c in range(4):
                    i = c + (4 if step == "km" else 0)
                    act.wait_ge(conv_out, i + 1)
                    act.activation(work[:, i % 2, T:2 * T], work[:, i % 2, 0:T], ACT.Sigmoid).then_inc(conv_sig, 1)

            def projection(step, k):
                for i in range(2):
                    n = TILE[step, k] + i
                    if step in ("om", "qd", "kd", "kx", "qx"):
                        m = {"om": OM, "qd": QD, "kd": KD, "kx": KX, "qx": QX}[step]
                        dst = m[:, (4 * k + 2 * i) * T:(4 * k + 2 * i + 2) * T]
                    elif step in ("vm", "vd", "vx"):
                        m = {"vm": VM, "vd": VD, "vx": VX}[step]
                        dst = nat(m)[:, i, k * BLK:(k + 1) * BLK]
                    if step == "vx":
                        wait_job(act, "bd", 1)
                    if step == "qx":
                        act.wait_ge(mix_done, 4)
                    if step in ("gm", "gd"):
                        act.wait_ge(tile_ready, n + 1)
                        g = GM if step == "gm" else GD
                        for j in range(2):
                            c = 4 * k + 2 * i + j
                            v = VCOL["b_gate"] + c + (KC if step == "gd" else 0)
                            last = act.activation(g[:, c * T:(c + 1) * T], bank[n % 4][:, j * T:(j + 1) * T],
                                                  ACT.Sigmoid, bias=vec[:, v:v + 1])
                        last.then_inc(evac["act"], 1)
                    elif step == "om":
                        copy_tile(n, dst, ACT.Sigmoid).then_inc(evac["act"], 1)
                    else:
                        copy_tile(n, dst).then_inc(evac["act"], 1)

            def upper_half(step):
                for i in range(4):
                    n = TILE[step, 0] + i
                    act.wait_ge(tile_ready, n + 1)
                    if step == "hmT":
                        wait_job(act, "om", 1)
                    for j in range(2):
                        c = 2 * i + j
                        src, dst = bank[n % 4][:, j * T:(j + 1) * T], fm(HALVED[step][0])[:, c, :]
                        if step == "hmT":
                            act.wait_ge(hm_gated, c + 1)
                            last = act.activation(dst, fm(OM)[:, c, :], ACT.Copy)
                        else:
                            v = VCOL["diff_gain"] if step == "hdT" else VCOL[GAIN[step]] + c
                            last = act.activation(dst, src, ACT.Copy, scale=vec[:, v:v + 1])
                    last.then_inc(hi_part, 1)

            for step, k in ORDER:
                if step == "vectors":
                    act.wait_ge(vec_cols, 1)
                    act.wait_ge(lam_sum, 2)
                    act.activation(lam_s[:, 2:4], lam_s[:, 0:2], ACT.Exp).then_inc(lam_exp, 1)
                    act.wait_ge(lam_bc, 1)
                    act.activation(neg_lam[:, :], A[2][:, 0:1], ACT.Copy)
                    act.activation(fin_gain[:, 0:BLK], A[0][:, :], ACT.Copy)
                    act.activation(fin_gain[:, BLK:D], A[1][:, :], ACT.Copy).then_inc(vec_done, 1)
                elif step == "normx":
                    act.wait_ge(x_in, 16)
                    root_mean_square(step, k, RES)
                elif step == "split":
                    split(k)
                elif step == "normmem":
                    act.wait_ge(mem_in, 16)
                    root_mean_square(step, k, MEMN, junk=nat(mat[4]))
                elif step == "norm1":
                    wait_job(act, "out", 1)
                    root_mean_square(step, k, RES)
                elif step == "norm2":
                    wait_job(act, "wo", k)
                    root_mean_square(step, k, RES, [k])
                elif step in ("qm", "km"):
                    conv_sigmoid(step)
                elif step == "gates":
                    act.wait_ge(if_ready, 1)
                    act.activation(if_nat[:, :], A[0][:, 0:TT * 2 * M_HEADS], ACT.Copy).then_inc(if_nat_ready, 1)
                    act.wait_ge(f_abs, 1)
                    link(act.activation(gate[:, 2, :], gate[:, 2, :], ACT.Exp, scale=-1.0))
                    act.activation(gate[:, 2, :], gate[:, 2, :], ACT.Ln, bias=1.0).then_inc(f_ln, 1)
                    act.wait_ge(bm_ready, 1)
                    act.activation(gate[:, 6, :], gate[:, 6, :], ACT.Exp, scale=-1.0).then_inc(em_ready, 1)
                elif step == "gates2":
                    act.wait_ge(gate_bc, 1)
                    for b in range(2):
                        act.activation(m_all[:, 2 * b:2 * b + 2, :].rearrange("p h t -> p (h t)"), A[b][:, :], ACT.Copy)
                    act.activation(a_em[:, :, :].rearrange("p t c -> p (t c)"), A[2][:, 0:4 * M_HEADS],
                                   ACT.Copy).then_inc(gate_cols, 1)
                elif step == "mls":
                    act.wait_ge(ml_gap, k + 1)
                    act.activation(decay[:, k % 2, :], decay[:, k % 2, :], ACT.Exp, scale=-1.0).then_inc(ml_decay, 1)
                elif step == "mlo":
                    act.wait_ge(ml_rden, k + 1)
                    for t in range(TT):
                        link(act.activation(nat(HM)[:, t, k * M_DV:(k + 1) * M_DV],
                                            A[2 + k % 2][:, t * M_DV:(t + 1) * M_DV], ACT.Copy,
                                            scale=stat[:, 24 + 2 * (k % 2) + t:25 + 2 * (k % 2) + t]))
                        last = act.activation(squares[:, t, 0:M_DV], nat(HM)[:, t, k * M_DV:(k + 1) * M_DV], ACT.Square,
                                              accum_out=stat[:, 32 + 4 * t + k:33 + 4 * t + k])
                    last.then_inc(ml_h, 1)
                elif step == "mlnorm":
                    root(step, k, slice(32, 40))
                elif step == "dfs":
                    act.wait_ge(df_max, k + 1)
                    if k >= 1:
                        act.wait_ge(df_a, k)
                    for c in range(2):
                        for t, cols in ((0, slice(0, P)), (1, slice(P, 3 * P))):
                            i = 40 + 2 * c + t
                            last = act.activation(work[:, c, cols], work[:, c, cols], ACT.Exp, scale=D_DH ** -0.5,
                                                  bias=stat[:, i:i + 1], accum_out=stat[:, i + 4:i + 5])
                    last.then_inc(df_exp, 1)
                elif step == "dft":
                    act.wait_ge(df_aT, k + 1)
                    act.activation(work_t[:, 0:3 * P], A[2][:, 0:3 * P], ACT.Copy).then_inc(df_aTs, 1)
                elif step == "dfo":
                    act.wait_ge(df_o, k + 1)
                    act.activation(nat(HD)[:, :, k * P:(k + 1) * P],
                                   A[3][:, (k % 2) * T:(k % 2 + 1) * T].rearrange("p (t d) -> p t d", t=TT),
                                   ACT.Copy).then_inc(df_h, 1)
                elif step == "dfnorm":
                    root(step, k, slice(48, 64))
                elif step == "xas":
                    act.wait_ge(xa_max, k + 1)
                    if k >= 2:
                        act.wait_ge(xa_pT, k - 1)
                    s = 40 + 4 * (k % 2)
                    for t in range(TT):
                        last = act.activation(work[:, k % 2, t * X_DH:(t + 1) * X_DH], A[k % 2][:, t * X_DH:(t + 1) * X_DH],
                                              ACT.Exp, scale=X_DH ** -0.5, bias=stat[:, s + t:s + t + 1],
                                              accum_out=stat[:, s + 2 + t:s + 3 + t])
                    last.then_inc(xa_exp, 1)
                elif step == "xat":
                    act.wait_ge(xa_pT, k + 1)
                    act.activation(work_t[:, :], A[2][:, :], ACT.Copy).then_inc(xa_pTs, 1)
                elif step == "xao":
                    act.wait_ge(xa_o, k + 1)
                    act.activation(OXT[0][:, 2 * k * T:(2 * k + 2) * T], A[3][:, :], ACT.Copy).then_inc(xa_hi, 1)
                elif step == "route":
                    act.wait_ge(lg_max, 1)
                    for t in range(TT):
                        last = act.activation(lg[:, 1, t, :], lg[:, 0, t, :], ACT.Exp, bias=stat[:, 24 + t:25 + t])
                    last.then_inc(lg_exp, 1)
                    act.wait_ge(combT_ready, 1)
                    act.activation(combT[:, :, :].rearrange("e t p -> e (t p)"), A[2][0:E, 0:T], ACT.Copy).then_inc(combT_done, 1)
                elif step in HALVED:
                    upper_half(step)
                elif step == "bd":
                    for i in range(2):
                        act.wait_ge(mix_sum, 2 * k + i + 1)
                        cols = slice((4 * k + 2 * i) * T, (4 * k + 2 * i + 2) * T)
                        act.activation(MIX[0][:, cols], GM[:, cols], ACT.Copy).then_inc(mix_hi, 1)
                elif step in EVACUATES and EVACUATES[step] == "act":
                    projection(step, k)

            def experts(before):
                with act.Fori(0, E) as e:
                    n = e + (before * E + 1)
                    act.wait_ge(g_clip, n)
                    act.activation(S_, G_, ACT.Sigmoid, scale=ALPHA).then_inc(g_sig, 1)
                    act.wait_ge(wT_ready, n)
                    act.activation(wT[:, :, :].rearrange("p t c -> p (t c)"), tbank[:, 0:T], ACT.Copy).then_inc(wT_done, 1)
                    act.wait_ge(aT_ready, n)
                    act.activation(work_t[:, :], tbank[:, :], ACT.Copy).then_inc(aT_done, 1)

            experts(0)
            act.wait_ge(route_done, 1)
            n_most = act.value_load(most_i[0:1, 0:1], min_val=0, max_val=T)
            for p in range(1, T // CAP):
                with act.If(n_most > p * CAP):
                    experts(p)
            act.wait_ge(fin_res, 1)
            for t in range(TT):
                last = act.activation(squares[:, t, :], nat(RES)[:, t, :], ACT.Square, accum_out=stat[:, 16 + t:17 + t])
            last.then_inc(norm_sq, 1)
            act.wait_ge(norm_var, NORM_VAR["final", 0] + 1)
            act.activation(stat[:, 18:20], stat[:, 18:20], ACT.Sqrt).then_inc(norm_std, 1)

        @block.vector
        def _(dve):
            n_step = [0]

            def link(ins):
                n_step[0] += 1
                ins.then_inc(dve_step, 1)
                dve.wait_ge(dve_step, n_step[0])

            def inverse_root(step, k, sums, cols, n):
                dve.tensor_scalar(stat[:, cols], stat[:, sums], 1.0 / n, EPS, ALU.mult, ALU.add).then_inc(norm_var, 1)
                dve.wait_ge(norm_std, NORM_VAR[step, k] + 1)
                link(dve.reciprocal(stat[:, cols], stat[:, cols]))

            def normalise(step, k, src, dst, tiles=range(TT)):
                dve.wait_ge(norm_sq, NORM_SQ[step, k] + 1)
                c = NORM_COL[step]
                a, b = tiles[0], tiles[-1] + 1
                inverse_root(step, k, slice(c + a, c + b), slice(8 + c + a, 8 + c + b), D)
                for t in tiles:
                    last = dve.tensor_scalar(nat(dst)[:, t, :], nat(src)[:, t, :], stat[:, 8 + c + t:9 + c + t], None, ALU.mult)
                last.then_inc(norm_done, 1)

            def split(n):
                for h in range(2):
                    dve.wait_ge(hi_made, 2 * n + h + 1)
                    cols = slice(h * KC * BLK // 2, (h + 1) * KC * BLK // 2)
                    last = dve.tensor_tensor(halves[:, n % 2, 1, cols], ring[:, n % 2, cols],
                                             halves[:, n % 2, 0, cols].bitcast(f32), ALU.subtract)
                last.then_inc(split_made, 1)

            def lower_half(step):
                first = HI_PART.index(step) * 4
                hi, lo = HALVED[step]
                for i in range(4):
                    n = TILE[step, 0] + i
                    dve.wait_ge(tile_ready, n + 1)
                    chunks = [(2 * i + j, bank[n % 4][:, j * T:(j + 1) * T]) for j in range(2)]
                    if step == "hmT":
                        for c, src in chunks:
                            v = VCOL["mlstm_gain"] + c
                            dve.scalar_tensor_tensor(fm(OM)[:, c, :], src, vec[:, v:v + 1], fm(OM)[:, c, :], ALU.mult,
                                                     ALU.mult).then_inc(hm_gated, 1)
                    dve.wait_ge(hi_part, first + i + 1)
                    for c, src in chunks:
                        upper, lower = fm(hi)[:, c, :].bitcast(f32), fm(lo)[:, c, :]
                        if step == "hmT":
                            last = dve.tensor_tensor(lower, fm(OM)[:, c, :], upper, ALU.subtract)
                        else:
                            v = VCOL["diff_gain"] if step == "hdT" else VCOL[GAIN[step]] + c
                            last = dve.scalar_tensor_tensor(lower, src, vec[:, v:v + 1], upper, ALU.mult, ALU.subtract)
                    last.then_inc(evac["dve"], 1)

            def convolve(step):
                for c in range(4):
                    i = c + (4 if step == "km" else 0)
                    n = TILE[step, 0] + c // 2
                    dve.wait_ge(tile_ready, n + 1)
                    src = bank[n % 4][:, (c % 2) * T:(c % 2 + 1) * T]
                    chunk = c + (4 if step == "km" else 0)
                    y = work[:, i % 2, 0:T]
                    tap = [vec[:, VCOL["conv_w"] + 8 * j + chunk:VCOL["conv_w"] + 8 * j + chunk + 1] for j in range(CONV_W)]
                    link(dve.tensor_scalar(y, src, tap[3], None, ALU.mult))
                    for back in (1, 2, 3):
                        ins = dve.scalar_tensor_tensor(y[:, back:T], src[:, 0:T - back], tap[3 - back], y[:, back:T],
                                                       ALU.mult, ALU.add)
                        if back < 3:
                            link(ins)
                        else:
                            ins.then_inc(conv_out, 1)
                    dve.wait_ge(conv_sig, i + 1)
                    ins = dve.scalar_tensor_tensor(fm(QK)[:, chunk, :], y, M_DK ** -0.5 if step == "qm" else 1.0,
                                                   work[:, i % 2, T:2 * T], ALU.mult, ALU.mult)
                    if c % 2:
                        ins.then_inc(evac["dve"], 1)

            def projection(step, k):
                for i in range(2):
                    n = TILE[step, k] + i
                    dve.wait_ge(tile_ready, n + 1)
                    src = bank[n % 4][:, :]
                    cols = slice((4 * k + 2 * i) * T, (4 * k + 2 * i + 2) * T)
                    if step == "bm":
                        wait_job(dve, "gm", 1)
                        ins = dve.tensor_tensor(GM[:, cols], src, GM[:, cols], ALU.mult)
                    elif step == "bd":
                        wait_job(dve, "gd", 1)
                        dve.tensor_tensor(GD[:, cols], src, GD[:, cols], ALU.mult).then_inc(evac["dve"], 1)
                        wait_evacuated(dve, n)
                        dve.tensor_tensor(GM[:, cols], GD[:, cols], GM[:, cols], ALU.add).then_inc(mix_sum, 1)
                        dve.wait_ge(mix_hi, 2 * k + i + 1)
                        dve.tensor_tensor(MIX[1][:, cols], GM[:, cols], MIX[0][:, cols].bitcast(f32),
                                          ALU.subtract).then_inc(mix_done, 1)
                        continue
                    elif step == "wo":
                        r = nat(RES)[:, k, i * BLK:(i + 1) * BLK]
                        ins = dve.tensor_tensor(r, src, r, ALU.add)
                    else:
                        r = nat(RES)[:, i, k * BLK:(k + 1) * BLK]
                        ins = dve.tensor_tensor(r, src, r, ALU.add)
                    ins.then_inc(evac["dve"], 1)

            def route():
                logit, prob, above, equal, mask, run = (lg[:, j, :, :] for j in range(6))
                dve.wait_ge(lg_ready, 1)
                link(dve.tensor_copy(logit, A[0][:, 0:TT * E].rearrange("p (t e) -> p t e", t=TT)))
                for t in range(TT):
                    last = dve.max(top[:, t, :], logit[:, t, :])
                link(last)
                dve.tensor_scalar(stat[:, 24:26], top[:, :, 0], -1.0, None, ALU.mult).then_inc(lg_max, 1)
                for t in range(TT):
                    fourth = top[:, t, TOP_K - 1:TOP_K]
                    dve.tensor_scalar(above[:, t, :], logit[:, t, :], fourth, None, ALU.is_gt)
                    last = dve.tensor_scalar(equal[:, t, :], logit[:, t, :], fourth, None, ALU.is_equal)
                link(last)
                link(dve.tensor_reduce(stat[:, 26:28], above, AX.X, ALU.add))
                dve.tensor_scalar(stat[:, 26:28], stat[:, 26:28], -1.0, float(TOP_K), ALU.mult, ALU.add)
                for t in range(TT):
                    last = dve.tensor_tensor_scan(run[:, t, :], ones[:, 0:E], equal[:, t, :], 0.0, ALU.mult, ALU.add)
                link(last)
                for t in range(TT):
                    last = dve.scalar_tensor_tensor(mask[:, t, :], run[:, t, :], stat[:, 26 + t:27 + t], equal[:, t, :],
                                                    ALU.is_le, ALU.mult)
                link(last)
                dve.tensor_tensor(mask, mask, above, ALU.add).then_inc(mask_ready, 1)
                dve.wait_ge(mask_ready, 1)
                dve.wait_ge(lg_exp, 1)
                link(dve.tensor_tensor(prob, prob, mask, ALU.mult))
                link(dve.tensor_reduce(stat[:, 28:30], prob, AX.X, ALU.add))
                link(dve.reciprocal(stat[:, 28:30], stat[:, 28:30]))
                for t in range(TT):
                    last = dve.tensor_scalar(comb[:, t, 0:E], prob[:, t, :], stat[:, 28 + t:29 + t], None, ALU.mult)
                last.then_inc(comb_ready, 1)
                dve.wait_ge(rank_ready, 1)
                places = A[1][:, 0:TT * E].rearrange("p (t e) -> p t e", t=TT)
                link(dve.scalar_tensor_tensor(rank[:, :, 0:E], places, 1.0, mask, ALU.add, ALU.mult))
                link(dve.tensor_scalar(rank[:, :, 0:E], rank[:, :, 0:E], -1.0, None, ALU.add))
                link(dve.tensor_reduce(most[:, 0:1], A[1][:, TT * E:(TT + 1) * E], AX.X, ALU.max))
                dve.tensor_copy(most_i[:, :], most[:, 0:1]).then_inc(route_done, 1)

            for step, k in ORDER:
                if step == "vectors":
                    dve.wait_ge(small_in, 16 * N_SMALL)
                    dve.wait_ge(consts_done, CONSTS)
                    dve.wait_ge(vec_ready, 1)
                    link(dve.tensor_copy(vec[:, :], A[3][:, 0:NVEC]))
                    v = vec[:, VCOL["diff_gain"]:VCOL["diff_gain"] + 1]
                    dve.tensor_scalar(v, v, 1.0 - LAM_INIT, None, ALU.mult).then_inc(vec_cols, 1)
                    dve.wait_ge(vec_cols, 1)
                    for j in range(2):
                        last = dve.tensor_tensor_reduce(
                            out=lam_w[:, :], in0=lam_row[:, 2 * j * D_DH:(2 * j + 1) * D_DH],
                            in1=lam_row[:, (2 * j + 1) * D_DH:(2 * j + 2) * D_DH], scale=1.0, scalar=0.0,
                            op0=ALU.mult, op1=ALU.add, accum_out=lam_s[:, j:j + 1])
                        last.then_inc(lam_sum, 1)
                        dve.wait_ge(lam_sum, j + 1)
                    dve.wait_ge(lam_exp, 1)
                    link(dve.tensor_tensor(lam_s[:, 0:1], lam_s[:, 3:4], lam_s[:, 2:3], ALU.subtract))
                    dve.tensor_scalar(lam_s[:, 1:2], lam_s[:, 0:1], -LAM_INIT, None, ALU.add).then_inc(lam_set, 1)
                elif step == "normx":
                    normalise(step, k, RES, XN)
                elif step == "split":
                    split(k)
                elif step in HALVED:
                    lower_half(step)
                elif step in ("qm", "km"):
                    convolve(step)
                elif step == "gates":
                    dve.wait_ge(if_rows, 1)
                    dve.tensor_scalar(gate[:, 0, :], A[1][0:M_HEADS, 0:T], b_if_c[:, 0:1], None, ALU.add)
                    link(dve.tensor_scalar(gate[:, 1, :], A[1][0:M_HEADS, T:2 * T], b_if_c[:, 1:2], None, ALU.add))
                    dve.scalar_tensor_tensor(gate[:, 2, :], gate[:, 1, :], -1.0, gate[:, 1, :], ALU.mult,
                                             ALU.max).then_inc(f_abs, 1)
                    link(dve.tensor_scalar(gate[:, 3, :], gate[:, 1, :], 0.0, None, ALU.min))
                    dve.wait_ge(f_ln, 1)
                    link(dve.tensor_tensor(gate[:, 3, :], gate[:, 3, :], gate[:, 2, :], ALU.subtract))
                    link(dve.tensor_tensor_scan(gate[:, 4, :], ones[0:M_HEADS, :], gate[:, 3, :], 0.0, ALU.mult, ALU.add))
                    link(dve.tensor_tensor(gate[:, 0, :], gate[:, 0, :], gate[:, 4, :], ALU.subtract))
                    link(dve.tensor_tensor_scan(gate[:, 5, :], gate[:, 0, :], gate[:, 0, :], 0.0, ALU.max, ALU.max))
                    dve.tensor_tensor(gate[:, 6, :], gate[:, 4, :], gate[:, 5, :], ALU.add).then_inc(bm_ready, 1)
                elif step == "gates2":
                    pass
                elif step == "mls":
                    if k == 0:
                        dve.wait_ge(gate_cols, 1)
                    if k >= 2:
                        dve.wait_ge(ml_num, k - 1)
                    d = decay[:, k % 2, :]
                    dve.tensor_scalar(d[:, 0:T], m_all[:, k, :], a_em[:, 0, k:k + 1], 0.0, ALU.subtract, ALU.max)
                    dve.tensor_scalar(d[:, T:T + P], m_all[:, k, P:T], a_em[:, 1, k:k + 1], 0.0, ALU.subtract,
                                      ALU.max).then_inc(ml_gap, 1)
                    dve.wait_ge(ml_decay, k + 1)
                    for b in (0, 2):
                        last = dve.tensor_tensor(d[:, b * P:(b + 1) * P], d[:, b * P:(b + 1) * P], causal[:, :], ALU.mult)
                    link(last)
                    dve.wait_ge(ml_scores, k + 1)
                    dve.tensor_tensor(d, A[k % 2][:, 0:3 * P], d, ALU.mult).then_inc(ml_probs, 1)
                elif step == "mlo":
                    dve.wait_ge(ml_num, k + 1)
                    if k >= 2:
                        dve.wait_ge(ml_h, k - 1)
                    c = 24 + 2 * (k % 2)
                    den, em = A[k % 2][:, 3 * P:3 * P + TT], a_em[:, :, M_HEADS + k]
                    link(dve.tensor_tensor(stat[:, c:c + 2], den, em, ALU.max))
                    link(dve.scalar_tensor_tensor(stat[:, c:c + 2], den, -1.0, stat[:, c:c + 2], ALU.mult, ALU.max))
                    dve.reciprocal(stat[:, c:c + 2], stat[:, c:c + 2]).then_inc(ml_rden, 1)
                elif step == "mlnorm":
                    dve.wait_ge(ml_h, M_HEADS)
                    inverse_root(step, k, slice(32, 40), slice(32, 40), M_DV)
                    for j in range(2 * M_HEADS):
                        v = HM[:, j * M_DV:(j + 1) * M_DV]
                        last = dve.tensor_scalar(v, v, stat[:, 32 + j:33 + j], None, ALU.mult)
                    last.then_inc(hm_done, 1)
                elif step == "normmem":
                    normalise(step, k, MEMN, MEMN)
                elif step == "dfs":
                    dve.wait_ge(df_scores, k + 1)
                    if k >= 1:
                        dve.wait_ge(df_a, k)
                    for c in range(2):
                        dve.tensor_tensor_reduce(out=work[:, c, 0:P], in0=A[c][:, 0:P], in1=chunk_mask[:, 0, :], scale=1.0,
                                                 scalar=NEG, op0=ALU.add, op1=ALU.max, accum_out=stat[:, 40 + 2 * c:41 + 2 * c])
                        last = dve.tensor_tensor_reduce(
                            out=work[:, c, P:3 * P], in0=A[c][:, P:3 * P],
                            in1=chunk_mask[:, 1:3, :].rearrange("p b k -> p (b k)"), scale=1.0,
                            scalar=NEG, op0=ALU.add, op1=ALU.max, accum_out=stat[:, 41 + 2 * c:42 + 2 * c])
                    link(last)
                    dve.tensor_scalar(stat[:, 40:44], stat[:, 40:44], -(D_DH ** -0.5), None, ALU.mult).then_inc(df_max, 1)
                elif step == "dfa":
                    dve.wait_ge(df_exp, k + 1)
                    link(dve.reciprocal(stat[:, 44:48], stat[:, 44:48]))
                    link(dve.tensor_scalar(stat[:, 46:48], stat[:, 46:48], neg_lam[:, 0:1], None, ALU.mult))
                    if k >= 1:
                        dve.wait_ge(df_aT, k)
                    for t, cols in ((0, slice(0, P)), (1, slice(P, 3 * P))):
                        link(dve.tensor_scalar(work[:, 2, cols], work[:, 1, cols], stat[:, 46 + t:47 + t], None, ALU.mult))
                        last = dve.scalar_tensor_tensor(work[:, 3, cols], work[:, 0, cols], stat[:, 44 + t:45 + t],
                                                        work[:, 2, cols], ALU.mult, ALU.add)
                    last.then_inc(df_a, 1)
                elif step == "dfnorm":
                    dve.wait_ge(df_h, D_HEADS)
                    for t in range(TT):
                        link(dve.tensor_tensor(squares[:, t, :], nat(HD)[:, t, :], nat(HD)[:, t, :], ALU.mult))
                        link(dve.tensor_reduce(stat[:, 48 + 8 * t:56 + 8 * t], squares[:, t, :].rearrange("p (h d) -> p h d", d=P),
                                               AX.X, ALU.add))
                    inverse_root(step, k, slice(48, 64), slice(48, 64), P)
                    for j in range(TT * D_HEADS):
                        v = HD[:, j * P:(j + 1) * P]
                        last = dve.tensor_scalar(v, v, stat[:, 48 + j:49 + j], None, ALU.mult)
                    last.then_inc(hd_done, 1)
                elif step == "norm1":
                    normalise(step, k, RES, NRM)
                elif step == "xas":
                    dve.wait_ge(xa_scores, k + 1)
                    s = 40 + 4 * (k % 2)
                    link(dve.tensor_reduce(stat[:, s:s + 2], A[k % 2][:, :].rearrange("p (t m) -> p t m", t=TT), AX.X, ALU.max))
                    dve.tensor_scalar(stat[:, s:s + 2], stat[:, s:s + 2], -(X_DH ** -0.5), None, ALU.mult).then_inc(xa_max, 1)
                    dve.wait_ge(xa_exp, k + 1)
                    link(dve.reciprocal(stat[:, s + 2:s + 4], stat[:, s + 2:s + 4]))
                    for t in range(TT):
                        w = work[:, k % 2, t * X_DH:(t + 1) * X_DH]
                        last = dve.tensor_scalar(w, w, stat[:, s + 2 + t:s + 3 + t], None, ALU.mult)
                    last.then_inc(xa_p, 1)
                elif step == "xao":
                    dve.wait_ge(xa_hi, k + 1)
                    cols = slice(2 * k * T, (2 * k + 2) * T)
                    dve.tensor_tensor(OXT[1][:, cols], A[3][:, :], OXT[0][:, cols].bitcast(f32),
                                      ALU.subtract).then_inc(xa_h, 1)
                elif step == "norm2":
                    normalise(step, k, RES, H2, [k])
                elif step == "x2T":
                    gain = vec[:, VCOL["norm_ffn"]:VCOL["norm_ffn"] + KC]
                    for i in range(2):
                        n = TILE[step, k] + i
                        dve.wait_ge(tile_ready, n + 1)
                        dve.tensor_tensor(fm(X2T)[:, 4 * i:4 * i + 4, k * P:(k + 1) * P],
                                          bank[n % 4][:, :].rearrange("p (c t) -> p c t", t=P),
                                          gain[:, 4 * i:4 * i + 4].unsqueeze(2).to_broadcast([P, 4, P]),
                                          ALU.mult).then_inc(evac["dve"], 1)
                elif step == "route":
                    route()
                elif step in EVACUATES and EVACUATES[step] == "dve":
                    projection(step, k)

            def place_tokens(column):
                for t in range(TT):
                    last = dve.tensor_scalar(pick[:, t, :], slot_no[:, 0:CAP], rank[:, t, column], None, ALU.is_equal)
                last.then_inc(pick_ready, 1)

            def gathered(value):
                dve.wait_ge(xg_ready, value)
                gain = vec[:, VCOL["norm_ffn"]:VCOL["norm_ffn"] + KC]
                dve.tensor_tensor(xg[:, :, :], xbank[:, :].rearrange("p (k c) -> p k c", c=CAP),
                                  gain.unsqueeze(2).to_broadcast([P, KC, CAP]), ALU.mult).then_inc(xg_done, 1)

            def experts(before):
                made = before * (E + 1)
                if before:
                    dve.tensor_scalar(rank[:, :, :], rank[:, :, :], -float(CAP), None, ALU.add).then_inc(rank_moved, 1)
                    dve.wait_ge(rank_moved, before)
                    dve.wait_ge(xg_ready, made)
                place_tokens(slice(0, 1))
                gathered(made + 1)
                with dve.Fori(0, E) as e:
                    n = e + (before * E + 1)
                    for t in range(TT):
                        last = dve.tensor_scalar(pickw[:, t, :], slot_no[:, :], rank[:, t, bass.ds(e, 1)],
                                                 comb[:, t, bass.ds(e, 1)], ALU.is_equal, ALU.mult)
                    last.then_inc(pickw_ready, 1)
                    dve.wait_ge(xg_ready, e + (made + 1))
                    place_tokens(bass.ds(e + 1, 1))
                    dve.wait_ge(g_ready, n)
                    dve.tensor_scalar(G_, gbank[:, :], LIMIT, None, ALU.min).then_inc(g_clip, 1)
                    dve.wait_ge(u_ready, n)
                    dve.tensor_scalar(U_, ubank[:, :], LIMIT, -LIMIT, ALU.min, ALU.max)
                    dve.wait_ge(g_sig, n)
                    dve.tensor_tensor(S_, S_, G_, ALU.mult).then_inc(gs_done, 1)
                    dve.wait_ge(gs_done, n)
                    dve.scalar_tensor_tensor(A_, U_, 1.0, S_, ALU.add, ALU.mult).then_inc(a_ready, 1)
                    gathered(e + (made + 2))
                    dve.wait_ge(y_ready, n)
                    dve.tensor_copy(y_sb, tbank[:, :]).then_inc(y_done, 1)
                dve.wait_ge(added, (before + 1) * E)

            dve.wait_ge(route_done, 1)
            experts(0)
            n_most = dve.value_load(most_i[0:1, 0:1], min_val=0, max_val=T)
            for p in range(1, T // CAP):
                with dve.If(n_most > p * CAP):
                    experts(p)
            for t in range(TT):
                for h in range(2):
                    r = nat(RES)[:, t, h * HALF:(h + 1) * HALF]
                    last = dve.tensor_tensor(r, bank[2 * t + h][:, :], r, ALU.add)
            last.then_inc(fin_res, 1)
            dve.wait_ge(norm_sq, len(NORM_SQ) + 1)
            inverse_root("final", 0, slice(16, 18), slice(18, 20), D)
            for t in range(TT):
                r = nat(RES)[:, t, :]
                dve.scalar_tensor_tensor(r, r, stat[:, 18 + t:19 + t], fin_gain[:, :], ALU.mult, ALU.mult).then_inc(out_ready, 1)

        @block.tensor
        def _(pe):
            pe.wait_ge(consts_done, CONSTS)
            pe.wait_ge(small_in, 16 * N_SMALL)

            inputs = {"kx": (MEMT, "memT"), "vx": (MEMT, "memT"), "bm": (HMT, "hmT"), "bd": (HDT, "hdT"), "qx": (X1T, "x1T")}
            natural = {"xT": XN, "hmT": HM, "memT": MEMN, "hdT": HD, "x1T": NRM, "x2T": H2}
            norm_of = {"xT": "normx", "memT": "normmem", "x1T": "norm1", "x2T": "norm2"}

            def transpose_all(step, k):
                src = nat(natural[step])
                if step in norm_of:
                    pe.wait_ge(norm_done, NORM_SQ[norm_of[step], k] + 1)
                elif step == "hmT":
                    pe.wait_ge(hm_done, 1)
                else:
                    pe.wait_ge(hd_done, 1)
                for i in range(tiles_of(step)):
                    n = TILE[step, k] + i
                    wait_evacuated(pe, n - 4)
                    for q in range(4):
                        t, c = (k, 4 * i + q) if step == "x2T" else (q % 2, 2 * i + q // 2)
                        last = pe.transpose(bank[n % 4][:, q * P:(q + 1) * P], src[:, t, c * P:(c + 1) * P], ident[:, :])
                    last.then_inc(tile_ready, 1)

            def three_passes(out, still, moving):
                for kk in range(KC):
                    for a, b in ((0, 0), (0, 1), (1, 0)):
                        last = pe.matmul(out, still(a, kk), moving(b, kk), start=kk + a + b == 0,
                                         stop=kk == KC - 1 and a == 1)
                return last

            def projection(step, k):
                if step == "wo":
                    operand = OXT
                    pe.wait_ge(xa_h, X_HEADS)
                elif step == "out":
                    operand = MIX
                    pe.wait_ge(mix_done, 4)
                else:
                    operand, job = inputs.get(step, (XT, "xT"))
                    wait_job(pe, job)
                b = BLOCKS.index((step, k))
                if step == "wo":
                    b = NB - 1
                pe.wait_ge(split_made, b + 1)

                def weights(b, half, kk, cols):
                    return halves[:, b % 2, half, :].rearrange("p (k n) -> p k n", k=KC)[:, kk, cols]

                for i in range(2):
                    n = TILE[step, k] + i
                    wait_evacuated(pe, n - 4)
                    if step in TOKEN_MAJOR:
                        t, wb = (k, NB - 2 + i) if step == "wo" else (i, b)
                        last = three_passes(bank[n % 4][:, :], lambda a, kk: fm(operand[a])[:, kk, t * P:(t + 1) * P],
                                            lambda a, kk: weights(wb, a, kk, slice(0, BLK)))
                    else:
                        for j in range(2):
                            c = (2 * i + j) * P
                            last = three_passes(bank[n % 4][:, j * T:(j + 1) * T],
                                                lambda a, kk: weights(b, a, kk, slice(c, c + P)),
                                                lambda a, kk: fm(operand[a])[:, kk, :])
                    last.then_inc(tile_ready, 1)

            def one(out, lhsT, rhs):
                return pe.matmul(out, lhsT, rhs, start=True, stop=True)

            for step, k in ORDER:
                if step == "vectors":
                    pe.transpose(A[3][:, 0:NVEC], vec_rows[:, :], ident[0:NVEC, 0:NVEC]).then_inc(vec_ready, 1)
                    pe.wait_ge(lam_set, 1)
                    for h in range(2):
                        one(A[h][:, :], ones[0:1, 0:P], fin_row[0:1, h * HALF:(h + 1) * HALF])
                    one(A[2][:, 0:1], ones[0:1, 0:P], lam_s[0:1, 1:2]).then_inc(lam_bc, 1)
                elif step in TRANSPOSES:
                    transpose_all(step, k)
                elif step in EVACUATES:
                    projection(step, k)
                elif step == "gates":
                    wait_job(pe, "xT")
                    pe.wait_ge(vec_done, 1)
                    for t in range(TT):
                        for half in range(2):
                            for kk in range(KC):
                                last = pe.matmul(A[0][:, 2 * t * M_HEADS:2 * (t + 1) * M_HEADS],
                                                 fm(XT[half])[:, kk, t * P:(t + 1) * P].bitcast(f32), w_if[:, kk, :],
                                                 start=half + kk == 0, stop=half == 1 and kk == KC - 1)
                    last.then_inc(if_ready, 1)
                    pe.wait_ge(if_nat_ready, 1)
                    for g in range(2):
                        for t in range(TT):
                            c = (2 * t + g) * M_HEADS
                            last = pe.transpose(A[1][0:M_HEADS, g * T + t * P:g * T + (t + 1) * P],
                                                if_nat[:, c:c + M_HEADS], ident[:, :])
                    last.then_inc(if_rows, 1)
                elif step == "gates2":
                    pe.wait_ge(em_ready, 1)
                    for h in range(M_HEADS):
                        one(A[h // 2][:, (h % 2) * T:(h % 2 + 1) * T], head_row[:, h, :], gate[:, 5, :])
                    for t in range(TT):
                        for j, row in ((0, 0), (1, 6)):
                            c = (2 * t + j) * M_HEADS
                            last = pe.transpose(A[2][:, c:c + M_HEADS], gate[:, row, t * P:(t + 1) * P],
                                                ident[0:M_HEADS, 0:M_HEADS])
                    last.then_inc(gate_bc, 1)
                elif step == "mls":
                    wait_job(pe, "km")
                    if k == 0:
                        pe.wait_ge(gate_cols, 1)
                    if k >= 2:
                        pe.wait_ge(ml_rden, k - 1)
                    q, key = fm(QK)[:, k, :], fm(QK)[:, M_HEADS + k, :]
                    one(A[k % 2][:, 0:T], key[:, 0:P], q)
                    one(A[k % 2][:, T:T + P], key[:, P:T], q[:, P:T]).then_inc(ml_scores, 1)
                elif step == "mlo":
                    wait_job(pe, "vm", 1)
                    pe.wait_ge(ml_probs, k + 1)
                    if k >= 2:
                        pe.wait_ge(ml_h, k - 1)
                    w, num, den = decay[:, k % 2, :], A[2 + k % 2], A[k % 2]
                    v = [nat(VM)[:, t, k * M_DV:(k + 1) * M_DV] for t in range(TT)]
                    for rhs, dst in ((v, [num[:, t * M_DV:(t + 1) * M_DV] for t in range(TT)]),
                                     ([ones[:, 0:1]] * TT, [den[:, 3 * P + t:3 * P + t + 1] for t in range(TT)])):
                        one(dst[0], w[:, 0:P], rhs[0])
                        pe.matmul(dst[1], w[:, P:2 * P], rhs[0], start=True, stop=False)
                        last = pe.matmul(dst[1], w[:, 2 * P:3 * P], rhs[1], start=False, stop=True)
                    last.then_inc(ml_num, 1)
                elif step == "dfs":
                    wait_job(pe, "kd", 1)
                    wait_job(pe, "qd", 1)
                    if k >= 1:
                        pe.wait_ge(df_max, k)
                    for cols, qs, ks in ((slice(0, P), slice(0, P), slice(0, P)), (slice(P, 3 * P), slice(P, T), slice(0, T))):
                        for c in range(2):
                            rows = slice(c * D_DH, (c + 1) * D_DH)
                            last = one(A[c][:, cols], fm(QD)[rows, k, qs], fm(KD)[rows, k, ks])
                    last.then_inc(df_scores, 1)
                elif step == "dft":
                    pe.wait_ge(df_a, k + 1)
                    if k >= 1:
                        pe.wait_ge(df_aTs, k)
                    for b in range(3):
                        last = pe.transpose(A[2][:, b * P:(b + 1) * P], work[:, 3, b * P:(b + 1) * P], ident[:, :])
                    last.then_inc(df_aT, 1)
                elif step == "dfo":
                    wait_job(pe, "vd", k // 4)
                    pe.wait_ge(df_aTs, k + 1)
                    if k >= 2:
                        pe.wait_ge(df_h, k - 1)
                    o = A[3][:, (k % 2) * T:(k % 2 + 1) * T]
                    v = [nat(VD)[:, t, k * P:(k + 1) * P] for t in range(TT)]
                    one(o[:, 0:P], work_t[:, 0:P], v[0])
                    pe.matmul(o[:, P:T], work_t[:, P:2 * P], v[0], start=True, stop=False)
                    pe.matmul(o[:, P:T], work_t[:, 2 * P:3 * P], v[1], start=False, stop=True).then_inc(df_o, 1)
                elif step == "xas":
                    wait_job(pe, "qx", 1)
                    wait_job(pe, "kx", 1)
                    if k >= 2:
                        pe.wait_ge(xa_exp, k - 1)
                    for t in range(TT):
                        for j in range(2):
                            last = pe.matmul(A[k % 2][:, t * T:(t + 1) * T], fm(QX)[:, 2 * k + j, t * P:(t + 1) * P],
                                             fm(KX)[:, 2 * k + j, :], start=j == 0, stop=j == 1)
                    last.then_inc(xa_scores, 1)
                elif step == "xat":
                    pe.wait_ge(xa_p, k + 1)
                    if k >= 1:
                        pe.wait_ge(xa_pTs, k)
                    for m in range(TT):
                        for t in range(TT):
                            c = (2 * m + t) * P
                            last = pe.transpose(A[2][:, c:c + P], work[:, k % 2, t * X_DH + m * P:t * X_DH + (m + 1) * P],
                                                ident[:, :])
                    last.then_inc(xa_pT, 1)
                elif step == "xao":
                    wait_job(pe, "vx", 1)
                    pe.wait_ge(xa_pTs, k + 1)
                    if k >= 1:
                        pe.wait_ge(xa_h, k)
                    for j in range(2):
                        for m in range(TT):
                            c = k * X_DH + j * P
                            last = pe.matmul(A[3][:, j * T:(j + 1) * T], nat(VX)[:, m, c:c + P],
                                             work_t[:, m * T:(m + 1) * T], start=m == 0, stop=m == 1)
                    last.then_inc(xa_o, 1)
                elif step == "route":
                    wait_job(pe, "x2T", 1)
                    for t in range(TT):
                        for kk in range(KC):
                            pe.matmul(A[0][:, t * E:(t + 1) * E], fm(X2T)[:, kk, t * P:(t + 1) * P], w_r[:, kk, :],
                                      start=kk == 0, stop=False)
                        last = pe.matmul(A[0][:, t * E:(t + 1) * E], ones[0:1, 0:P], b_r[0:1, :], start=False, stop=True)
                    last.then_inc(lg_ready, 1)
                    pe.wait_ge(mask_ready, 1)
                    mask = lg[:, 4, :, :]
                    one(A[1][:, 0:E], strict[:, :], mask[:, 0, :])
                    for c, last_lhs in ((E, strict), (2 * E, ones)):
                        pe.matmul(A[1][:, c:c + E], ones[:, 0:P], mask[:, 0, :], start=True, stop=False)
                        last = pe.matmul(A[1][:, c:c + E], last_lhs[:, 0:P], mask[:, 1, :], start=False, stop=True)
                    last.then_inc(rank_ready, 1)
                    pe.wait_ge(comb_ready, 1)
                    for t in range(TT):
                        last = pe.transpose(A[2][0:E, t * P:(t + 1) * P], comb[:, t, 0:E], ident[:, :])
                    last.then_inc(combT_ready, 1)
                    pe.wait_ge(combT_done, 1)
                    pe.wait_ge(bias_in, 32)
                    for n in range(len(OWNER) - 4, len(OWNER)):
                        wait_evacuated(pe, n)
                    for t in range(TT):
                        for h in range(2):
                            pe.matmul(bank[2 * t + h][:, :], combT[:, t, :], bdn[:, h * HALF:(h + 1) * HALF],
                                      start=True, stop=False, skip_group_check=True)

            def gather():
                for kk in range(KC):
                    for t in range(TT):
                        last = pe.matmul(xbank[:, kk * CAP:(kk + 1) * CAP], nat(H2)[:, t, kk * P:(kk + 1) * P],
                                         pick[:, t, :], start=t == 0, stop=t == TT - 1)
                last.then_inc(xg_ready, 1)

            def experts(before):
                made = before * (E + 1)
                pe.wait_ge(pick_ready, made + 1)
                if before:
                    pe.wait_ge(xg_done, made)
                gather()
                with pe.Fori(0, E) as e:
                    n = e + (before * E + 1)
                    arrived = [(e + (before * E + 1 + (NB // 2 if j < 2 else 0))) * 16 for j in range(SLOTS)]
                    pe.wait_ge(xg_done, e + (made + 1))
                    for part, dst, ready in ((0, gbank, g_ready), (1, ubank, u_ready)):
                        for h in range(2):
                            j = 2 * part + h
                            pe.wait_ge(w_loaded[j], arrived[j])
                            for kk in range(4):
                                for half in range(2):
                                    last = pe.matmul(dst[half * CAP:(half + 1) * CAP, :], xg[:, 4 * h + kk, :],
                                                     ring[:, j, kk * D + half * HALF:kk * D + (half + 1) * HALF],
                                                     start=4 * h + kk == 0, stop=False)
                            last.then_inc(w_used[j], 1)
                        if part == 0:
                            pe.wait_ge(sel_ready, n)
                        for half in range(2):
                            c = part * D + half * HALF
                            last = pe.matmul(dst[half * CAP:(half + 1) * CAP, :], sel[:, :], bgu[:, c:c + HALF],
                                             start=False, stop=True)
                        last.then_inc(ready, 1)
                    pe.wait_ge(pick_ready, e + (made + 2))
                    gather()
                    pe.wait_ge(pickw_ready, n)
                    for t in range(TT):
                        last = pe.transpose(tbank[:, t * P:(t + 1) * P], pickw[:, t, :], ident[:, :])
                    last.then_inc(wT_ready, 1)
                    pe.wait_ge(wT_done, n)
                    pe.wait_ge(a_ready, n)
                    for c in range(4):
                        last = pe.transpose(tbank[:, c * P:(c + 1) * P], A_[:, c * P:(c + 1) * P], ident[:, :])
                    last.then_inc(aT_ready, 1)
                    pe.wait_ge(aT_done, n)
                    for h in range(2):
                        pe.wait_ge(w_loaded[4 + h], arrived[4 + h])
                        for c in range(4):
                            for half in range(2):
                                last = pe.matmul(tbank[half * CAP:(half + 1) * CAP, :],
                                                 work_t[:, c * P + h * CAP:c * P + (h + 1) * CAP],
                                                 ring[:, 4 + h, c * D + half * HALF:c * D + (half + 1) * HALF],
                                                 start=4 * h + c == 0, stop=4 * h + c == 7)
                        last.then_inc(w_used[4] if h == 0 else y_ready, 1)
                    pe.wait_ge(y_done, n)
                    for t in range(TT):
                        for h in range(2):
                            rows = slice(h * CAP, (h + 1) * CAP)
                            last = pe.matmul(bank[2 * t + h][:, :], wT[rows, t, :], y_sb[rows, :],
                                             start=False, stop=False, skip_group_check=True)
                    last.then_inc(added, 1)

            experts(0)
            n_most = pe.value_load(most_i[0:1, 0:1], min_val=0, max_val=T)
            for p in range(1, T // CAP):
                with pe.If(n_most > p * CAP):
                    experts(p)


_INS = ["x", "mem", "norm_mix", "w_in", "conv_w", "b_if", "mlstm_gain", "diff_lambda", "diff_gain", "w_branch_m",
        "w_branch_d", "b_gate", "w_out", "norm_xattn", "norm_mem", "wq_x", "wkv_x", "wo_x", "norm_ffn", "w_router",
        "b_router", "w_gu", "b_gu", "w_dn", "b_dn", "norm_final"]


def kernel(**inputs):
    import numpy as np
    import concourse.bacc as bacc
    from concourse.bass_utils import run_bass_kernel_spmd

    nc = bacc.Bacc("TRN2", target_bir_lowering=False, num_devices=1)
    arrays, args = {}, []
    for name in _INS:
        a = np.ascontiguousarray(inputs[name])
        arrays[f"in_{name}"] = a
        args.append(nc.dram_tensor(f"in_{name}", a.shape, mybir.dt.from_np(a.dtype), kind="ExternalInput").ap())
    args.append(nc.dram_tensor("out_0", (1, T, D), mybir.dt.float32, kind="ExternalOutput").ap())
    program(nc, *args)
    r = run_bass_kernel_spmd(nc, [arrays], core_ids=[0])
    return r.results[0]["out_0"]
```

```python
from contextlib import ExitStack

import concourse.bass as bass
from concourse import mybir

P = 128
D = 1024
T = 256
TT = T // P
KC = D // P
BLK = 512
SLOTS = 9
EXPERT_BLOCKS = 6
GROUP = 3
EPS = 1e-6
M_HEADS, M_DK, M_DV = 4, 128, 256
D_HEADS, D_DH = 8, 64
X_HEADS, X_DH = 4, 256
E, TOP_K = 32, 4
LEAD = E % GROUP
TURNS = GROUP * EXPERT_BLOCKS // SLOTS
CAP = 64
HALF = D // 2
F_ROW = 32
LIMIT, ALPHA = 7.0, 1.702
LAM_INIT = 0.8 - 0.6
CONV_W = 4
NEG = -1e30
IF_COL = 3072
COL = {"qm": 0, "km": 512, "vm": 1024, "om": 2048, "qd": 3080, "kd": 4104, "vd": 5128, "gm": 6152, "gd": 7176}

VECS = [("norm_mix", 8), ("norm_xattn", 8), ("norm_mem", 8), ("norm_ffn", 8), ("mlstm_gain", 8),
        ("diff_gain", 1), ("b_gate", 16), ("conv_w", 32)]
VCOL, NVEC = {}, 0
for _name, _n in VECS:
    VCOL[_name] = NVEC
    NVEC += _n

EVACUATES = {
    "xT": "dve", "qm": "dve", "km": "dve", "vm": "act", "om": "act", "qd": "act", "kd": "act", "vd": "act",
    "hmT": "dve", "memT": "dve", "kx": "act", "vx": "act", "gm": "act", "bm": "dve", "hdT": "dve",
    "gd": "act", "bd": "dve", "out": "dve", "x1T": "dve", "qx": "act", "wo": "dve", "x2T": "dve",
}
TRANSPOSES = ("xT", "hmT", "memT", "hdT", "x1T", "x2T")
TOKEN_MAJOR = ("vm", "vd", "vx", "out", "wo")


def numbered(steps):
    count, out = {}, []
    for step in steps.split():
        out.append((step, count.get(step, 0)))
        count[step] = out[-1][1] + 1
    return out


ORDER = numbered("""
    normx split split vectors xT split split qm split split lambda gates km gates2 split split vm
    mls split split vm mls split split om mlo mls mlo split split om mls mlo split split qd mlo
    split split qd mlnorm split split kd hmT split split kd dfs split split dfa vd dft dfs dfa dfo
    split split vd dft dfs split dfo split dfa gm dft dfs dfa dfo split split gm dft split dfs dfo
    dfa bm split dft dfs dfa dfo split split bm dft dfs dfa dfo normmem split split gd dft dfs dfa
    dfo split split gd dft memT split dfo dfnorm split kx hdT split split split kx split split bd
    split split bd split vx split split out split split out norm1 split split vx x1T split split
    split qx qx split xas xas xat split xas xao split xat xas xao xat xao xat xao wo norm2 wo x2T
    norm2 logits x2T logits route
""")


def tiles_of(step):
    return 4 if step in TRANSPOSES and step != "x2T" else 2


def nth(events):
    return {x: i for i, x in enumerate(x for x in ORDER if x[0] in events)}


NORM_SQ = nth(("normx", "normmem", "norm1", "norm2"))
NORM_VAR = nth(("normx", "normmem", "norm1", "norm2", "mlnorm", "dfnorm"))
NORM_VAR["final", 0] = len(NORM_VAR)
NORM_COL = {"normx": 0, "norm1": 2, "norm2": 4, "normmem": 6}


def plan():
    first, owner, blocks = {}, [], []
    count = {"act": 0, "dve": 0}
    for step, k in ORDER:
        if step not in EVACUATES:
            continue
        first[step, k] = len(owner)
        for _ in range(tiles_of(step)):
            count[EVACUATES[step]] += 1
            owner.append((EVACUATES[step], count[EVACUATES[step]]))
        if step not in TRANSPOSES:
            blocks.append((step, k))
    return first, owner, blocks


TILE, OWNER, BLOCKS = plan()
NB = len(BLOCKS)


def program(nc, x, mem, norm_mix, w_in, conv_w, b_if, mlstm_gain, diff_lambda, diff_gain, w_branch_m,
            w_branch_d, b_gate, w_out, norm_xattn, norm_mem, wq_x, wkv_x, wo_x, norm_ffn, w_router,
            b_router, w_gu, b_gu, w_dn, b_dn, norm_final, out):
    f32, f32r, i32 = mybir.dt.float32, mybir.dt.float32r, mybir.dt.int32
    ALU, ACT, AX = mybir.AluOpType, mybir.ActivationFunctionType, mybir.AxisListType
    assert NB % 2 == 0 and BLOCKS[-2:] == [("wo", 0), ("wo", 1)]

    ctx = ExitStack()
    with ctx:
        def sb(name, shape, dt=f32):
            return ctx.enter_context(nc.sbuf_tensor(name, shape, dt))

        def sem(name):
            return ctx.enter_context(nc.semaphore(name))

        base = (nc.sbuf_base + 31) // 32 * 32
        BLOCK_BYTES, MAT_BYTES = KC * BLK * 4, TT * D * 4
        MATS = (SLOTS - 3) * BLOCK_BYTES
        arena = sb("arena", [P, (MATS + 11 * MAT_BYTES) // 4])
        assert nc.sbuf_base == base + 4 * arena.shape[1]

        def at(name, shape, offset, dt=f32):
            return nc.alloc_sbuf_tensor_at(name, shape, dt, offset=base + offset)

        ring = at("ring", [P, SLOTS, KC * BLK], 0)
        halves = at("halves", [P, 2, 2, KC * BLK], 2 * BLOCK_BYTES, f32r)
        mat = [at(f"mat{i}", [P, TT * D], MATS + i * MAT_BYTES) for i in range(11)]

        def pair(i):
            return [at(f"{part}{i}", [P, TT * D], MATS + (i + j) * MAT_BYTES, f32r)
                    for j, part in enumerate(("hi", "lo"))]

        pair0, pair2, pair4 = pair(0), pair(2), pair(4)
        RES, QK, VM, HM, OM, QD, KD, VD, GM = (mat[i] for i in (7, 2, 3, 8, 6, 4, 5, 9, 10))
        XN, MEMN, HD, GD, KX, VX, NRM, QX = (mat[i] for i in (9, 2, 8, 6, 9, 6, 8, 10))
        XT, MEMT = pair0, pair0
        HMT, MIX, OXT = pair2, pair2, pair2
        HDT, X1T = pair4, pair4

        def nat(m):
            return m[:, :].rearrange("p (t d) -> p t d", t=TT)

        def fm(m):
            return m[:, :].rearrange("p (c t) -> p c t", t=T)

        ident = sb("ident", [P, P])
        ones = sb("ones", [P, T])
        strict = sb("strict", [P, P], f32r)
        ones_r = sb("ones_r", [P, P], f32r)
        chosen = sb("chosen", [P, TT, E], f32r)
        causal = sb("causal", [P, P])
        chunk_mask = sb("chunk_mask", [P, 3, P])
        slot_no = sb("slot_no", [P, 2 * CAP])
        head_row = QD[0:M_HEADS, 0:M_HEADS * P].rearrange("h (j p) -> h j p", p=P)
        vec_rows = QD[0:NVEC, M_HEADS * P:(M_HEADS + 1) * P]
        vec = sb("vec", [P, NVEC])
        w_if = sb("w_if", [P, KC * 2 * M_HEADS])
        w_if_halves = at("w_if_halves", [P, 2, KC, 2 * F_ROW], MATS + 10 * MAT_BYTES, f32r)
        w_if_used = w_if_halves[:, :, :, :].rearrange("p a k (g r) -> p a (k g) r", g=2)[:, :, :, 0:M_HEADS]
        b_if_c = sb("b_if_c", [M_HEADS, 2])
        lam_row = GM[:, D + 6 * P:D + 6 * P + 4 * D_DH]
        lam_s = sb("lam_s", [P, 4])
        neg_lam = sb("neg_lam", [P, 1])
        w_r = sb("w_r", [P, KC, E])
        b_r = sb("b_r", [1, E])
        fin_gain = sb("fin_gain", [P, D])
        head_squares = fin_gain[:, 0:T].rearrange("p (t d) -> p t d", t=TT)
        stat = sb("stat", [P, 64])
        gate = OM[0:M_HEADS, :].rearrange("h (j t) -> h j t", t=T)
        a_em = sb("a_em", [P, TT, 2 * M_HEADS])
        m_all = GM[:, 0:M_HEADS * T].rearrange("p (h t) -> p h t", t=T)
        decay = GM[:, D:D + 6 * P].rearrange("p (b n) -> p b n", b=2)
        work = sb("work", [P, 4, BLK])
        work_t = sb("work_t", [P, BLK])
        X2T = work[:, :, :].rearrange("p a n -> p (a n)")
        squares = work[:, :, :].rearrange("p (t a) n -> p t (a n)", t=TT)
        bgu = KX
        bdn = VX[0:E, 0:D]

        bank = [ctx.enter_context(nc.psum_tensor(f"bank{i}", [P, BLK], f32)) for i in range(8)]
        A = bank[4:8]

        consts_done = sem("consts_done")
        small_in = sem("small_in")
        x_in, mem_in = sem("x_in"), sem("mem_in")
        w_loaded = [sem(f"w_loaded{i}") for i in range(SLOTS)]
        w_used = sem("w_used")
        tile_ready = sem("tile_ready")
        hi_made, split_made, wo_split = sem("hi_made"), sem("split_made"), sem("wo_split")
        hi_part = sem("hi_part")
        if_rows = sem("if_rows")
        evac = {"act": sem("evac_act"), "dve": sem("evac_dve")}
        dve_step, act_step, pool_step = sem("dve_step"), sem("act_step"), sem("pool_step")
        norm_sq, norm_var, norm_std, norm_done = sem("norm_sq"), sem("norm_var"), sem("norm_std"), sem("norm_done")
        vec_cols = sem("vec_cols")
        hm_gated, mix_sum, mix_hi, mix_done = sem("hm_gated"), sem("mix_sum"), sem("mix_hi"), sem("mix_done")
        vec_ready, w_if_hi, w_if_split = sem("vec_ready"), sem("w_if_hi"), sem("w_if_split")
        lam_sum, lam_exp, fin_gain_in = sem("lam_sum"), sem("lam_exp"), sem("fin_gain_in")
        conv_out, conv_sig = sem("conv_out"), sem("conv_sig")
        f_abs, f_ln, bm_ready, em_ready = sem("f_abs"), sem("f_ln"), sem("bm_ready"), sem("em_ready")
        gate_bc, gate_cols = sem("gate_bc"), sem("gate_cols")
        ml_gap, ml_decay, ml_scores, ml_probs, ml_num, ml_rden, ml_h = (
            sem("ml_gap"), sem("ml_decay"), sem("ml_scores"), sem("ml_probs"), sem("ml_num"), sem("ml_rden"), sem("ml_h"))
        hm_done = sem("hm_done")
        df_scores, df_max, df_exp, df_a, df_aT, df_aTs, df_o, df_h, hd_done = (
            sem("df_scores"), sem("df_max"), sem("df_exp"), sem("df_a"), sem("df_aT"), sem("df_aTs"),
            sem("df_o"), sem("df_h"), sem("hd_done"))
        xa_scores, xa_max, xa_exp, xa_p, xa_pT, xa_pTs, xa_o, xa_hi, xa_h = (
            sem("xa_scores"), sem("xa_max"), sem("xa_exp"), sem("xa_p"), sem("xa_pT"), sem("xa_pTs"), sem("xa_o"),
            sem("xa_hi"), sem("xa_h"))
        lg_ready, lg_max, lg_exp, mask_ready, rank_ready, comb_ready, combT_ready, combT_done, route_done = (
            sem("lg_ready"), sem("lg_max"), sem("lg_exp"), sem("mask_ready"), sem("rank_ready"),
            sem("comb_ready"), sem("combT_ready"), sem("combT_done"), sem("route_done"))
        pick_ready, pickw_ready, xg_ready, xg_done, sel_ready = (
            sem("pick_ready"), sem("pickw_ready"), sem("xg_ready"), sem("xg_done"), sem("sel_ready"))
        g_ready, u_ready, g_clip, g_sig, gs_done, a_ready, aT_ready, aT_done, wT_ready, wT_done = (
            sem("g_ready"), sem("u_ready"), sem("g_clip"), sem("g_sig"), sem("gs_done"), sem("a_ready"),
            sem("aT_ready"), sem("aT_done"), sem("wT_ready"), sem("wT_done"))
        y_ready, y_done, added, rank_moved = sem("y_ready"), sem("y_done"), sem("added"), sem("rank_moved")
        out_ready, stored = sem("out_ready"), sem("stored")
        N_SMALL, CONSTS = 13, 12
        bias_in = sem("bias_in")

        H2 = NRM
        taken = [0]

        def part(*shape, rows=P):
            n = shape[0] * shape[1]
            taken[0] += n
            return QX[0:rows, taken[0] - n:taken[0]].rearrange("p (a b) -> p a b", b=shape[1])

        xg = part(KC, CAP)
        pick = part(TT, CAP)
        pickw = part(TT, 2 * CAP)
        wT = part(TT, P)
        combT = part(TT, P, rows=E)
        lg = part(8 * TT, E).rearrange("p (j t) e -> p j t e", t=TT)
        sel = sb("sel", [P, CAP])
        rank = sb("rank", [P, TT, E + 1])
        comb = sb("comb", [P, TT, E + 1])
        top = sb("top", [P, TT, 8])
        most = sb("most", [P, 2])
        most_i = sb("most_i", [P, 1], i32)
        G_, U_, S_, A_ = (work[:, j, :] for j in range(4))
        y_sb = VX[:, D:D + BLK]
        gbank, ubank, xbank, tbank = bank[4], bank[5], bank[6], bank[7]

        HALVED = {"xT": XT, "hmT": HMT, "memT": MEMT, "hdT": HDT, "x1T": X1T}
        HI_PART = [step for step, _ in ORDER if step in HALVED]
        GAIN = {"xT": "norm_mix", "memT": "norm_mem", "x1T": "norm_xattn"}

        def wait_evacuated(eng, n):
            if n >= 0:
                who, k = OWNER[n]
                eng.wait_ge(evac[who], k)

        def wait_job(eng, step, k=0):
            wait_evacuated(eng, TILE[step, k] + tiles_of(step) - 1)

        def wait_split(eng, n, h=1):
            if n >= NB - 2:
                eng.wait_ge(wo_split, 2 * (n - (NB - 2)) + h + 1)
            else:
                eng.wait_ge(split_made, 2 * n + h + 1)

        def block_done(eng, n):
            step, k = BLOCKS[n]
            eng.wait_ge(tile_ready, TILE["wo", 1] + k + 1 if step == "wo" else TILE[step, k] + 2)

        def slot_of(before, e, j):
            turns, slot = divmod((before * E + e) * EXPERT_BLOCKS + j, SLOTS)
            return slot, turns

        block = ctx.enter_context(nc.Block())

        @block.sync
        def _(sp):
            sources = {"kx": (wkv_x[0], 0), "vx": (wkv_x[0], D), "bm": (w_branch_m[0], 0), "bd": (w_branch_d[0], 0),
                       "out": (w_out[0], 0), "qx": (wq_x[0], 0), "wo": (wo_x[0], 0)}
            sp.dma_start(nat(RES), x[0].rearrange("(t p) d -> p t d", p=P)).then_inc(x_in, 16)
            def small_inputs():
                sp.dma_start(b_if_c[:, :], b_if[0].rearrange("(g h) -> h g", g=2),
                             allow_slow_non_contiguous=True).then_inc(small_in, 16)
                sp.dma_start(lam_row, diff_lambda.rearrange("l a d -> l (a d)")
                             .to_broadcast([P, 4 * D_DH])).then_inc(small_in, 16)
                sp.dma_start(w_r[:, :, :], w_router[0].rearrange("(k p) n -> p k n", p=P)).then_inc(small_in, 16)
                sp.dma_start(b_r[:, :], b_router).then_inc(small_in, 16)
            for n, (step, k) in enumerate(BLOCKS):
                w, c = sources[step] if step in sources else (w_in[0], COL[step])
                c += k * BLK
                if n == 1:
                    small_inputs()
                    sp.wait_ge(small_in, 16 * N_SMALL)
                if n >= 2:
                    wait_split(sp, n - 2)
                sp.dma_start(ring[:, n % 2, :].rearrange("p (k n) -> p k n", k=KC),
                             w[:, c:c + BLK].rearrange("(k p) n -> p k n", p=P)).then_inc(w_loaded[n % 2], 16)
                if (step, k) == ("gd", 1):
                    block_done(sp, BLOCKS.index(("bm", 1)))
                    sp.dma_start(nat(MEMN), mem[0].rearrange("(t p) d -> p t d", p=P)).then_inc(mem_in, 16)

            gu = w_gu[0].rearrange("e (h k p) n -> p e h k n", h=2, p=P)
            dn = w_dn[0].rearrange("e (h k p) n -> p e h k n", h=2, p=P)

            def load_block(e, slot, j):
                part, h = j // 2, j % 2
                src = (gu[:, bass.ds(e, 1), h, :, part * D:(part + 1) * D] if part < 2
                       else dn[:, bass.ds(e, 1), h, :, :])
                sp.dma_start(ring[:, slot, :].rearrange("p (k n) -> p k n", k=4),
                             src.rearrange("p e k n -> p (e k) n")).then_inc(w_loaded[slot], 16)

            def load_again(before, e, lead, j):
                done = e + before * E
                if j == 2:
                    sp.wait_ge(y_ready, done - 1)
                else:
                    sp.wait_ge(w_used, (done - 1) * (EXPERT_BLOCKS - 1) + (j - 1 if j < 2 else j - 2))
                load_block(e, slot_of(before, lead, j)[0], j)

            block_done(sp, BLOCKS.index(("vx", 1)))
            load_block(1, 6, 0)
            block_done(sp, BLOCKS.index(("qx", 1)))
            load_block(1, 8, 2)
            sp.wait_ge(df_h, D_HEADS)
            sp.dma_start(fin_gain[:, :],
                         norm_final.rearrange("(l d) -> l d", l=1).to_broadcast([P, D])).then_inc(fin_gain_in, 16)
            for j in range(EXPERT_BLOCKS):
                if j < 2:
                    wait_split(sp, NB - 2 + j)
                else:
                    block_done(sp, NB - 2 + (j - 2) // 2)
                load_block(0, j, j)
            load_block(1, 7, 1)

            def stream(before):
                for e in range(LEAD):
                    for j in range(EXPERT_BLOCKS):
                        if before or EXPERT_BLOCKS * e + j >= SLOTS:
                            load_again(before, e, e, j)
                with sp.Fori(0, (E - LEAD) // GROUP) as i:
                    for q in range(LEAD, LEAD + GROUP):
                        for j in range(EXPERT_BLOCKS):
                            load_again(before, i * GROUP + q, q, j)

            stream(0)
            sp.wait_ge(route_done, 1)
            n_most = sp.value_load(most_i[0:1, 0:1], min_val=0, max_val=T)
            for p in range(1, T // CAP):
                with sp.If(n_most > p * CAP):
                    stream(p)
            for t in range(TT):
                sp.wait_ge(out_ready, t + 1)
                sp.dma_start(out[0, t * P:(t + 1) * P, :], nat(RES)[:, t, :]).then_inc(stored, 16)
            sp.wait_ge(stored, 16 * TT)

        @block.gpsimd
        def _(pool):
            steps = [0]

            def after(ins):
                steps[0] += 1
                ins.then_inc(pool_step, 1)
                pool.wait_ge(pool_step, steps[0])

            pool.memset(ones[:, :], 1.0).then_inc(consts_done, 1)
            pool.wait_ge(consts_done, 1)
            after(pool.memset(ident[:, :], 0.0))
            pool.affine_select(out=ident[:, :], in_=ident[:, :], compare_op=ALU.not_equal, fill=1.0, base=0,
                               pattern=[[-1, P]], channel_multiplier=1).then_inc(consts_done, 1)
            pool.memset(w_if_halves[:, :, :, :].bitcast(f32), 0.0).then_inc(consts_done, 1)
            pool.tensor_copy(ones_r[:, :], ones[:, 0:P]).then_inc(consts_done, 1)
            pool.affine_select(out=strict[:, :], in_=ones[:, 0:P], compare_op=ALU.is_gt, fill=0.0, base=0,
                               pattern=[[1, P]], channel_multiplier=-1).then_inc(consts_done, 1)
            after(pool.memset(causal[:, :], 1.0))
            pool.affine_select(out=causal[:, :], in_=causal[:, :], compare_op=ALU.is_ge, fill=0.0, base=0,
                               pattern=[[1, P]], channel_multiplier=-1).then_inc(consts_done, 1)
            after(pool.memset(chunk_mask[:, :, :], 0.0))
            for b in (0, 2):
                pool.memset(chunk_mask[0:64, b, 64:P], NEG).then_inc(consts_done, 1)
            pool.iota(slot_no[:, :], pattern=[[0, 2], [1, CAP]], base=0, channel_multiplier=0,
                      allow_small_or_imprecise_dtypes=True).then_inc(consts_done, 1)
            after(pool.memset(head_row[:, :, :], 0.0))
            pool.affine_select(out=head_row[:, :, :], in_=head_row[:, :, :], compare_op=ALU.not_equal, fill=1.0,
                               base=0, pattern=[[-1, M_HEADS], [0, P]], channel_multiplier=1).then_inc(consts_done, 1)
            pool.memset(rank[:, :, E:E + 1], -1.0).then_inc(consts_done, 1)
            pool.memset(comb[:, :, E:E + 1], 0.0).then_inc(consts_done, 1)

            def selectors(before, first):
                with pool.Fori(first, E) as e:
                    pool.wait_ge(u_ready, e + before * E)
                    pool.tensor_copy(sel[:, :], ident[:, bass.ds(e, 1)].to_broadcast([P, CAP])).then_inc(sel_ready, 1)

            pool.wait_ge(consts_done, CONSTS)
            for n in range(NB - 2, NB):
                for h in range(2):
                    pool.wait_ge(hi_made, 2 * n + h + 1)
                    cols = slice(h * KC * BLK // 2, (h + 1) * KC * BLK // 2)
                    hi, lo = (halves[:, n % 2, a, cols] for a in range(2))
                    pool.tensor_tensor(lo, ring[:, n % 2, cols], hi.bitcast(f32), ALU.subtract).then_inc(wo_split, 1)
            pool.wait_ge(xa_scores, X_HEADS)
            after(pool.memset(bgu[:, :], 0.0))
            pool.dma_start(bgu[0:E, :], b_gu[0]).then_inc(bias_in, 16)
            pool.wait_ge(xa_o, X_HEADS)
            pool.dma_start(bdn, b_dn[0]).then_inc(bias_in, 16)
            pool.tensor_copy(sel[:, :], ident[:, 0:1].to_broadcast([P, CAP])).then_inc(sel_ready, 1)
            selectors(0, 1)
            pool.wait_ge(route_done, 1)
            n_most = pool.value_load(most_i[0:1, 0:1], min_val=0, max_val=T)
            for p in range(1, T // CAP):
                with pool.If(n_most > p * CAP):
                    selectors(p, 0)

        @block.scalar
        def _(act):
            n_step = [0]

            def link(ins):
                n_step[0] += 1
                ins.then_inc(act_step, 1)
                act.wait_ge(act_step, n_step[0])

            def small(dst, src):
                act.dma_start(dst, src).then_inc(small_in, 16)

            act.wait_ge(consts_done, 1)
            act.activation(stat[:, 63:64], ones[:, 0:1], ACT.Sqrt)

            rows = {"norm_mix": norm_mix, "norm_xattn": norm_xattn, "norm_mem": norm_mem, "norm_ffn": norm_ffn,
                    "diff_gain": diff_gain, "b_gate": b_gate}
            for name, n in VECS:
                if name in rows:
                    src = rows[name].rearrange("l (r p) -> (l r) p", p=P)
                elif name == "mlstm_gain":
                    src = mlstm_gain[0].rearrange("h (r p) -> (h r) p", p=P)
                else:
                    src = conv_w[0].rearrange("j (r p) -> (j r) p", p=P)
                small(vec_rows[VCOL[name]:VCOL[name] + n, :], src)
            small(w_if[:, :].rearrange("p (k n) -> p k n", k=KC),
                  w_in[0][:, IF_COL:IF_COL + 2 * M_HEADS].rearrange("(k p) n -> p k n", p=P))
            def root_mean_square(step, k, src, tiles=range(TT), junk=squares):
                c = NORM_COL[step]
                for t in tiles:
                    last = act.activation(junk[:, t, :], nat(src)[:, t, :], ACT.Square, accum_out=stat[:, c + t:c + t + 1])
                last.then_inc(norm_sq, 1)
                root(step, k, slice(8 + c + tiles[0], 9 + c + tiles[-1]))

            def root(step, k, cols):
                act.wait_ge(norm_var, NORM_VAR[step, k] + 1)
                act.activation(stat[:, cols], stat[:, cols], ACT.Sqrt).then_inc(norm_std, 1)

            def copy_tile(n, dst, func=ACT.Copy, **kw):
                act.wait_ge(tile_ready, n + 1)
                return act.activation(dst, bank[n % 4][:, :], func, **kw)

            def split(n, h):
                if h == 0:
                    act.wait_ge(w_loaded[n % 2], 16 * (n // 2 + 1))
                    if n >= 2:
                        block_done(act, n - 2)
                cols = slice(h * KC * BLK // 2, (h + 1) * KC * BLK // 2)
                act.activation(halves[:, n % 2, 0, cols], ring[:, n % 2, cols], ACT.Copy).then_inc(hi_made, 1)

            def conv_sigmoid(step):
                for c in range(4):
                    i = c + (4 if step == "km" else 0)
                    act.wait_ge(conv_out, i + 1)
                    act.activation(work[:, i % 4, T:2 * T], work[:, i % 4, 0:T], ACT.Sigmoid).then_inc(conv_sig, 1)

            def projection(step, k):
                for i in range(2):
                    n = TILE[step, k] + i
                    if step in ("om", "qd", "kd", "kx", "qx"):
                        m = {"om": OM, "qd": QD, "kd": KD, "kx": KX, "qx": QX}[step]
                        dst = m[:, (4 * k + 2 * i) * T:(4 * k + 2 * i + 2) * T]
                    elif step in ("vm", "vd", "vx"):
                        m = {"vm": VM, "vd": VD, "vx": VX}[step]
                        dst = nat(m)[:, i, k * BLK:(k + 1) * BLK]
                    if step == "vx":
                        wait_job(act, "bd", 1)
                    if step == "qx":
                        act.wait_ge(mix_done, 4)
                    if step in ("gm", "gd"):
                        act.wait_ge(tile_ready, n + 1)
                        g = GM if step == "gm" else GD
                        for j in range(2):
                            c = 4 * k + 2 * i + j
                            v = VCOL["b_gate"] + c + (KC if step == "gd" else 0)
                            last = act.activation(g[:, c * T:(c + 1) * T], bank[n % 4][:, j * T:(j + 1) * T],
                                                  ACT.Sigmoid, bias=vec[:, v:v + 1])
                        last.then_inc(evac["act"], 1)
                    elif step == "om":
                        copy_tile(n, dst, ACT.Sigmoid).then_inc(evac["act"], 1)
                    else:
                        copy_tile(n, dst).then_inc(evac["act"], 1)

            def upper_half(step):
                for i in range(4):
                    n = TILE[step, 0] + i
                    act.wait_ge(tile_ready, n + 1)
                    if step == "hmT":
                        wait_job(act, "om", 1)
                    for j in range(2):
                        c = 2 * i + j
                        src, dst = bank[n % 4][:, j * T:(j + 1) * T], fm(HALVED[step][0])[:, c, :]
                        if step == "hmT":
                            act.wait_ge(hm_gated, c + 1)
                            last = act.activation(dst, fm(OM)[:, c, :], ACT.Copy)
                        else:
                            v = VCOL["diff_gain"] if step == "hdT" else VCOL[GAIN[step]] + c
                            last = act.activation(dst, src, ACT.Copy, scale=vec[:, v:v + 1])
                    last.then_inc(hi_part, 1)

            for step, k in ORDER:
                if step == "vectors":
                    act.wait_ge(vec_cols, 1)
                    act.activation(w_if_used[:, 0], w_if[:, :].rearrange("p (c n) -> p c n", n=M_HEADS),
                                   ACT.Copy).then_inc(w_if_hi, 1)
                elif step == "lambda":
                    act.wait_ge(lam_sum, 2)
                    act.activation(lam_s[:, 2:4], lam_s[:, 0:2], ACT.Exp).then_inc(lam_exp, 1)
                elif step == "normx":
                    act.wait_ge(x_in, 16)
                    root_mean_square(step, k, RES)
                elif step == "split":
                    split(*divmod(k, 2))
                elif step == "normmem":
                    act.wait_ge(mem_in, 16)
                    root_mean_square(step, k, MEMN, junk=nat(mat[3]))
                elif step == "norm1":
                    wait_job(act, "out", 1)
                    root_mean_square(step, k, RES)
                elif step == "norm2":
                    wait_job(act, "wo", k)
                    root_mean_square(step, k, RES, [k], junk=nat(QX))
                elif step in ("qm", "km"):
                    conv_sigmoid(step)
                elif step == "gates":
                    act.wait_ge(f_abs, 1)
                    link(act.activation(gate[:, 2, :], gate[:, 2, :], ACT.Exp, scale=-1.0))
                    act.activation(gate[:, 2, :], gate[:, 2, :], ACT.Ln, bias=1.0).then_inc(f_ln, 1)
                    act.wait_ge(bm_ready, 1)
                    act.activation(gate[:, 6, :], gate[:, 6, :], ACT.Exp, scale=-1.0).then_inc(em_ready, 1)
                elif step == "gates2":
                    act.wait_ge(gate_bc, 1)
                    for b in range(2):
                        act.activation(m_all[:, 2 * b:2 * b + 2, :].rearrange("p h t -> p (h t)"), A[b][:, :], ACT.Copy)
                    act.activation(a_em[:, :, :].rearrange("p t c -> p (t c)"), A[2][:, 0:4 * M_HEADS],
                                   ACT.Copy).then_inc(gate_cols, 1)
                elif step == "mls":
                    act.wait_ge(ml_gap, k + 1)
                    act.activation(decay[:, k % 2, :], decay[:, k % 2, :], ACT.Exp, scale=-1.0).then_inc(ml_decay, 1)
                elif step == "mlo":
                    act.wait_ge(ml_rden, k + 1)
                    for t in range(TT):
                        link(act.activation(nat(HM)[:, t, k * M_DV:(k + 1) * M_DV],
                                            A[2 + k % 2][:, t * M_DV:(t + 1) * M_DV], ACT.Copy,
                                            scale=stat[:, 24 + 2 * (k % 2) + t:25 + 2 * (k % 2) + t]))
                        last = act.activation(squares[:, t, 0:M_DV], nat(HM)[:, t, k * M_DV:(k + 1) * M_DV], ACT.Square,
                                              accum_out=stat[:, 32 + 4 * t + k:33 + 4 * t + k])
                    last.then_inc(ml_h, 1)
                elif step == "mlnorm":
                    root(step, k, slice(32, 40))
                elif step == "dfs":
                    act.wait_ge(df_max, k + 1)
                    if k >= 1:
                        act.wait_ge(df_a, k)
                    for c in range(2):
                        for t, cols in ((0, slice(0, P)), (1, slice(P, 3 * P))):
                            i = 40 + 2 * c + t
                            last = act.activation(work[:, c, cols], work[:, c, cols], ACT.Exp, scale=D_DH ** -0.5,
                                                  bias=stat[:, i:i + 1], accum_out=stat[:, i + 4:i + 5])
                    last.then_inc(df_exp, 1)
                elif step == "dft":
                    act.wait_ge(df_aT, k + 1)
                    act.activation(work_t[:, 0:3 * P], A[2][:, 0:3 * P], ACT.Copy).then_inc(df_aTs, 1)
                elif step == "dfo":
                    act.wait_ge(df_o, k + 1)
                    act.activation(nat(HD)[:, :, k * P:(k + 1) * P],
                                   A[3][:, (k % 2) * T:(k % 2 + 1) * T].rearrange("p (t d) -> p t d", t=TT), ACT.Copy)
                    for t in range(TT):
                        last = act.activation(head_squares[:, t, :], A[3][:, (k % 2) * T + t * P:(k % 2) * T + (t + 1) * P],
                                              ACT.Square, accum_out=stat[:, 48 + D_HEADS * t + k:49 + D_HEADS * t + k])
                    last.then_inc(df_h, 1)
                elif step == "dfnorm":
                    root(step, k, slice(48, 64))
                elif step == "xas":
                    act.wait_ge(xa_max, k + 1)
                    if k >= 2:
                        act.wait_ge(xa_pT, k - 1)
                    s = 40 + 4 * (k % 2)
                    for t in range(TT):
                        last = act.activation(work[:, k % 2, t * X_DH:(t + 1) * X_DH], A[k % 2][:, t * X_DH:(t + 1) * X_DH],
                                              ACT.Exp, scale=X_DH ** -0.5, bias=stat[:, s + t:s + t + 1],
                                              accum_out=stat[:, s + 2 + t:s + 3 + t])
                    last.then_inc(xa_exp, 1)
                elif step == "xat":
                    act.wait_ge(xa_pT, k + 1)
                    act.activation(work_t[:, :], A[2][:, :], ACT.Copy).then_inc(xa_pTs, 1)
                elif step == "xao":
                    act.wait_ge(xa_o, k + 1)
                    act.activation(OXT[0][:, 2 * k * T:(2 * k + 2) * T], A[3][:, :], ACT.Copy).then_inc(xa_hi, 1)
                elif step == "route":
                    act.wait_ge(lg_max, 1)
                    for t in range(TT):
                        last = act.activation(lg[:, 1, t, :], lg[:, 0, t, :], ACT.Exp, bias=stat[:, 24 + t:25 + t])
                    last.then_inc(lg_exp, 1)
                    act.wait_ge(combT_ready, 1)
                    act.activation(combT[:, :, :].rearrange("e t p -> e (t p)"), A[3][0:E, 0:T], ACT.Copy).then_inc(combT_done, 1)
                elif step in HALVED:
                    upper_half(step)
                elif step == "bd":
                    for i in range(2):
                        act.wait_ge(mix_sum, 2 * k + i + 1)
                        cols = slice((4 * k + 2 * i) * T, (4 * k + 2 * i + 2) * T)
                        act.activation(MIX[0][:, cols], GM[:, cols], ACT.Copy).then_inc(mix_hi, 1)
                elif step in EVACUATES and EVACUATES[step] == "act":
                    projection(step, k)

            def experts(before):
                with act.Fori(0, E) as e:
                    n = e + (before * E + 1)
                    act.wait_ge(g_clip, n)
                    act.activation(S_, G_, ACT.Sigmoid, scale=ALPHA).then_inc(g_sig, 1)
                    act.wait_ge(wT_ready, n)
                    act.activation(wT[:, :, :].rearrange("p t c -> p (t c)"), tbank[:, 0:T], ACT.Copy).then_inc(wT_done, 1)
                    act.wait_ge(aT_ready, n)
                    act.activation(work_t[:, :], tbank[:, :], ACT.Copy).then_inc(aT_done, 1)
                act.activation(stat[:, 30:31], stat[:, 8:9], ACT.Sqrt)
                act.wait_ge(added, (before + 1) * E)

            experts(0)
            act.wait_ge(route_done, 1)
            n_most = act.value_load(most_i[0:1, 0:1], min_val=0, max_val=T)
            for p in range(1, T // CAP):
                with act.If(n_most > p * CAP):
                    experts(p)
            for b in range(3):
                last = act.activation(work[:, b, :], bank[b][:, :], ACT.Square, accum_out=stat[:, 16 + b:17 + b])
            last.then_inc(norm_sq, 1)
            act.wait_ge(norm_var, NORM_VAR["final", 0] + 1)
            act.activation(stat[:, 20:22], stat[:, 20:22], ACT.Sqrt).then_inc(norm_std, 1)

        @block.vector
        def _(dve):
            n_step = [0]

            def link(ins):
                n_step[0] += 1
                ins.then_inc(dve_step, 1)
                dve.wait_ge(dve_step, n_step[0])

            def inverse_root(step, k, sums, cols, n):
                dve.tensor_scalar(stat[:, cols], stat[:, sums], 1.0 / n, EPS, ALU.mult, ALU.add).then_inc(norm_var, 1)
                dve.wait_ge(norm_std, NORM_VAR[step, k] + 1)
                link(dve.reciprocal(stat[:, cols], stat[:, cols]))

            def normalise(step, k, src, dst, tiles=range(TT)):
                dve.wait_ge(norm_sq, NORM_SQ[step, k] + 1)
                c = NORM_COL[step]
                a, b = tiles[0], tiles[-1] + 1
                inverse_root(step, k, slice(c + a, c + b), slice(8 + c + a, 8 + c + b), D)
                for t in tiles:
                    last = dve.tensor_scalar(nat(dst)[:, t, :], nat(src)[:, t, :], stat[:, 8 + c + t:9 + c + t], None, ALU.mult)
                last.then_inc(norm_done, 1)

            def split(n, h):
                dve.wait_ge(hi_made, 2 * n + h + 1)
                cols = slice(h * KC * BLK // 2, (h + 1) * KC * BLK // 2)
                dve.tensor_tensor(halves[:, n % 2, 1, cols], ring[:, n % 2, cols],
                                  halves[:, n % 2, 0, cols].bitcast(f32), ALU.subtract).then_inc(split_made, 1)

            def lower_half(step):
                first = HI_PART.index(step) * 4
                hi, lo = HALVED[step]
                for i in range(4):
                    n = TILE[step, 0] + i
                    dve.wait_ge(tile_ready, n + 1)
                    chunks = [(2 * i + j, bank[n % 4][:, j * T:(j + 1) * T]) for j in range(2)]
                    if step == "hmT":
                        for c, src in chunks:
                            v = VCOL["mlstm_gain"] + c
                            dve.scalar_tensor_tensor(fm(OM)[:, c, :], src, vec[:, v:v + 1], fm(OM)[:, c, :], ALU.mult,
                                                     ALU.mult).then_inc(hm_gated, 1)
                    dve.wait_ge(hi_part, first + i + 1)
                    for c, src in chunks:
                        upper, lower = fm(hi)[:, c, :].bitcast(f32), fm(lo)[:, c, :]
                        if step == "hmT":
                            last = dve.tensor_tensor(lower, fm(OM)[:, c, :], upper, ALU.subtract)
                        else:
                            v = VCOL["diff_gain"] if step == "hdT" else VCOL[GAIN[step]] + c
                            last = dve.scalar_tensor_tensor(lower, src, vec[:, v:v + 1], upper, ALU.mult, ALU.subtract)
                    last.then_inc(evac["dve"], 1)

            def convolve(step):
                first = 4 if step == "km" else 0

                def finish(c):
                    chunk = first + c
                    dve.wait_ge(conv_sig, chunk + 1)
                    ins = dve.scalar_tensor_tensor(fm(QK)[:, chunk, :], work[:, chunk % 4, 0:T],
                                                   M_DK ** -0.5 if step == "qm" else 1.0,
                                                   work[:, chunk % 4, T:2 * T], ALU.mult, ALU.mult)
                    if c % 2:
                        ins.then_inc(evac["dve"], 1)

                for c in range(4):
                    chunk = first + c
                    n = TILE[step, 0] + c // 2
                    dve.wait_ge(tile_ready, n + 1)
                    src = bank[n % 4][:, (c % 2) * T:(c % 2 + 1) * T]
                    y = work[:, chunk % 4, 0:T]
                    tap = [vec[:, VCOL["conv_w"] + 8 * j + chunk:VCOL["conv_w"] + 8 * j + chunk + 1] for j in range(CONV_W)]
                    link(dve.tensor_scalar(y, src, tap[3], None, ALU.mult))
                    for back in (1, 2, 3):
                        ins = dve.scalar_tensor_tensor(y[:, back:T], src[:, 0:T - back], tap[3 - back], y[:, back:T],
                                                       ALU.mult, ALU.add)
                        if back < 3:
                            link(ins)
                        else:
                            ins.then_inc(conv_out, 1)
                    if c:
                        finish(c - 1)
                finish(3)

            def projection(step, k):
                for i in range(2):
                    n = TILE[step, k] + i
                    dve.wait_ge(tile_ready, n + 1)
                    src = bank[n % 4][:, :]
                    cols = slice((4 * k + 2 * i) * T, (4 * k + 2 * i + 2) * T)
                    if step == "bm":
                        wait_job(dve, "gm", 1)
                        ins = dve.tensor_tensor(GM[:, cols], src, GM[:, cols], ALU.mult)
                    elif step == "bd":
                        wait_job(dve, "gd", 1)
                        dve.tensor_tensor(GD[:, cols], src, GD[:, cols], ALU.mult).then_inc(evac["dve"], 1)
                        wait_evacuated(dve, n)
                        dve.tensor_tensor(GM[:, cols], GD[:, cols], GM[:, cols], ALU.add).then_inc(mix_sum, 1)
                        dve.wait_ge(mix_hi, 2 * k + i + 1)
                        dve.tensor_tensor(MIX[1][:, cols], GM[:, cols], MIX[0][:, cols].bitcast(f32),
                                          ALU.subtract).then_inc(mix_done, 1)
                        continue
                    elif step == "wo":
                        r = nat(RES)[:, k, i * BLK:(i + 1) * BLK]
                        ins = dve.tensor_tensor(r, src, r, ALU.add)
                    else:
                        r = nat(RES)[:, i, k * BLK:(k + 1) * BLK]
                        ins = dve.tensor_tensor(r, src, r, ALU.add)
                    ins.then_inc(evac["dve"], 1)

            def place_tokens(column):
                for t in range(TT):
                    last = dve.tensor_scalar(pick[:, t, :], slot_no[:, 0:CAP], rank[:, t, column], None, ALU.is_equal)
                last.then_inc(pick_ready, 1)

            def route():
                logit, prob, above, equal, mask, run = (lg[:, j, :, :] for j in range(6))
                picked = chosen[:, :, :].bitcast(f32)
                dve.wait_ge(lg_ready, TT)
                link(dve.tensor_copy(logit, A[0][:, 0:TT * E].rearrange("p (t e) -> p t e", t=TT)))
                for t in range(TT):
                    last = dve.max(top[:, t, :], logit[:, t, :])
                link(last)
                dve.tensor_scalar(stat[:, 24:26], top[:, :, 0], -1.0, None, ALU.mult).then_inc(lg_max, 1)
                for t in range(TT):
                    fourth = top[:, t, TOP_K - 1:TOP_K]
                    dve.tensor_scalar(above[:, t, :], logit[:, t, :], fourth, None, ALU.is_gt)
                    last = dve.tensor_scalar(equal[:, t, :], logit[:, t, :], fourth, None, ALU.is_equal)
                link(last)
                link(dve.tensor_reduce(stat[:, 26:28], above, AX.X, ALU.add))
                dve.tensor_scalar(stat[:, 26:28], stat[:, 26:28], -1.0, float(TOP_K), ALU.mult, ALU.add)
                for t in range(TT):
                    last = dve.tensor_tensor_scan(run[:, t, :], ones[:, 0:E], equal[:, t, :], 0.0, ALU.mult, ALU.add)
                link(last)
                for t in range(TT):
                    last = dve.scalar_tensor_tensor(mask[:, t, :], run[:, t, :], stat[:, 26 + t:27 + t], equal[:, t, :],
                                                    ALU.is_le, ALU.mult)
                link(last)
                dve.tensor_tensor(chosen[:, :, :], mask, above, ALU.add).then_inc(mask_ready, 1)
                dve.wait_ge(mask_ready, 1)
                dve.wait_ge(lg_exp, 1)
                link(dve.tensor_tensor(prob, prob, picked, ALU.mult))
                link(dve.tensor_reduce(stat[:, 28:30], prob, AX.X, ALU.add))
                link(dve.reciprocal(stat[:, 28:30], stat[:, 28:30]))
                for t in range(TT):
                    last = dve.tensor_scalar(comb[:, t, 0:E], prob[:, t, :], stat[:, 28 + t:29 + t], None, ALU.mult)
                last.then_inc(comb_ready, 1)
                dve.wait_ge(rank_ready, 1)
                places = A[1][:, 0:TT * E].rearrange("p (t e) -> p t e", t=TT)
                link(dve.scalar_tensor_tensor(rank[:, :, 0:E], places, 1.0, picked, ALU.add, ALU.mult))
                link(dve.tensor_scalar(rank[:, :, 0:E], rank[:, :, 0:E], -1.0, None, ALU.add))
                place_tokens(slice(0, 1))
                link(dve.tensor_reduce(most[:, 0:1], A[1][:, TT * E:(TT + 1) * E], AX.X, ALU.max))
                dve.tensor_copy(most_i[:, :], most[:, 0:1]).then_inc(route_done, 1)

            for step, k in ORDER:
                if step == "vectors":
                    dve.wait_ge(small_in, 16 * N_SMALL)
                    dve.wait_ge(consts_done, CONSTS)
                    dve.wait_ge(vec_ready, 1)
                    link(dve.tensor_copy(vec[:, :], A[3][:, 0:NVEC]))
                    v = vec[:, VCOL["diff_gain"]:VCOL["diff_gain"] + 1]
                    dve.tensor_scalar(v, v, 1.0 - LAM_INIT, None, ALU.mult).then_inc(vec_cols, 1)
                    dve.wait_ge(w_if_hi, 1)
                    dve.tensor_tensor(w_if_used[:, 1], w_if[:, :].rearrange("p (c n) -> p c n", n=M_HEADS),
                                      w_if_used[:, 0].bitcast(f32), ALU.subtract).then_inc(w_if_split, 1)
                elif step == "lambda":
                    for j in range(2):
                        last = dve.tensor_tensor_reduce(
                            out=work_t[:, 0:D_DH], in0=lam_row[:, 2 * j * D_DH:(2 * j + 1) * D_DH],
                            in1=lam_row[:, (2 * j + 1) * D_DH:(2 * j + 2) * D_DH], scale=1.0, scalar=0.0,
                            op0=ALU.mult, op1=ALU.add, accum_out=lam_s[:, j:j + 1])
                        last.then_inc(lam_sum, 1)
                        dve.wait_ge(lam_sum, j + 1)
                    dve.wait_ge(lam_exp, 1)
                    link(dve.tensor_tensor(lam_s[:, 0:1], lam_s[:, 3:4], lam_s[:, 2:3], ALU.subtract))
                    link(dve.tensor_scalar(neg_lam[:, :], lam_s[:, 0:1], -LAM_INIT, None, ALU.add))
                elif step == "normx":
                    normalise(step, k, RES, XN)
                elif step == "split":
                    if k < 2 * (NB - 2):
                        split(*divmod(k, 2))
                elif step in HALVED:
                    lower_half(step)
                elif step in ("qm", "km"):
                    convolve(step)
                elif step == "gates":
                    dve.wait_ge(if_rows, 1)
                    dve.tensor_scalar(gate[:, 0, :], A[0][0:M_HEADS, 0:T], b_if_c[:, 0:1], None, ALU.add)
                    link(dve.tensor_scalar(gate[:, 1, :], A[0][F_ROW:F_ROW + M_HEADS, 0:T], b_if_c[:, 1:2], None,
                                           ALU.add))
                    dve.scalar_tensor_tensor(gate[:, 2, :], gate[:, 1, :], -1.0, gate[:, 1, :], ALU.mult,
                                             ALU.max).then_inc(f_abs, 1)
                    link(dve.tensor_scalar(gate[:, 3, :], gate[:, 1, :], 0.0, None, ALU.min))
                    dve.wait_ge(f_ln, 1)
                    link(dve.tensor_tensor(gate[:, 3, :], gate[:, 3, :], gate[:, 2, :], ALU.subtract))
                    link(dve.tensor_tensor_scan(gate[:, 4, :], ones[0:M_HEADS, :], gate[:, 3, :], 0.0, ALU.mult, ALU.add))
                    link(dve.tensor_tensor(gate[:, 0, :], gate[:, 0, :], gate[:, 4, :], ALU.subtract))
                    link(dve.tensor_tensor_scan(gate[:, 5, :], gate[:, 0, :], gate[:, 0, :], 0.0, ALU.max, ALU.max))
                    dve.tensor_tensor(gate[:, 6, :], gate[:, 4, :], gate[:, 5, :], ALU.add).then_inc(bm_ready, 1)
                elif step == "gates2":
                    pass
                elif step == "mls":
                    if k == 0:
                        dve.wait_ge(gate_cols, 1)
                    if k >= 2:
                        dve.wait_ge(ml_num, k - 1)
                    d = decay[:, k % 2, :]
                    dve.tensor_scalar(d[:, 0:T], m_all[:, k, :], a_em[:, 0, k:k + 1], 0.0, ALU.subtract, ALU.max)
                    dve.tensor_scalar(d[:, T:T + P], m_all[:, k, P:T], a_em[:, 1, k:k + 1], 0.0, ALU.subtract,
                                      ALU.max).then_inc(ml_gap, 1)
                    dve.wait_ge(ml_decay, k + 1)
                    for b in (0, 2):
                        last = dve.tensor_tensor(d[:, b * P:(b + 1) * P], d[:, b * P:(b + 1) * P], causal[:, :], ALU.mult)
                    link(last)
                    dve.wait_ge(ml_scores, k + 1)
                    dve.tensor_tensor(d, A[k % 2][:, 0:3 * P], d, ALU.mult).then_inc(ml_probs, 1)
                elif step == "mlo":
                    dve.wait_ge(ml_num, k + 1)
                    if k >= 2:
                        dve.wait_ge(ml_h, k - 1)
                    c = 24 + 2 * (k % 2)
                    den, em = A[k % 2][:, 3 * P:3 * P + TT], a_em[:, :, M_HEADS + k]
                    link(dve.tensor_tensor(stat[:, c:c + 2], den, em, ALU.max))
                    link(dve.scalar_tensor_tensor(stat[:, c:c + 2], den, -1.0, stat[:, c:c + 2], ALU.mult, ALU.max))
                    dve.reciprocal(stat[:, c:c + 2], stat[:, c:c + 2]).then_inc(ml_rden, 1)
                elif step == "mlnorm":
                    dve.wait_ge(ml_h, M_HEADS)
                    inverse_root(step, k, slice(32, 40), slice(32, 40), M_DV)
                    for j in range(2 * M_HEADS):
                        v = HM[:, j * M_DV:(j + 1) * M_DV]
                        last = dve.tensor_scalar(v, v, stat[:, 32 + j:33 + j], None, ALU.mult)
                    last.then_inc(hm_done, 1)
                elif step == "normmem":
                    normalise(step, k, MEMN, MEMN)
                elif step == "dfs":
                    dve.wait_ge(df_scores, k + 1)
                    if k >= 1:
                        dve.wait_ge(df_a, k)
                    for c in range(2):
                        dve.tensor_tensor_reduce(out=work[:, c, 0:P], in0=A[c][:, 0:P], in1=chunk_mask[:, 0, :], scale=1.0,
                                                 scalar=NEG, op0=ALU.add, op1=ALU.max, accum_out=stat[:, 40 + 2 * c:41 + 2 * c])
                        last = dve.tensor_tensor_reduce(
                            out=work[:, c, P:3 * P], in0=A[c][:, P:3 * P],
                            in1=chunk_mask[:, 1:3, :].rearrange("p b k -> p (b k)"), scale=1.0,
                            scalar=NEG, op0=ALU.add, op1=ALU.max, accum_out=stat[:, 41 + 2 * c:42 + 2 * c])
                    link(last)
                    dve.tensor_scalar(stat[:, 40:44], stat[:, 40:44], -(D_DH ** -0.5), None, ALU.mult).then_inc(df_max, 1)
                elif step == "dfa":
                    dve.wait_ge(df_exp, k + 1)
                    link(dve.reciprocal(stat[:, 44:48], stat[:, 44:48]))
                    link(dve.tensor_scalar(stat[:, 46:48], stat[:, 46:48], neg_lam[:, 0:1], None, ALU.mult))
                    if k >= 1:
                        dve.wait_ge(df_aT, k)
                    for t, cols in ((0, slice(0, P)), (1, slice(P, 3 * P))):
                        link(dve.tensor_scalar(work[:, 2, cols], work[:, 1, cols], stat[:, 46 + t:47 + t], None, ALU.mult))
                        last = dve.scalar_tensor_tensor(work[:, 3, cols], work[:, 0, cols], stat[:, 44 + t:45 + t],
                                                        work[:, 2, cols], ALU.mult, ALU.add)
                    last.then_inc(df_a, 1)
                elif step == "dfnorm":
                    dve.wait_ge(df_h, D_HEADS)
                    inverse_root(step, k, slice(48, 64), slice(48, 64), P)
                    for j in range(TT * D_HEADS):
                        v = HD[:, j * P:(j + 1) * P]
                        last = dve.tensor_scalar(v, v, stat[:, 48 + j:49 + j], None, ALU.mult)
                    last.then_inc(hd_done, 1)
                elif step == "norm1":
                    normalise(step, k, RES, NRM)
                elif step == "xas":
                    dve.wait_ge(xa_scores, k + 1)
                    s = 40 + 4 * (k % 2)
                    link(dve.tensor_reduce(stat[:, s:s + 2], A[k % 2][:, :].rearrange("p (t m) -> p t m", t=TT), AX.X, ALU.max))
                    dve.tensor_scalar(stat[:, s:s + 2], stat[:, s:s + 2], -(X_DH ** -0.5), None, ALU.mult).then_inc(xa_max, 1)
                    dve.wait_ge(xa_exp, k + 1)
                    link(dve.reciprocal(stat[:, s + 2:s + 4], stat[:, s + 2:s + 4]))
                    for t in range(TT):
                        w = work[:, k % 2, t * X_DH:(t + 1) * X_DH]
                        last = dve.tensor_scalar(w, w, stat[:, s + 2 + t:s + 3 + t], None, ALU.mult)
                    last.then_inc(xa_p, 1)
                elif step == "xao":
                    dve.wait_ge(xa_hi, k + 1)
                    cols = slice(2 * k * T, (2 * k + 2) * T)
                    dve.tensor_tensor(OXT[1][:, cols], A[3][:, :], OXT[0][:, cols].bitcast(f32),
                                      ALU.subtract).then_inc(xa_h, 1)
                elif step == "norm2":
                    normalise(step, k, RES, H2, [k])
                elif step == "x2T":
                    gain = vec[:, VCOL["norm_ffn"]:VCOL["norm_ffn"] + KC]
                    for i in range(2):
                        n = TILE[step, k] + i
                        dve.wait_ge(tile_ready, n + 1)
                        dve.tensor_tensor(fm(X2T)[:, 4 * i:4 * i + 4, k * P:(k + 1) * P],
                                          bank[n % 4][:, :].rearrange("p (c t) -> p c t", t=P),
                                          gain[:, 4 * i:4 * i + 4].unsqueeze(2).to_broadcast([P, 4, P]),
                                          ALU.mult).then_inc(evac["dve"], 1)
                elif step == "route":
                    route()
                elif step in EVACUATES and EVACUATES[step] == "dve":
                    projection(step, k)

            def gathered(value):
                dve.wait_ge(xg_ready, value)
                gain = vec[:, VCOL["norm_ffn"]:VCOL["norm_ffn"] + KC]
                dve.tensor_tensor(xg[:, :, :], xbank[:, :].rearrange("p (k c) -> p k c", c=CAP),
                                  gain.unsqueeze(2).to_broadcast([P, KC, CAP]), ALU.mult).then_inc(xg_done, 1)

            def experts(before):
                made = before * (E + 1)
                if before:
                    dve.tensor_scalar(rank[:, :, :], rank[:, :, :], -float(CAP), None, ALU.add).then_inc(rank_moved, 1)
                    dve.wait_ge(rank_moved, before)
                    dve.wait_ge(xg_ready, made)
                    place_tokens(slice(0, 1))
                gathered(made + 1)
                with dve.Fori(0, E) as e:
                    n = e + (before * E + 1)
                    for t in range(TT):
                        last = dve.tensor_scalar(pickw[:, t, :], slot_no[:, :], rank[:, t, bass.ds(e, 1)],
                                                 comb[:, t, bass.ds(e, 1)], ALU.is_equal, ALU.mult)
                    last.then_inc(pickw_ready, 1)
                    dve.wait_ge(xg_ready, e + (made + 1))
                    place_tokens(bass.ds(e + 1, 1))
                    dve.wait_ge(g_ready, n)
                    dve.tensor_scalar(G_, gbank[:, :], LIMIT, None, ALU.min).then_inc(g_clip, 1)
                    dve.wait_ge(u_ready, n)
                    dve.tensor_scalar(U_, ubank[:, :], LIMIT, -LIMIT, ALU.min, ALU.max)
                    dve.wait_ge(g_sig, n)
                    dve.tensor_tensor(S_, S_, G_, ALU.mult).then_inc(gs_done, 1)
                    dve.wait_ge(gs_done, n)
                    dve.scalar_tensor_tensor(A_, U_, 1.0, S_, ALU.add, ALU.mult).then_inc(a_ready, 1)
                    dve.wait_ge(y_ready, n)
                    dve.tensor_copy(y_sb, tbank[:, :]).then_inc(y_done, 1)
                    gathered(e + (made + 2))
                dve.wait_ge(added, (before + 1) * E)

            dve.wait_ge(route_done, 1)
            n_most = dve.value_load(most_i[0:1, 0:1], min_val=0, max_val=T)
            experts(0)
            for p in range(1, T // CAP):
                with dve.If(n_most > p * CAP):
                    experts(p)
            r = nat(RES)[:, TT - 1, HALF:D]
            link(dve.tensor_copy(r, bank[3][:, :]))
            link(dve.tensor_tensor_reduce(out=work[:, 3, :], in0=r, in1=r, scale=1.0, scalar=0.0, op0=ALU.mult,
                                          op1=ALU.add, accum_out=stat[:, 19:20]))
            dve.wait_ge(norm_sq, len(NORM_SQ) + 1)
            sums = stat[:, 16:20].rearrange("p (t h) -> p t h", h=2)
            link(dve.tensor_tensor(stat[:, 20:22], sums[:, :, 0], sums[:, :, 1], ALU.add))
            inverse_root("final", 0, slice(20, 22), slice(20, 22), D)
            dve.wait_ge(fin_gain_in, 16)
            for t in range(TT):
                for h in range(2):
                    cols = slice(h * HALF, (h + 1) * HALF)
                    last = dve.scalar_tensor_tensor(nat(RES)[:, t, cols], bank[2 * t + h][:, :], stat[:, 20 + t:21 + t],
                                                    fin_gain[:, cols], ALU.mult, ALU.mult)
                last.then_inc(out_ready, 1)

        @block.tensor
        def _(pe):
            def keep_warm(n):
                for _ in range(n):
                    pe.matmul(A[2][:, 0:T], ones[:, 0:P], ones[:, :], start=True, stop=True)

            pe.wait_ge(consts_done, 1)
            keep_warm(12)
            pe.wait_ge(consts_done, CONSTS)
            pe.wait_ge(small_in, 16 * N_SMALL)

            inputs = {"kx": (MEMT, "memT"), "vx": (MEMT, "memT"), "bm": (HMT, "hmT"), "bd": (HDT, "hdT"), "qx": (X1T, "x1T")}
            natural = {"xT": XN, "hmT": HM, "memT": MEMN, "hdT": HD, "x1T": NRM, "x2T": H2}
            norm_of = {"xT": "normx", "memT": "normmem", "x1T": "norm1", "x2T": "norm2"}

            def transpose_all(step, k):
                src = nat(natural[step])
                if step in norm_of:
                    pe.wait_ge(norm_done, NORM_SQ[norm_of[step], k] + 1)
                elif step == "hmT":
                    pe.wait_ge(hm_done, 1)
                else:
                    pe.wait_ge(hd_done, 1)
                for i in range(tiles_of(step)):
                    n = TILE[step, k] + i
                    wait_evacuated(pe, n - 4)
                    for q in range(4):
                        t, c = (k, 4 * i + q) if step == "x2T" else (q % 2, 2 * i + q // 2)
                        last = pe.transpose(bank[n % 4][:, q * P:(q + 1) * P], src[:, t, c * P:(c + 1) * P], ident[:, :])
                    last.then_inc(tile_ready, 1)

            transposed = set()

            def three_passes(out, still, moving, split=None, operand=None):
                if operand in transposed:
                    operand = None
                transposed.add(operand)
                for kk in range(KC):
                    if operand is not None and kk % 2 == 0:
                        wait_evacuated(pe, TILE[operand, 0] + kk // 2)
                    if split is not None and kk % (KC // 2) == 0:
                        wait_split(pe, split, kk // (KC // 2))
                    for a, b in ((0, 0), (0, 1), (1, 0)):
                        last = pe.matmul(out, still(a, kk), moving(b, kk), start=kk + a + b == 0,
                                         stop=kk == KC - 1 and a == 1)
                return last

            def projection(step, k):
                job = None
                if step == "wo":
                    operand = OXT
                    pe.wait_ge(xa_h, X_HEADS)
                elif step == "out":
                    operand = MIX
                    pe.wait_ge(mix_done, 4)
                else:
                    operand, job = inputs.get(step, (XT, "xT"))
                b = BLOCKS.index((step, k))

                def weights(b, half, kk, cols):
                    return halves[:, b % 2, half, :].rearrange("p (k n) -> p k n", k=KC)[:, kk, cols]

                for i in range(2):
                    n = TILE[step, k] + i
                    wait_evacuated(pe, n - 4)
                    if step in TOKEN_MAJOR:
                        t, wb = (k, NB - 2 + i) if step == "wo" else (i, b)
                        last = three_passes(bank[n % 4][:, :], lambda a, kk: fm(operand[a])[:, kk, t * P:(t + 1) * P],
                                            lambda a, kk: weights(wb, a, kk, slice(0, BLK)),
                                            split=wb if (k if step == "wo" else i) == 0 else None, operand=job)
                    else:
                        for j in range(2):
                            c = (2 * i + j) * P
                            last = three_passes(bank[n % 4][:, j * T:(j + 1) * T],
                                                lambda a, kk: weights(b, a, kk, slice(c, c + P)),
                                                lambda a, kk: fm(operand[a])[:, kk, :],
                                                split=b if i + j == 0 else None, operand=job)
                    last.then_inc(tile_ready, 1)

            def one(out, lhsT, rhs):
                return pe.matmul(out, lhsT, rhs, start=True, stop=True)

            def start_sums(t):
                for h in range(2):
                    wait_evacuated(pe, len(OWNER) - 4 + 2 * t + h)
                    pe.matmul(bank[2 * t + h][:, :], ident[:, :], nat(RES)[:, t, h * HALF:(h + 1) * HALF],
                              start=True, stop=False, skip_group_check=True)

            for step, k in ORDER:
                if step == "vectors":
                    pe.transpose(A[3][:, 0:NVEC], vec_rows, ident[0:NVEC, 0:NVEC]).then_inc(vec_ready, 1)
                elif step in TRANSPOSES:
                    transpose_all(step, k)
                    if step == "xT":
                        keep_warm(8)
                elif step in EVACUATES:
                    projection(step, k)
                elif step == "gates":
                    wait_job(pe, "xT")
                    pe.wait_ge(w_if_split, 1)
                    for kk in range(KC):
                        for a, b in ((0, 0), (0, 1), (1, 0)):
                            last = pe.matmul(A[0][0:2 * F_ROW, 0:T], w_if_halves[:, a, kk, :], fm(XT[b])[:, kk, :],
                                             start=kk + a + b == 0, stop=kk == KC - 1 and a == 1)
                    last.then_inc(if_rows, 1)
                elif step == "gates2":
                    pe.wait_ge(em_ready, 1)
                    for h in range(M_HEADS):
                        one(A[h // 2][:, (h % 2) * T:(h % 2 + 1) * T], head_row[:, h, :], gate[:, 5, :])
                    for t in range(TT):
                        for j, row in ((0, 0), (1, 6)):
                            c = (2 * t + j) * M_HEADS
                            last = pe.transpose(A[2][:, c:c + M_HEADS], gate[:, row, t * P:(t + 1) * P],
                                                ident[0:M_HEADS, 0:M_HEADS])
                    last.then_inc(gate_bc, 1)
                elif step == "mls":
                    wait_job(pe, "km")
                    if k == 0:
                        pe.wait_ge(gate_cols, 1)
                    if k >= 2:
                        pe.wait_ge(ml_rden, k - 1)
                    q, key = fm(QK)[:, k, :], fm(QK)[:, M_HEADS + k, :]
                    one(A[k % 2][:, 0:T], key[:, 0:P], q)
                    one(A[k % 2][:, T:T + P], key[:, P:T], q[:, P:T]).then_inc(ml_scores, 1)
                elif step == "mlo":
                    wait_job(pe, "vm", 1)
                    pe.wait_ge(ml_probs, k + 1)
                    if k >= 2:
                        pe.wait_ge(ml_h, k - 1)
                    w, num, den = decay[:, k % 2, :], A[2 + k % 2], A[k % 2]
                    v = [nat(VM)[:, t, k * M_DV:(k + 1) * M_DV] for t in range(TT)]
                    for rhs, dst in ((v, [num[:, t * M_DV:(t + 1) * M_DV] for t in range(TT)]),
                                     ([ones[:, 0:1]] * TT, [den[:, 3 * P + t:3 * P + t + 1] for t in range(TT)])):
                        one(dst[0], w[:, 0:P], rhs[0])
                        pe.matmul(dst[1], w[:, P:2 * P], rhs[0], start=True, stop=False)
                        last = pe.matmul(dst[1], w[:, 2 * P:3 * P], rhs[1], start=False, stop=True)
                    last.then_inc(ml_num, 1)
                elif step == "dfs":
                    wait_job(pe, "kd", 1)
                    wait_job(pe, "qd", 1)
                    if k >= 1:
                        pe.wait_ge(df_max, k)
                    for cols, qs, ks in ((slice(0, P), slice(0, P), slice(0, P)), (slice(P, 3 * P), slice(P, T), slice(0, T))):
                        for c in range(2):
                            rows = slice(c * D_DH, (c + 1) * D_DH)
                            last = one(A[c][:, cols], fm(QD)[rows, k, qs], fm(KD)[rows, k, ks])
                    last.then_inc(df_scores, 1)
                elif step == "dft":
                    pe.wait_ge(df_a, k + 1)
                    if k >= 1:
                        pe.wait_ge(df_aTs, k)
                    for b in range(3):
                        last = pe.transpose(A[2][:, b * P:(b + 1) * P], work[:, 3, b * P:(b + 1) * P], ident[:, :])
                    last.then_inc(df_aT, 1)
                elif step == "dfo":
                    wait_job(pe, "vd", k // 4)
                    pe.wait_ge(df_aTs, k + 1)
                    if k >= 2:
                        pe.wait_ge(df_h, k - 1)
                    o = A[3][:, (k % 2) * T:(k % 2 + 1) * T]
                    v = [nat(VD)[:, t, k * P:(k + 1) * P] for t in range(TT)]
                    one(o[:, 0:P], work_t[:, 0:P], v[0])
                    pe.matmul(o[:, P:T], work_t[:, P:2 * P], v[0], start=True, stop=False)
                    pe.matmul(o[:, P:T], work_t[:, 2 * P:3 * P], v[1], start=False, stop=True).then_inc(df_o, 1)
                elif step == "xas":
                    wait_job(pe, "qx", 1)
                    wait_job(pe, "kx", 1)
                    if k >= 2:
                        pe.wait_ge(xa_exp, k - 1)
                    for t in range(TT):
                        for j in range(2):
                            last = pe.matmul(A[k % 2][:, t * T:(t + 1) * T], fm(QX)[:, 2 * k + j, t * P:(t + 1) * P],
                                             fm(KX)[:, 2 * k + j, :], start=j == 0, stop=j == 1)
                    last.then_inc(xa_scores, 1)
                elif step == "xat":
                    pe.wait_ge(xa_p, k + 1)
                    if k >= 1:
                        pe.wait_ge(xa_pTs, k)
                    for m in range(TT):
                        for t in range(TT):
                            c = (2 * m + t) * P
                            last = pe.transpose(A[2][:, c:c + P], work[:, k % 2, t * X_DH + m * P:t * X_DH + (m + 1) * P],
                                                ident[:, :])
                    last.then_inc(xa_pT, 1)
                elif step == "xao":
                    wait_job(pe, "vx", 1)
                    pe.wait_ge(xa_pTs, k + 1)
                    if k >= 1:
                        pe.wait_ge(xa_h, k)
                    for j in range(2):
                        for m in range(TT):
                            c = k * X_DH + j * P
                            last = pe.matmul(A[3][:, j * T:(j + 1) * T], nat(VX)[:, m, c:c + P],
                                             work_t[:, m * T:(m + 1) * T], start=m == 0, stop=m == 1)
                    last.then_inc(xa_o, 1)
                elif step == "logits":
                    if k == 1:
                        keep_warm(2)
                    wait_job(pe, "x2T", k)
                    for kk in range(KC):
                        pe.matmul(A[0][:, k * E:(k + 1) * E], fm(X2T)[:, kk, k * P:(k + 1) * P], w_r[:, kk, :],
                                  start=kk == 0, stop=False)
                    pe.matmul(A[0][:, k * E:(k + 1) * E], ones[0:1, 0:P], b_r[0:1, :], start=False,
                              stop=True).then_inc(lg_ready, 1)
                elif step == "route":
                    keep_warm(2)
                    start_sums(0)
                    pe.wait_ge(mask_ready, 1)
                    one(A[1][:, 0:E], strict[:, :], chosen[:, 0, :])
                    for c, last_lhs in ((E, strict), (2 * E, ones_r)):
                        pe.matmul(A[1][:, c:c + E], ones_r[:, :], chosen[:, 0, :], start=True, stop=False)
                        last = pe.matmul(A[1][:, c:c + E], last_lhs[:, :], chosen[:, 1, :], start=False, stop=True)
                    last.then_inc(rank_ready, 1)
                    pe.wait_ge(comb_ready, 1)
                    for t in range(TT):
                        last = pe.transpose(A[3][0:E, t * P:(t + 1) * P], comb[:, t, 0:E], ident[:, :])
                    last.then_inc(combT_ready, 1)
                    start_sums(1)

            def add_biases():
                pe.wait_ge(combT_done, 1)
                pe.wait_ge(bias_in, 32)
                for t in range(TT):
                    for h in range(2):
                        pe.matmul(bank[2 * t + h][:, :], combT[:, t, :], bdn[:, h * HALF:(h + 1) * HALF],
                                  start=False, stop=False, skip_group_check=True)

            def gather(chunks=range(KC)):
                for kk in chunks:
                    for t in range(TT):
                        last = pe.matmul(xbank[:, kk * CAP:(kk + 1) * CAP], nat(H2)[:, t, kk * P:(kk + 1) * P],
                                         pick[:, t, :], start=t == 0, stop=t == TT - 1)
                if kk == KC - 1:
                    last.then_inc(xg_ready, 1)

            def experts(before):
                made = before * (E + 1)
                pe.wait_ge(pick_ready, made + 1)
                if before:
                    pe.wait_ge(xg_done, made)
                gather()
                if not before:
                    add_biases()
                for e in range(LEAD):
                    expert(e, 0, e, before)
                with pe.Fori(0, (E - LEAD) // GROUP) as i:
                    for q in range(LEAD, LEAD + GROUP):
                        expert(i * GROUP + q, i, q, before)

            def expert(e, i, lead, before):
                n, made = e + (before * E + 1), before * (E + 1)
                slots, arrived = [], []
                for j in range(EXPERT_BLOCKS):
                    slot, turns = slot_of(before, lead, j)
                    slots.append(slot)
                    arrived.append((i * TURNS + (turns + 1 + (NB // 2 if slot < 2 else 0))) * 16)
                pe.wait_ge(xg_done, e + (made + 1))
                for part, dst, ready in ((0, gbank, g_ready), (1, ubank, u_ready)):
                    for h in range(2):
                        j = 2 * part + h
                        pe.wait_ge(w_loaded[slots[j]], arrived[j])
                        for kk in range(4):
                            for half in range(2):
                                last = pe.matmul(dst[half * CAP:(half + 1) * CAP, :], xg[:, 4 * h + kk, :],
                                                 ring[:, slots[j], kk * D + half * HALF:kk * D + (half + 1) * HALF],
                                                 start=4 * h + kk == 0, stop=False)
                        last.then_inc(w_used, 1)
                    if part == 0:
                        pe.wait_ge(sel_ready, n)
                    for half in range(2):
                        c = part * D + half * HALF
                        last = pe.matmul(dst[half * CAP:(half + 1) * CAP, :], sel[:, :], bgu[:, c:c + HALF],
                                         start=False, stop=True)
                    last.then_inc(ready, 1)
                pe.wait_ge(pickw_ready, n)
                for t in range(TT):
                    last = pe.transpose(tbank[:, t * P:(t + 1) * P], pickw[:, t, :], ident[:, :])
                last.then_inc(wT_ready, 1)
                pe.wait_ge(pick_ready, e + (made + 2))
                gather(range(4))
                pe.wait_ge(wT_done, n)
                pe.wait_ge(a_ready, n)
                for c in range(4):
                    last = pe.transpose(tbank[:, c * P:(c + 1) * P], A_[:, c * P:(c + 1) * P], ident[:, :])
                last.then_inc(aT_ready, 1)
                gather(range(4, 6))
                pe.wait_ge(aT_done, n)
                for h in range(2):
                    pe.wait_ge(w_loaded[slots[4 + h]], arrived[4 + h])
                    for c in range(4):
                        for half in range(2):
                            last = pe.matmul(tbank[half * CAP:(half + 1) * CAP, :],
                                             work_t[:, c * P + h * CAP:c * P + (h + 1) * CAP],
                                             ring[:, slots[4 + h], c * D + half * HALF:c * D + (half + 1) * HALF],
                                             start=4 * h + c == 0, stop=4 * h + c == 7)
                    last.then_inc(w_used if h == 0 else y_ready, 1)
                gather(range(6, KC))
                pe.wait_ge(y_done, n)
                for t in range(TT):
                    for h in range(2):
                        rows = slice(h * CAP, (h + 1) * CAP)
                        last = pe.matmul(bank[2 * t + h][:, :], wT[rows, t, :], y_sb[rows, :],
                                         start=False, stop=False, skip_group_check=True)
                last.then_inc(added, 1)

            experts(0)
            n_most = pe.value_load(most_i[0:1, 0:1], min_val=0, max_val=T)
            for p in range(1, T // CAP):
                with pe.If(n_most > p * CAP):
                    experts(p)


_INS = ["x", "mem", "norm_mix", "w_in", "conv_w", "b_if", "mlstm_gain", "diff_lambda", "diff_gain", "w_branch_m",
        "w_branch_d", "b_gate", "w_out", "norm_xattn", "norm_mem", "wq_x", "wkv_x", "wo_x", "norm_ffn", "w_router",
        "b_router", "w_gu", "b_gu", "w_dn", "b_dn", "norm_final"]


def kernel(**inputs):
    import numpy as np
    import concourse.bacc as bacc
    from concourse.bass_utils import run_bass_kernel_spmd

    nc = bacc.Bacc("TRN2", target_bir_lowering=False, num_devices=1)
    arrays, args = {}, []
    for name in _INS:
        a = np.ascontiguousarray(inputs[name])
        arrays[f"in_{name}"] = a
        args.append(nc.dram_tensor(f"in_{name}", a.shape, mybir.dt.from_np(a.dtype), kind="ExternalInput").ap())
    args.append(nc.dram_tensor("out_0", (1, T, D), mybir.dt.float32, kind="ExternalOutput").ap())
    program(nc, *args)
    r = run_bass_kernel_spmd(nc, [arrays], core_ids=[0])
    return r.results[0]["out_0"]
```
